# Optimizing a Trainium2 kernel written in Bass

```python
import math
import jax, jax.numpy as jnp
from jax import lax
import numpy as np
import jax
import jax.numpy as jnp

D_MODEL = 1024
BATCH = 1
SEQ = 256
DEPTH = 2

N_MIXERS = 2
SSM_EXPAND = 2
SSM_D_INNER = SSM_EXPAND * D_MODEL
SSM_HEADDIM = 64
SSM_N_HEADS = SSM_D_INNER // SSM_HEADDIM
SSM_N_GROUPS = 8
SSM_HEADS_PER_GROUP = SSM_N_HEADS // SSM_N_GROUPS
SSM_D_STATE = 128
SSM_CONV_K = 4
SSM_CHUNK = 128
SSM_CONV_DIM = SSM_D_INNER + 2 * SSM_N_GROUPS * SSM_D_STATE
SSM_IN_DIM = SSM_D_INNER + SSM_CONV_DIM + SSM_N_HEADS
ATTN_HEAD_DIM = 64
ATTN_N_HEADS = D_MODEL // (2 * ATTN_HEAD_DIM)
ATTN_V_DIM = 2 * ATTN_HEAD_DIM
ATTN_QKV_DIM = 3 * D_MODEL
ROT_DIM = ATTN_HEAD_DIM // 4
ROPE_THETA = 500000.0
Q_BLOCK = 128
MOE_GROUPS = 4
MOE_EXPERTS_PER_GROUP = 8
MOE_N_EXPERTS = MOE_GROUPS * MOE_EXPERTS_PER_GROUP
MOE_TOP_K = 2
MOE_D_FF = 512
MOE_BLOCK = 128
DEEPNORM_ALPHA = (2 * DEPTH) ** 0.25
DEEPNORM_BETA = (8 * DEPTH) ** -0.25
NORM_EPS = 1e-5
N_SSM_LAYERS = (DEPTH + N_MIXERS - 1) // N_MIXERS
N_ATTN_LAYERS = DEPTH // N_MIXERS


def layer_norm(x, g, b):
    xf = x.astype(jnp.float32)
    mu = jnp.mean(xf, axis=-1, keepdims=True)
    var = jnp.mean(jnp.square(xf - mu), axis=-1, keepdims=True)
    y = (xf - mu) * lax.rsqrt(var + NORM_EPS) * g.astype(jnp.float32) + b.astype(jnp.float32)
    return y.astype(x.dtype)

def causal_depthwise_conv(u, w, bias):
    k = w.shape[0]
    out = lax.conv_general_dilated(u, w[:, None, :], window_strides=(1,), padding=[(k - 1, 0)],
                                   dimension_numbers=("NWC", "WIO", "NWC"),
                                   feature_group_count=u.shape[-1])
    return out + bias

def ssd_chunked(xh, dt, a, bm, cm):
    b, s = xh.shape[0], xh.shape[1]
    c = s // SSM_CHUNK
    G, R, P, N, L = SSM_N_GROUPS, SSM_HEADS_PER_GROUP, SSM_HEADDIM, SSM_D_STATE, SSM_CHUNK
    dtc = dt.reshape(b, c, L, G, R)
    xdt = xh.reshape(b, c, L, G, R, P) * dtc[..., None]
    bc = bm.reshape(b, c, L, G, N)
    cc = cm.reshape(b, c, L, G, N)
    a_cum = jnp.cumsum(dtc * a, axis=2)
    causal = jnp.tril(jnp.ones((L, L), dtype=bool))
    seg = a_cum[:, :, :, None] - a_cum[:, :, None, :]
    decay_ls = jnp.exp(jnp.where(causal[:, :, None, None], seg, -jnp.inf))
    cb = jnp.einsum("bclgn,bcsgn->bclsg", cc, bc)
    y_diag = jnp.einsum("bclsgr,bcsgrp->bclgrp", cb[..., None] * decay_ls, xdt)
    decay_to_end = jnp.exp(a_cum[:, :, -1:] - a_cum)
    chunk_states = jnp.einsum("bclgn,bclgrp->bcgrpn", bc, xdt * decay_to_end[..., None])
    chunk_decay = jnp.exp(a_cum[:, :, -1])

    def step(h, inp):
        st, dec = inp
        return h * dec[..., None, None] + st, h

    h0 = jnp.zeros((b, G, R, P, N), jnp.float32)
    _, prev = lax.scan(step, h0, (jnp.moveaxis(chunk_states, 1, 0), jnp.moveaxis(chunk_decay, 1, 0)))
    prev = jnp.moveaxis(prev, 0, 1)
    y_off = jnp.einsum("bclgn,bcgrpn->bclgrp", cc, prev) * jnp.exp(a_cum)[..., None]
    return (y_diag + y_off).reshape(b, s, G, R, P)

def mamba2_mixer(x, w_in, conv_w, conv_b, dt_bias, a_log, d_skip, norm_w, w_out):
    b, s, _ = x.shape
    G, R, P, N = SSM_N_GROUPS, SSM_HEADS_PER_GROUP, SSM_HEADDIM, SSM_D_STATE
    zxbcdt = x @ w_in
    z = zxbcdt[..., :SSM_D_INNER]
    xbc = zxbcdt[..., SSM_D_INNER:SSM_D_INNER + SSM_CONV_DIM]
    dt_raw = zxbcdt[..., SSM_D_INNER + SSM_CONV_DIM:]
    xbc = jax.nn.silu(causal_depthwise_conv(xbc, conv_w, conv_b))
    xs = xbc[..., :SSM_D_INNER]
    bm = xbc[..., SSM_D_INNER:SSM_D_INNER + G * N].reshape(b, s, G, N).astype(jnp.float32)
    cm = xbc[..., SSM_D_INNER + G * N:].reshape(b, s, G, N).astype(jnp.float32)
    dt = jax.nn.softplus(dt_raw.astype(jnp.float32) + dt_bias.astype(jnp.float32)).reshape(b, s, G, R)
    a = -jnp.exp(a_log.astype(jnp.float32)).reshape(G, R)
    xh = xs.reshape(b, s, G, R, P).astype(jnp.float32)
    y = ssd_chunked(xh, dt, a, bm, cm) + d_skip.astype(jnp.float32).reshape(G, R)[..., None] * xh
    yg = (y.reshape(b, s, SSM_D_INNER) * jax.nn.silu(z.astype(jnp.float32))).reshape(b, s, G, SSM_D_INNER // G)
    yg = yg * lax.rsqrt(jnp.mean(jnp.square(yg), axis=-1, keepdims=True) + NORM_EPS)
    yg = yg.reshape(b, s, SSM_D_INNER) * norm_w.astype(jnp.float32)
    return yg.astype(x.dtype) @ w_out

def rope_tables(positions):
    inv = ROPE_THETA ** (-jnp.arange(0, ROT_DIM, 2, dtype=jnp.float32) / ROT_DIM)
    ang = positions.astype(jnp.float32)[..., None] * inv
    return jnp.cos(ang), jnp.sin(ang)

def apply_partial_rope(t, cos, sin):
    half = ROT_DIM // 2
    tf = t[..., :ROT_DIM].astype(jnp.float32)
    r1, r2 = tf[..., :half], tf[..., half:]
    c = cos[:, :, None, None, :]
    s = sin[:, :, None, None, :]
    rot = jnp.concatenate([r1 * c - r2 * s, r2 * c + r1 * s], axis=-1).astype(t.dtype)
    return jnp.concatenate([rot, t[..., ROT_DIM:]], axis=-1)

def diff_attention(x, cos, sin, w_qkv, lam_q1, lam_k1, lam_q2, lam_k2, subln_w, w_o, lambda_init):
    b, s, _ = x.shape
    H, Dh = ATTN_N_HEADS, ATTN_HEAD_DIM
    qkv = x @ w_qkv
    q = qkv[..., :D_MODEL].reshape(b, s, H, 2, Dh)
    k = qkv[..., D_MODEL:2 * D_MODEL].reshape(b, s, H, 2, Dh)
    v = qkv[..., 2 * D_MODEL:].reshape(b, s, H, ATTN_V_DIM)
    q = apply_partial_rope(q, cos, sin)
    k = apply_partial_rope(k, cos, sin)
    scale = Dh ** -0.5
    lam = (jnp.exp(jnp.sum(lam_q1.astype(jnp.float32) * lam_k1.astype(jnp.float32)))
           - jnp.exp(jnp.sum(lam_q2.astype(jnp.float32) * lam_k2.astype(jnp.float32))) + lambda_init)
    outs = []
    for i in range(s // Q_BLOCK):
        kv_len = (i + 1) * Q_BLOCK
        qb = q[:, i * Q_BLOCK:kv_len]
        kb = k[:, :kv_len]
        vb = v[:, :kv_len]
        sc = jnp.einsum("bqhcd,bkhcd->bhcqk", qb, kb).astype(jnp.float32) * scale
        q_pos = i * Q_BLOCK + jnp.arange(Q_BLOCK)
        mask = jnp.arange(kv_len)[None, :] <= q_pos[:, None]
        p = jax.nn.softmax(jnp.where(mask, sc, -jnp.inf), axis=-1)
        attn = p[:, :, 0] - lam * p[:, :, 1]
        outs.append(jnp.einsum("bhqk,bkhe->bqhe", attn.astype(v.dtype), vb))
    o = jnp.concatenate(outs, axis=1).astype(jnp.float32)
    o = o * lax.rsqrt(jnp.mean(jnp.square(o), axis=-1, keepdims=True) + NORM_EPS)
    o = o * subln_w.astype(jnp.float32) * (1.0 - lambda_init)
    return o.reshape(b, s, H * ATTN_V_DIM).astype(x.dtype) @ w_o

def hier_moe(x, w_group, w_expert, w_gate, w_up, w_down):
    b, s, d = x.shape
    T = b * s
    A = T * MOE_TOP_K
    xf = x.reshape(T, d)
    g_prob = jax.nn.softmax((xf @ w_group).astype(jnp.float32), axis=-1)
    g_sel = jnp.argmax(g_prob, axis=-1)
    g_gate = jnp.take_along_axis(g_prob, g_sel[:, None], axis=-1)[:, 0]
    e_logits = (xf @ w_expert).astype(jnp.float32).reshape(T, MOE_GROUPS, MOE_EXPERTS_PER_GROUP)
    e_logits = jnp.take_along_axis(e_logits, g_sel[:, None, None], axis=1)[:, 0]
    top_p, top_i = lax.top_k(jax.nn.softmax(e_logits, axis=-1), MOE_TOP_K)
    top_p = top_p / jnp.sum(top_p, axis=-1, keepdims=True)
    weight = (g_gate[:, None] * top_p).reshape(A)
    expert_id = (g_sel[:, None] * MOE_EXPERTS_PER_GROUP + top_i).reshape(A).astype(jnp.int32)
    token_id = jnp.repeat(jnp.arange(T, dtype=jnp.int32), MOE_TOP_K)
    order = jnp.argsort(expert_id)
    sorted_e = expert_id[order]
    counts = jax.ops.segment_sum(jnp.ones((A,), jnp.int32), expert_id, num_segments=MOE_N_EXPERTS)
    padded = ((counts + MOE_BLOCK - 1) // MOE_BLOCK) * MOE_BLOCK
    starts = jnp.cumsum(counts) - counts
    pends = jnp.cumsum(padded)
    pstarts = pends - padded
    dest = pstarts[sorted_e] + (jnp.arange(A, dtype=jnp.int32) - starts[sorted_e])
    n_blocks = -(-A // MOE_BLOCK) + MOE_N_EXPERTS
    P = n_blocks * MOE_BLOCK
    row_tok = jnp.full((P,), T, jnp.int32).at[dest].set(token_id[order])
    row_w = jnp.zeros((P,), x.dtype).at[dest].set(weight[order].astype(x.dtype))
    block_expert = jnp.minimum(jnp.searchsorted(pends, jnp.arange(n_blocks, dtype=jnp.int32) * MOE_BLOCK,
                                                side="right"), MOE_N_EXPERTS - 1)
    xpad = jnp.concatenate([xf, jnp.zeros((1, d), x.dtype)], axis=0)
    rows = xpad[row_tok].reshape(n_blocks, MOE_BLOCK, d)

    def expert_block(args):
        xb, e = args
        h = jax.nn.silu(xb @ w_gate[e]) * (xb @ w_up[e])
        return h @ w_down[e]

    yb = lax.map(expert_block, (rows, block_expert)).reshape(P, d)
    out = jax.ops.segment_sum(yb * row_w[:, None], row_tok, num_segments=T + 1)[:T]
    return out.reshape(b, s, d)

def first_inputs(seed: int = 0) -> dict:
    key = jax.random.key(seed)
    ks = jax.random.split(key, 32)
    f32 = jnp.float32
    nrm = lambda k, shape, sc: jax.random.normal(k, shape, f32) * sc
    x = jax.random.normal(ks[0], (BATCH, SEQ, D_MODEL), f32)
    start = jax.random.randint(ks[1], (BATCH, 1), 0, 1024, dtype=jnp.int32)
    positions = (start + jnp.arange(SEQ, dtype=jnp.int32)[None, :]).astype(jnp.int32)
    ln_mix_g = 1.0 + nrm(ks[2], (DEPTH, D_MODEL), 0.02)
    ln_mix_b = nrm(ks[3], (DEPTH, D_MODEL), 0.02)
    ln_ffn_g = 1.0 + nrm(ks[4], (DEPTH, D_MODEL), 0.02)
    ln_ffn_b = nrm(ks[5], (DEPTH, D_MODEL), 0.02)
    ns = N_SSM_LAYERS
    ssm_w_in = nrm(ks[6], (ns, D_MODEL, SSM_IN_DIM), D_MODEL ** -0.5)
    ssm_conv_w = nrm(ks[7], (ns, SSM_CONV_K, SSM_CONV_DIM), SSM_CONV_K ** -0.5)
    ssm_conv_b = nrm(ks[8], (ns, SSM_CONV_DIM), 0.02)
    u = jax.random.uniform(ks[9], (ns, SSM_N_HEADS), f32)
    dt0 = jnp.exp(u * (math.log(0.1) - math.log(0.001)) + math.log(0.001))
    ssm_dt_bias = dt0 + jnp.log(-jnp.expm1(-dt0))
    ssm_a_log = jnp.log(jax.random.uniform(ks[10], (ns, SSM_N_HEADS), f32, 1.0, 16.0))
    ssm_d = 1.0 + nrm(ks[11], (ns, SSM_N_HEADS), 0.02)
    ssm_norm_w = 1.0 + nrm(ks[12], (ns, SSM_D_INNER), 0.02)
    ssm_w_out = nrm(ks[13], (ns, SSM_D_INNER, D_MODEL), SSM_D_INNER ** -0.5 * DEEPNORM_BETA)
    na = N_ATTN_LAYERS
    attn_w_qkv = nrm(ks[14], (na, D_MODEL, ATTN_QKV_DIM), D_MODEL ** -0.5)
    attn_lam_q1 = nrm(ks[15], (na, ATTN_HEAD_DIM), 0.1)
    attn_lam_k1 = nrm(ks[16], (na, ATTN_HEAD_DIM), 0.1)
    attn_lam_q2 = nrm(ks[17], (na, ATTN_HEAD_DIM), 0.1)
    attn_lam_k2 = nrm(ks[18], (na, ATTN_HEAD_DIM), 0.1)
    attn_subln_w = 1.0 + nrm(ks[19], (na, ATTN_V_DIM), 0.02)
    attn_w_o = nrm(ks[20], (na, ATTN_N_HEADS * ATTN_V_DIM, D_MODEL), D_MODEL ** -0.5 * DEEPNORM_BETA)
    moe_w_group = nrm(ks[21], (DEPTH, D_MODEL, MOE_GROUPS), D_MODEL ** -0.5)
    moe_w_expert = nrm(ks[22], (DEPTH, D_MODEL, MOE_N_EXPERTS), D_MODEL ** -0.5)
    moe_w_gate = nrm(ks[23], (DEPTH, MOE_N_EXPERTS, D_MODEL, MOE_D_FF), D_MODEL ** -0.5)
    moe_w_up = nrm(ks[24], (DEPTH, MOE_N_EXPERTS, D_MODEL, MOE_D_FF), D_MODEL ** -0.5)
    moe_w_down = nrm(ks[25], (DEPTH, MOE_N_EXPERTS, MOE_D_FF, D_MODEL), MOE_D_FF ** -0.5 * DEEPNORM_BETA)
    return {"x": x, "positions": positions,
            "ln_mix_g": ln_mix_g, "ln_mix_b": ln_mix_b, "ln_ffn_g": ln_ffn_g, "ln_ffn_b": ln_ffn_b,
            "ssm_w_in": ssm_w_in, "ssm_conv_w": ssm_conv_w, "ssm_conv_b": ssm_conv_b,
            "ssm_dt_bias": ssm_dt_bias, "ssm_a_log": ssm_a_log, "ssm_d": ssm_d,
            "ssm_norm_w": ssm_norm_w, "ssm_w_out": ssm_w_out,
            "attn_w_qkv": attn_w_qkv, "attn_lam_q1": attn_lam_q1, "attn_lam_k1": attn_lam_k1,
            "attn_lam_q2": attn_lam_q2, "attn_lam_k2": attn_lam_k2, "attn_subln_w": attn_subln_w,
            "attn_w_o": attn_w_o,
            "moe_w_group": moe_w_group, "moe_w_expert": moe_w_expert,
            "moe_w_gate": moe_w_gate, "moe_w_up": moe_w_up, "moe_w_down": moe_w_down}

def first_block(x, positions, ln_mix_g, ln_mix_b, ln_ffn_g, ln_ffn_b,
              ssm_w_in, ssm_conv_w, ssm_conv_b, ssm_dt_bias, ssm_a_log, ssm_d, ssm_norm_w, ssm_w_out,
              attn_w_qkv, attn_lam_q1, attn_lam_k1, attn_lam_q2, attn_lam_k2, attn_subln_w, attn_w_o,
              moe_w_group, moe_w_expert, moe_w_gate, moe_w_up, moe_w_down):
    cos, sin = rope_tables(positions)
    h = x
    for layer in range(DEPTH):
        j = layer // N_MIXERS
        if layer % N_MIXERS == 0:
            mix = mamba2_mixer(h, ssm_w_in[j], ssm_conv_w[j], ssm_conv_b[j], ssm_dt_bias[j],
                               ssm_a_log[j], ssm_d[j], ssm_norm_w[j], ssm_w_out[j])
        else:
            lambda_init = 0.8 - 0.6 * math.exp(-0.3 * layer)
            mix = diff_attention(h, cos, sin, attn_w_qkv[j], attn_lam_q1[j], attn_lam_k1[j],
                                 attn_lam_q2[j], attn_lam_k2[j], attn_subln_w[j], attn_w_o[j], lambda_init)
        h = layer_norm(DEEPNORM_ALPHA * h + mix, ln_mix_g[layer], ln_mix_b[layer])
        ffn = hier_moe(h, moe_w_group[layer], moe_w_expert[layer], moe_w_gate[layer],
                       moe_w_up[layer], moe_w_down[layer])
        h = layer_norm(DEEPNORM_ALPHA * h + ffn, ln_ffn_g[layer], ln_ffn_b[layer])
    return h


N_META = 16
EXPAND = 2
D_INNER = EXPAND * D_MODEL
BLOCK = 128
ROPE_THETA_2 = 10000.0
EPS = 1e-6
NEG_INF = -1e30

MLA_HEADS = 8
MLA_Q_RANK = 384
MLA_KV_RANK = 256
MLA_NOPE = 128
MLA_ROPE = 64
MLA_QK = MLA_NOPE + MLA_ROPE
MLA_V = 128
MLA_WIDTH = MLA_HEADS * MLA_V

SWA_HEADS = 8
SWA_KV_HEADS = 2
SWA_REP = SWA_HEADS // SWA_KV_HEADS
SWA_HEAD_DIM = 128
SWA_WINDOW = 128
SWA_WIDTH = SWA_HEADS * SWA_HEAD_DIM
SWA_KV_WIDTH = SWA_KV_HEADS * SWA_HEAD_DIM

LRU_WIDTH = D_INNER
LRU_BLOCKS = 16
LRU_BLOCK_DIM = LRU_WIDTH // LRU_BLOCKS
LRU_C = 8.0
CONV_WIDTH = 4
CONV_PAD_LEFT = 2
CONV_PAD_RIGHT = 1

EVEN_SPLITS = (MLA_Q_RANK, MLA_KV_RANK, MLA_ROPE, SWA_WIDTH, SWA_KV_WIDTH, SWA_KV_WIDTH, D_INNER)
EVEN_IN = MLA_Q_RANK + MLA_KV_RANK + MLA_ROPE + SWA_WIDTH + 2 * SWA_KV_WIDTH + D_INNER
ODD_SPLITS = (LRU_WIDTH, D_INNER)
ODD_IN = LRU_WIDTH + D_INNER
N_EVEN = (DEPTH + 1) // 2
N_ODD = DEPTH // 2


def rms_norm(x, g):
    xf = x.astype(jnp.float32)
    y = xf * lax.rsqrt(jnp.mean(xf * xf, axis=-1, keepdims=True) + EPS)
    return (y * g.astype(jnp.float32)).astype(x.dtype)

def rope_tables_2(T, dim):
    inv = ROPE_THETA_2 ** (-jnp.arange(0, dim, 2, dtype=jnp.float32) / dim)
    ang = jnp.arange(T, dtype=jnp.float32)[:, None] * inv[None, :]
    return jnp.cos(ang), jnp.sin(ang)

def apply_rope(x, cos, sin):
    x1, x2 = jnp.split(x, 2, axis=-1)
    c = cos.astype(x.dtype)
    s = sin.astype(x.dtype)
    return jnp.concatenate([x1 * c - x2 * s, x1 * s + x2 * c], axis=-1)

def split_cols(z, sizes):
    out = []
    start = 0
    for s in sizes:
        out.append(z[..., start:start + s])
        start += s
    return out

def blocked_dense_attention(q, k, v, scale):
    B, H, T, dq = q.shape
    dv = v.shape[-1]
    nb = (T - N_META) // BLOCK

    def attend(qb):
        s = jnp.einsum('bhqd,bhkd->bhqk', qb, k, preferred_element_type=jnp.float32) * scale
        p = jax.nn.softmax(s, axis=-1).astype(v.dtype)
        return jnp.einsum('bhqk,bhkd->bhqd', p, v)

    o_meta = attend(q[:, :, :N_META])
    qb = q[:, :, N_META:].reshape(B, H, nb, BLOCK, dq).transpose(2, 0, 1, 3, 4)
    o_real = lax.map(attend, qb).transpose(1, 2, 0, 3, 4).reshape(B, H, nb * BLOCK, dv)
    return jnp.concatenate([o_meta, o_real], axis=2)

def banded_window_attention(q, k, v, sink, scale):
    B, G, R, T, d = q.shape
    L = T - N_META
    nb = L // BLOCK
    k_m, v_m = k[:, :, :N_META], v[:, :, :N_META]
    k_r, v_r = k[:, :, N_META:], v[:, :, N_META:]
    sink_l = sink.astype(jnp.float32).reshape(G, R)

    def band(t):
        tp = jnp.pad(t, ((0, 0), (0, 0), (BLOCK, BLOCK), (0, 0))).reshape(B, G, nb + 2, BLOCK, d)
        return jnp.concatenate([tp[:, :, :-2], tp[:, :, 1:-1], tp[:, :, 2:]], axis=3)

    k_b, v_b = band(k_r), band(v_r)
    q_b = q[:, :, :, N_META:].reshape(B, G, R, nb, BLOCK, d)
    blk = jnp.arange(nb)[:, None, None]
    qpos = blk * BLOCK + jnp.arange(BLOCK)[None, :, None]
    kpos = blk * BLOCK - BLOCK + jnp.arange(3 * BLOCK)[None, None, :]
    valid = (jnp.abs(qpos - kpos) <= SWA_WINDOW) & (kpos >= 0) & (kpos < L)
    s_meta = jnp.einsum('bgrnqd,bgmd->bgrnqm', q_b, k_m, preferred_element_type=jnp.float32) * scale
    s_band = jnp.einsum('bgrnqd,bgnkd->bgrnqk', q_b, k_b, preferred_element_type=jnp.float32) * scale
    s_band = jnp.where(valid, s_band, NEG_INF)
    s_sink = jnp.broadcast_to(sink_l[None, :, :, None, None, None], (B, G, R, nb, BLOCK, 1))
    p = jax.nn.softmax(jnp.concatenate([s_sink, s_meta, s_band], axis=-1), axis=-1).astype(v.dtype)
    o_real = (jnp.einsum('bgrnqm,bgmd->bgrnqd', p[..., 1:1 + N_META], v_m)
              + jnp.einsum('bgrnqk,bgnkd->bgrnqd', p[..., 1 + N_META:], v_b))
    o_real = o_real.reshape(B, G, R, L, d)

    q_m = q[:, :, :, :N_META]
    k_f, v_f = k_r[:, :, :BLOCK], v_r[:, :, :BLOCK]
    valid_m = (N_META + jnp.arange(BLOCK)[None, :] - jnp.arange(N_META)[:, None]) <= SWA_WINDOW
    s_mm = jnp.einsum('bgrqd,bgmd->bgrqm', q_m, k_m, preferred_element_type=jnp.float32) * scale
    s_mf = jnp.einsum('bgrqd,bgkd->bgrqk', q_m, k_f, preferred_element_type=jnp.float32) * scale
    s_mf = jnp.where(valid_m, s_mf, NEG_INF)
    s_ms = jnp.broadcast_to(sink_l[None, :, :, None, None], (B, G, R, N_META, 1))
    p_m = jax.nn.softmax(jnp.concatenate([s_ms, s_mm, s_mf], axis=-1), axis=-1).astype(v.dtype)
    o_meta = (jnp.einsum('bgrqm,bgmd->bgrqd', p_m[..., 1:1 + N_META], v_m)
              + jnp.einsum('bgrqk,bgkd->bgrqd', p_m[..., 1 + N_META:], v_f))
    return jnp.concatenate([o_meta, o_real], axis=3)

def mla_mixer(c_q, c_kv, k_pe, g_q_lat, g_kv_lat, w_uq, w_ukv, g_qn, g_kn, cos, sin):
    B, T, _ = c_q.shape
    q = jnp.einsum('btr,rhd->bhtd', rms_norm(c_q, g_q_lat), w_uq)
    kv = jnp.einsum('btr,rhd->bhtd', rms_norm(c_kv, g_kv_lat), w_ukv)
    k_nope, v = kv[..., :MLA_NOPE], kv[..., MLA_NOPE:]
    k_pe = jnp.broadcast_to(k_pe[:, None], (B, MLA_HEADS, T, MLA_ROPE))
    k = jnp.concatenate([k_nope, k_pe], axis=-1)
    q = rms_norm(q, g_qn)
    k = rms_norm(k, g_kn)
    q = jnp.concatenate([q[..., :MLA_NOPE], apply_rope(q[..., MLA_NOPE:], cos, sin)], axis=-1)
    k = jnp.concatenate([k[..., :MLA_NOPE], apply_rope(k[..., MLA_NOPE:], cos, sin)], axis=-1)
    o = blocked_dense_attention(q, k, v, MLA_QK ** -0.5)
    return o.transpose(0, 2, 1, 3).reshape(B, T, MLA_WIDTH)

def swa_mixer(q_s, k_s, v_s, g_qn, g_kn, sink, cos, sin):
    B, T, _ = q_s.shape
    q = q_s.reshape(B, T, SWA_HEADS, SWA_HEAD_DIM).transpose(0, 2, 1, 3)
    k = k_s.reshape(B, T, SWA_KV_HEADS, SWA_HEAD_DIM).transpose(0, 2, 1, 3)
    v = v_s.reshape(B, T, SWA_KV_HEADS, SWA_HEAD_DIM).transpose(0, 2, 1, 3)
    q = apply_rope(rms_norm(q, g_qn), cos, sin)
    k = apply_rope(rms_norm(k, g_kn), cos, sin)
    q = q.reshape(B, SWA_KV_HEADS, SWA_REP, T, SWA_HEAD_DIM)
    o = banded_window_attention(q, k, v, sink, SWA_HEAD_DIM ** -0.5)
    return o.reshape(B, SWA_HEADS, T, SWA_HEAD_DIM).transpose(0, 2, 1, 3).reshape(B, T, SWA_WIDTH)

def even_layer(z, w_in, g_q_lat, g_kv_lat, w_uq, w_ukv, mla_g_qn, mla_g_kn,
               swa_g_qn, swa_g_kn, sink, w_out, rope_mla, rope_swa):
    zp = jnp.einsum('btd,de->bte', z, w_in)
    c_q, c_kv, k_pe, q_s, k_s, v_s, gate = split_cols(zp, EVEN_SPLITS)
    y_a = mla_mixer(c_q, c_kv, k_pe, g_q_lat, g_kv_lat, w_uq, w_ukv,
                    mla_g_qn, mla_g_kn, rope_mla[0], rope_mla[1])
    y_b = swa_mixer(q_s, k_s, v_s, swa_g_qn, swa_g_kn, sink, rope_swa[0], rope_swa[1])
    y = jnp.concatenate([y_a, y_b], axis=-1) * jax.nn.silu(gate)
    return jnp.einsum('bte,ed->btd', y, w_out)

def lru_direction(xc, w_a, b_a, w_x, b_x, lam, reverse):
    B, T, W = xc.shape
    xb = xc.reshape(B, T, LRU_BLOCKS, LRU_BLOCK_DIM)
    r = jax.nn.sigmoid((jnp.einsum('btnd,nde->btne', xb, w_a).reshape(B, T, W) + b_a).astype(jnp.float32))
    i = jax.nn.sigmoid((jnp.einsum('btnd,nde->btne', xb, w_x).reshape(B, T, W) + b_x).astype(jnp.float32))
    log_a = -LRU_C * r * jax.nn.softplus(-lam.astype(jnp.float32))
    a = jnp.exp(log_a)
    b = jnp.sqrt(-jnp.expm1(2.0 * log_a)) * i * xc.astype(jnp.float32)

    def step(h, ab):
        a_t, b_t = ab
        h = a_t * h + b_t
        return h, h

    _, hs = lax.scan(step, jnp.zeros((B, W), jnp.float32),
                     (a.swapaxes(0, 1), b.swapaxes(0, 1)), reverse=reverse)
    return hs.swapaxes(0, 1).astype(xc.dtype)

def odd_layer(z, w_in, conv_w, conv_b, w_a, b_a, w_x, b_x, lam, w_out):
    zp = jnp.einsum('btd,de->bte', z, w_in)
    u, gate = split_cols(zp, ODD_SPLITS)
    T = u.shape[1]
    up = jnp.pad(u, ((0, 0), (CONV_PAD_LEFT, CONV_PAD_RIGHT), (0, 0)))
    xc = conv_b
    for tap in range(CONV_WIDTH):
        xc = xc + up[:, tap:tap + T] * conv_w[tap]
    y = (lru_direction(xc, w_a[0], b_a[0], w_x[0], b_x[0], lam[0], reverse=False)
         + lru_direction(xc, w_a[1], b_a[1], w_x[1], b_x[1], lam[1], reverse=True))
    y = y * jax.nn.silu(gate)
    return jnp.einsum('bte,ed->btd', y, w_out)

def second_inputs(seed: int = 0) -> dict:
    key = jax.random.key(seed)
    ks = jax.random.split(key, 24)
    f32 = jnp.float32

    def nrm(k, shape, scale):
        return jax.random.normal(k, shape, f32) * scale

    def gain(k, shape):
        return 1.0 + 0.01 * jax.random.normal(k, shape, f32)

    u = jax.random.uniform(ks[23], (N_ODD, 2, LRU_WIDTH), f32, 0.9, 0.999)
    a0 = u ** (1.0 / LRU_C)
    lru_lambda = jnp.log(a0) - jnp.log1p(-a0)

    return {
        "x": nrm(ks[0], (BATCH, SEQ, D_MODEL), 1.0),
        "meta_tokens": nrm(ks[1], (N_META, D_MODEL), 1.0),
        "norm_g": gain(ks[2], (DEPTH, D_MODEL)),
        "even_w_in": nrm(ks[3], (N_EVEN, D_MODEL, EVEN_IN), D_MODEL ** -0.5),
        "mla_g_q_lat": gain(ks[4], (N_EVEN, MLA_Q_RANK)),
        "mla_g_kv_lat": gain(ks[5], (N_EVEN, MLA_KV_RANK)),
        "mla_w_uq": nrm(ks[6], (N_EVEN, MLA_Q_RANK, MLA_HEADS, MLA_QK), MLA_Q_RANK ** -0.5),
        "mla_w_ukv": nrm(ks[7], (N_EVEN, MLA_KV_RANK, MLA_HEADS, MLA_NOPE + MLA_V), MLA_KV_RANK ** -0.5),
        "mla_g_qn": gain(ks[8], (N_EVEN, MLA_QK)),
        "mla_g_kn": gain(ks[9], (N_EVEN, MLA_QK)),
        "swa_g_qn": gain(ks[10], (N_EVEN, SWA_HEAD_DIM)),
        "swa_g_kn": gain(ks[11], (N_EVEN, SWA_HEAD_DIM)),
        "swa_sink": nrm(ks[12], (N_EVEN, SWA_HEADS), 0.5),
        "even_w_out": nrm(ks[13], (N_EVEN, D_INNER, D_MODEL), D_INNER ** -0.5),
        "odd_w_in": nrm(ks[14], (N_ODD, D_MODEL, ODD_IN), D_MODEL ** -0.5),
        "lru_conv_w": nrm(ks[15], (N_ODD, CONV_WIDTH, LRU_WIDTH), CONV_WIDTH ** -0.5),
        "lru_conv_b": nrm(ks[16], (N_ODD, LRU_WIDTH), 0.01),
        "lru_w_a": nrm(ks[17], (N_ODD, 2, LRU_BLOCKS, LRU_BLOCK_DIM, LRU_BLOCK_DIM), LRU_BLOCK_DIM ** -0.5),
        "lru_b_a": nrm(ks[18], (N_ODD, 2, LRU_WIDTH), 0.01),
        "lru_w_x": nrm(ks[19], (N_ODD, 2, LRU_BLOCKS, LRU_BLOCK_DIM, LRU_BLOCK_DIM), LRU_BLOCK_DIM ** -0.5),
        "lru_b_x": nrm(ks[20], (N_ODD, 2, LRU_WIDTH), 0.01),
        "lru_lambda": lru_lambda,
        "odd_w_out": nrm(ks[21], (N_ODD, D_INNER, D_MODEL), D_INNER ** -0.5),
    }

def second_block(x, meta_tokens, norm_g, even_w_in, mla_g_q_lat, mla_g_kv_lat, mla_w_uq, mla_w_ukv,
              mla_g_qn, mla_g_kn, swa_g_qn, swa_g_kn, swa_sink, even_w_out,
              odd_w_in, lru_conv_w, lru_conv_b, lru_w_a, lru_b_a, lru_w_x, lru_b_x,
              lru_lambda, odd_w_out):
    B = x.shape[0]
    meta = jnp.broadcast_to(meta_tokens.astype(x.dtype)[None], (B, N_META, D_MODEL))
    h = jnp.concatenate([meta, x], axis=1)
    T = h.shape[1]
    rope_mla = rope_tables_2(T, MLA_ROPE)
    rope_swa = rope_tables_2(T, SWA_HEAD_DIM)
    for l in range(DEPTH):
        z = rms_norm(h, norm_g[l])
        j = l // 2
        if l % 2 == 0:
            y = even_layer(z, even_w_in[j], mla_g_q_lat[j], mla_g_kv_lat[j], mla_w_uq[j], mla_w_ukv[j],
                           mla_g_qn[j], mla_g_kn[j], swa_g_qn[j], swa_g_kn[j], swa_sink[j],
                           even_w_out[j], rope_mla, rope_swa)
        else:
            y = odd_layer(z, odd_w_in[j], lru_conv_w[j], lru_conv_b[j], lru_w_a[j], lru_b_a[j],
                          lru_w_x[j], lru_b_x[j], lru_lambda[j], odd_w_out[j])
        h = h + y
    return h[:, N_META:]


def setup_inputs(seed=0):
    out = dict(first_inputs(seed))
    for name, value in second_inputs(seed + 1).items():
        if name != "x":
            out[name + "_2"] = value
    return out


def reference(
    x, positions, ln_mix_g, ln_mix_b, ln_ffn_g, ln_ffn_b, ssm_w_in, ssm_conv_w, ssm_conv_b,
    ssm_dt_bias, ssm_a_log, ssm_d, ssm_norm_w, ssm_w_out, attn_w_qkv, attn_lam_q1, attn_lam_k1,
    attn_lam_q2, attn_lam_k2, attn_subln_w, attn_w_o, moe_w_group, moe_w_expert, moe_w_gate,
    moe_w_up, moe_w_down, meta_tokens_2, norm_g_2, even_w_in_2, mla_g_q_lat_2, mla_g_kv_lat_2,
    mla_w_uq_2, mla_w_ukv_2, mla_g_qn_2, mla_g_kn_2, swa_g_qn_2, swa_g_kn_2, swa_sink_2,
    even_w_out_2, odd_w_in_2, lru_conv_w_2, lru_conv_b_2, lru_w_a_2, lru_b_a_2, lru_w_x_2,
    lru_b_x_2, lru_lambda_2, odd_w_out_2,
):
    x = first_block(
        x, positions, ln_mix_g, ln_mix_b, ln_ffn_g, ln_ffn_b, ssm_w_in, ssm_conv_w, ssm_conv_b,
        ssm_dt_bias, ssm_a_log, ssm_d, ssm_norm_w, ssm_w_out, attn_w_qkv, attn_lam_q1,
        attn_lam_k1, attn_lam_q2, attn_lam_k2, attn_subln_w, attn_w_o, moe_w_group,
        moe_w_expert, moe_w_gate, moe_w_up, moe_w_down,
    )
    return second_block(
        x, meta_tokens_2, norm_g_2, even_w_in_2, mla_g_q_lat_2, mla_g_kv_lat_2, mla_w_uq_2,
        mla_w_ukv_2, mla_g_qn_2, mla_g_kn_2, swa_g_qn_2, swa_g_kn_2, swa_sink_2, even_w_out_2,
        odd_w_in_2, lru_conv_w_2, lru_conv_b_2, lru_w_a_2, lru_b_a_2, lru_w_x_2, lru_b_x_2,
        lru_lambda_2, odd_w_out_2,
    )


_drawn_inputs = setup_inputs


def setup_inputs(seed=0):
    import zlib

    import numpy as np

    out = dict(_drawn_inputs(seed))
    spreads = {}
    factors = {'ssm_d': 5.437,
     'ssm_norm_w': 3.256,
     'attn_lam_k2': 3.53,
     'attn_subln_w': 5.825,
     'norm_g_2': 6.636,
     'mla_g_q_lat_2': 8.0,
     'mla_g_kv_lat_2': 8.0,
     'mla_g_qn_2': 8.0,
     'mla_g_kn_2': 8.0,
     'swa_g_qn_2': 8.0,
     'swa_g_kn_2': 8.0,
     'swa_sink_2': 8.0,
     'lru_b_a_2': 64.0,
     'lru_b_x_2': 63.924,
     'lru_conv_b_2': 8.0}
    for name, (base, spread) in spreads.items():
        noise = np.random.default_rng([zlib.crc32(name.encode()), seed]).standard_normal(out[name].shape)
        drawn = base * np.exp(spread * noise) if base else spread * noise
        out[name] = jnp.asarray(drawn.astype(out[name].dtype))
    for name, factor in factors.items():
        out[name] = (out[name] * factor).astype(out[name].dtype)
    return out
```

```python
import math
from contextlib import ExitStack

import numpy as np
import concourse.bass as bass
from concourse import mybir

ALU = mybir.AluOpType
ACT = mybir.ActivationFunctionType
AXX = mybir.AxisListType.X
F32 = mybir.dt.float32
BF16 = mybir.dt.bfloat16
I32 = mybir.dt.int32
U32 = mybir.dt.uint32
U16 = mybir.dt.uint16

NSLOT = 7
CAP = 64
OVERFLOW = True
NE = 32
ALPHA = 4.0 ** 0.25
EPS1 = 1e-5
EPS2 = 1e-6
NEG = -1e30
LOW = -3.0e38
LI = 0.8 - 0.6 * math.exp(-0.3)

COLS = {}
_n = 0
for _name, _w in (("conv_w", 128), ("conv_b", 32), ("norm_w", 16), ("subln", 1), ("ng0", 8), ("ng1", 8),
                  ("gq", 3), ("gkv", 2), ("lconv_w", 64), ("lconv_b", 16), ("ba", 32), ("bx", 32),
                  ("lam", 32), ("lamv", 4)):
    COLS[_name] = (_n, _w)
    _n += _w
NCOL = _n
ROWS = {}
_n = 0
for _name, _w in (("dt_bias", 32), ("a_log", 32), ("ssm_d", 32), ("mgq", 192), ("mgk", 192),
                  ("sgq", 128), ("sgk", 128), ("sink", 8), ("inv", 8), ("iota", 64)):
    ROWS[_name] = (_n, _w)
    _n += _w
NROW = _n


class Later:

    def matmul(self, *a, **k):
        return lambda e: e.matmul(*a, **k)

    def transpose(self, *a, **k):
        return lambda e: e.transpose(*a, **k)

    def tensor_copy(self, *a, **k):
        return lambda e: e.tensor_copy(*a, **k)

    def memset(self, *a, **k):
        return lambda e: e.memset(*a, **k)

    def tensor_tensor(self, *a, **k):
        return lambda e: e.tensor_tensor(*a, **k)

    def tensor_scalar(self, *a, **k):
        return lambda e: e.tensor_scalar(*a, **k)

    def scalar_tensor_tensor(self, *a, **k):
        return lambda e: e.scalar_tensor_tensor(*a, **k)

    def tensor_reduce(self, *a, **k):
        return lambda e: e.tensor_reduce(*a, **k)

    def reciprocal(self, *a, **k):
        return lambda e: e.reciprocal(*a, **k)

    def bn_stats(self, *a, **k):
        return lambda e: e.bn_stats(*a, **k)

    def bn_aggr(self, *a, **k):
        return lambda e: e.bn_aggr(*a, **k)

    def max(self, *a, **k):
        return lambda e: e.max(*a, **k)

    def max_index(self, *a, **k):
        return lambda e: e.max_index(*a, **k)

    def tensor_tensor_scan(self, *a, **k):
        return lambda e: e.tensor_tensor_scan(*a, **k)

    def copy(self, *a, **k):
        return lambda e: e.copy(*a, **k)

    def activation(self, *a, **k):
        return lambda e: e.activation(*a, **k)

    def dma_start(self, *a, **k):
        return lambda e: e.dma_start(*a, **k)

    def wait_ge(self, *a, **k):
        return lambda e: e.wait_ge(*a, **k)


LATER = Later()


class Queue:

    def __init__(self, sem):
        self.sem, self.items, self.n, self.seen = sem, [], 0, {}

    def wait(self, *toks):
        for tok in toks:
            if tok is None:
                continue
            if isinstance(tok, list):
                self.wait(*tok)
                continue
            sem, val = tok
            if self.seen.get(sem.name, 0) < val:
                self.seen[sem.name] = val
                self.items.append(LATER.wait_ge(sem, val))

    def now(self):
        return (self.sem, self.n) if self.n else None

    def raw(self, fn, *after):
        self.wait(*after)
        self.items.append(fn(LATER))

    def op(self, fn, *after):
        self.wait(*after)
        self.n += 1
        go = fn(LATER)
        self.items.append(lambda e: go(e).then_inc(self.sem, 1))
        return (self.sem, self.n)

    def seq(self, fn, *after):
        return self.op(fn, self.now(), *after)

    def dma(self, fn, dsem, *after):
        self.wait(*after)
        dsem[1] += 16
        go, s = fn(LATER), dsem[0]
        self.items.append(lambda e: go(e).then_inc(s, 16))
        return (dsem[0], dsem[1])

    def play(self, e):
        for f in self.items:
            f(e)


class Bank:

    def __init__(self, t):
        self.t, self.tok, self.held = t, None, False

    @property
    def free(self):
        return self.tok

    @free.setter
    def free(self, tok):
        self.tok, self.held = tok, False


def weave(*gens):
    gens = [list(g) for g in gens]
    while gens:
        for g in list(gens):
            for _ in range(g[1]):
                try:
                    next(g[0])
                except StopIteration:
                    gens.remove(g)
                    break


def chain(*gens):
    for g in gens:
        yield from g


def run(gen):
    for _ in gen:
        pass


def bc(ap, axis, n):
    a = ap.unsqueeze(axis)
    s = list(a.shape)
    s[axis] = n
    return a.broadcast_to(s)


def build(nc, A, out):
    ctx = ExitStack()
    with ctx:
        def sb(name, shape, dt=F32):
            return ctx.enter_context(nc.sbuf_tensor(name, shape, dt))

        def sem(name):
            return ctx.enter_context(nc.semaphore(name))

        pe, dve, act, pool, sp = (Queue(sem("s_" + n)) for n in ("pe", "dve", "act", "pool", "sp"))
        banks = [Bank(ctx.enter_context(nc.psum_tensor(f"ps{i}", [128, 512], F32))) for i in range(8)]
        rot = [0, 0]

        def bank8():
            for _ in range(8):
                rot[0] += 1
                b = banks[rot[0] % 8]
                if not b.held:
                    b.held = True
                    return b
            raise AssertionError("every bank is held")

        def bank4():
            rot[1] += 1
            return banks[rot[1] % 4]

        ring = sb("ring", [128, NSLOT, 4096])
        slot_sem = [[sem(f"slot{i}"), 0] for i in range(NSLOT)]
        slot_free = [None] * NSLOT
        rp = [0]

        cF = sb("cF", [128, 3, 128])
        ident, triu, triS = cF[:, 0, :], cF[:, 1, :], cF[:, 2, :]
        cB = sb("cB", [128, 8, 128], BF16)
        identb, negU = cB[:, 0, :], cB[:, 1:5, :]
        swm = sb("swm", [128, 3, 272], BF16)
        ones = sb("ones", [128, 128])
        halves = sb("halves", [128, 8])
        flags = sb("flags", [128, 2])
        col = sb("col", [128, NCOL])
        row = sb("row", [128, NROW])
        posi = sb("posi", [128, 2], I32)

        def C(name, i=0, n=1):
            b = COLS[name][0]
            return col[:, b + i:b + i + n]

        def R(name):
            b, w = ROWS[name]
            return row[:, b:b + w]

        h = sb("h", [128, 3, 1024])
        xT = sb("xT", [128, 8, 384])
        lnb = sb("lnb", [128, 2, 1024])
        big = sb("big", [128, 16 * 272])
        work = sb("work", [128, 7680])
        small = sb("small", [128, 704])

        xs_ = {n: sem("x_" + n) for n in ("pe", "dve", "act", "dma", "arrived", "go_pe", "go_act", "go_sp")}
        ln_sem = [sem("lnd"), 0]
        c_sem = [sem("cst"), 0]
        out_sem = [sem("outd"), 0]
        d2 = [sem("d2"), 0]

        def area(t, at, shape):
            n = int(np.prod(shape))
            ap = t[:, at:at + n]
            if len(shape) == 2:
                ap = ap.rearrange("p (a b) -> p a b", a=shape[0])
            elif len(shape) == 3:
                ap = ap.rearrange("p (a b c) -> p a b c", a=shape[0], b=shape[1])
            elif len(shape) == 4:
                ap = ap.rearrange("p (a b c d) -> p a b c d", a=shape[0], b=shape[1], c=shape[2])
            return ap

        class Arena:
            def __init__(self, t, size):
                self.t, self.size, self.at = t, size, 0

            def __call__(self, *shape):
                n = int(np.prod(shape))
                assert self.at + n <= self.size, (self.at, n, self.size)
                a = area(self.t, self.at, shape)
                self.at += n
                return a

        def everyone():
            return [q.now() for q in (pe, dve, act, pool)]

        def barrier():
            t = everyone()
            for q in (pe, dve, act, pool):
                q.wait(*t)

        def cload(dst, src):
            return sp.dma(lambda e: e.dma_start(dst, src), c_sem)

        cload(h[:, 0:2, :], A["x"].rearrange("a (t p) d -> p (a t) d", p=128))
        cload(cF[:, :, :], A["cF"])
        cload(cB[:, :, :].bitcast(U16), A["cB"])
        cload(col[:, :], A["col"])
        cload(row[:, :], A["row"].broadcast_to([128, NROW]))
        cload(posi[:, :], A["pos"])
        tokC = cload(swm[:, :, :].bitcast(U16), A["swm"])

        def chunk(*pieces):
            i = rp[0] % NSLOT
            rp[0] += 1
            v = ring[:, i, :]
            for n, (view, src) in enumerate(pieces):
                tok = sp.dma(lambda e, d=view(v), s=src: e.dma_start(d, s), slot_sem[i],
                             slot_free[i] if n == 0 else None)
            slot_free[i] = None
            return v, tok, i

        def done(c, tok):
            slot_free[c[2]] = tok

        def kview(k, n, k0=0, n0=0, w=None):
            return lambda v: v[:, 0:k * n].rearrange("p (k n) -> p k n", k=k)[:, :, n0:n0 + (w or n)]

        def src(w, r0, r1, c0, c1):
            return w[r0:r1, c0:c1].rearrange("(k p) n -> p k n", p=128)

        def load_ln(i):
            return sp.dma(lambda e: e.dma_start(lnb[:, :, :], A["lnp"][i:i + 1, :, :].broadcast_to([128, 2, 1024])),
                          ln_sem, dve.now(), pool.now())

        t_ones = dve.seq(lambda e: e.memset(ones[:, :], 1.0))
        dve.seq(lambda e: e.memset(halves[:, :], -0.5))
        t_xz = dve.seq(lambda e: e.memset(xT[:, :, 256:384], 0.0))
        dve.seq(lambda e: e.memset(h[:, 2, :], 0.0))
        for q in (pe, dve, act, pool):
            q.wait(tokC, t_xz)

        def copy(q, dst, src_, *after):
            if q is act:
                return act.seq(lambda e: e.copy(dst, src_), *after)
            return q.seq(lambda e: e.tensor_copy(dst, src_), *after)

        def rsqrt(x):
            n = halves[:, 0:int(np.prod(x.shape[1:]))]
            if len(x.shape) == 3:
                n = n.rearrange("p (a b) -> p a b", a=x.shape[1])
            dve.wait(pool.seq(lambda e: e.tensor_tensor(x, x, n, ALU.pow), dve.now()))

        def to_T(t, tok):
            last = []
            for k in range(0, 8, 4):
                b = bank8()
                pe.wait(tok, b.free)
                for kk in range(4):
                    tp = pe.op(lambda e: e.transpose(b.t[:, kk * 128:kk * 128 + 128],
                                                     h[:, t, (k + kk) * 128:(k + kk + 1) * 128], ident))
                b.free = copy(act, xT[:, k:k + 4, t * 128:(t + 1) * 128],
                              b.t[:, :].rearrange("p (k t) -> p k t", k=4), tp)
                last.append(b.free)
            return last

        def add_residual(acc, tacc):
            for t in range(2):
                for n in range(2):
                    b = acc[t][n]
                    hh = h[:, t, n * 512:(n + 1) * 512]
                    b.free = dve.seq(lambda e: e.scalar_tensor_tensor(
                        out=hh, in0=hh, scalar=ALPHA, in1=b.t[:, :], op0=ALU.mult, op1=ALU.add), tacc)

        def layer_norm(tln):
            m = Arena(small, 704)
            st, mv, rs, nm = m(2, 2, 6), m(2, 2), m(2), m(2)
            for t in range(2):
                for n in range(2):
                    dve.seq(lambda e: e.bn_stats(st[:, t, n, :], h[:, t, n * 512:(n + 1) * 512]))
                dve.seq(lambda e: e.bn_aggr(mv[:, t, :], st[:, t, :, :].rearrange("p a b -> p (a b)")))
            dve.seq(lambda e: e.tensor_scalar(rs, mv[:, :, 1], EPS1, None, ALU.add))
            rsqrt(rs)
            tk = dve.seq(lambda e: e.scalar_tensor_tensor(out=nm, in0=mv[:, :, 0], scalar=-1.0, in1=rs,
                                                          op0=ALU.mult, op1=ALU.mult))
            last = []
            for t in range(2):
                tk2 = act.seq(lambda e: e.activation(h[:, t, :], h[:, t, :], ACT.Identity, bias=nm[:, t:t + 1],
                                                     scale=rs[:, t:t + 1]), tk)
                dve.seq(lambda e: e.tensor_tensor(h[:, t, :], h[:, t, :], lnb[:, 0, :], ALU.mult), tk2, tln)
                tk3 = dve.seq(lambda e: e.tensor_tensor(h[:, t, :], h[:, t, :], lnb[:, 1, :], ALU.add))
                last += to_T(t, tk3)
            return tk3, last

        def mm(outp, l, r, start, stop, skip=False):
            return lambda e: e.matmul(outp, l, r, start=start, stop=stop, skip_group_check=skip)

        def project(bout, lhs, rhs, ks, *after, start=True, stop=True):
            ks = list(ks)
            pe.wait(*after)
            for k in ks[:-1]:
                pe.raw(mm(bout, lhs(k), rhs(k), start and k == ks[0], False))
            k = ks[-1]
            return pe.op(mm(bout, lhs(k), rhs(k), start and k == ks[0], stop))

        def out_proj(w, actT, t_act, acc, halves_):
            kt = w.shape[0] // 128
            for k0 in halves_:
                for n in range(2):
                    c = chunk((kview(8, 512), src(w, k0 * 128, k0 * 128 + 1024, n * 512, n * 512 + 512)))
                    wv = kview(8, 512)(c[0])
                    for t in range(2):
                        b = acc[t][n]
                        tk = project(b.t[:, :], lambda k: actT[:, k, t * 128:(t + 1) * 128],
                                     lambda k: wv[:, k - k0, :], range(k0, k0 + 8),
                                     c[1], t_act(), b.free if k0 == 0 else None,
                                     start=k0 == 0, stop=k0 == kt - 8)
                        yield
                    done(c, tk)

        def moe(layer, txT, th):
            barrier()
            assert not any(b.held for b in banks)
            tln = load_ln(layer * 2 + 1)
            m = Arena(work, 7680)
            wr = m(8, 36)
            tw = sp.dma(lambda e: e.dma_start(wr, A["wr"][layer]), d2, everyone())
            gl, el, mk, wg, rk, oh, tmp = m(2, 8), m(2, 32), m(2, 32), m(2, 32), m(2, 32), m(2, 32), m(2, 32)
            gm, mx, mi, fi, s4 = m(2, 4), m(2, 8), m(2, 8), m(2, 8), m(2, 8)
            wres, wtmp, flag = m(2, 32), m(2, 32), flags[:, layer:layer + 1]
            S, SW, SWT = m(2, 2, 128), m(2, 2, 128), m(2, 2, 128)
            xgT, sg, hs, hT = m(2, 8, 128), m(512), m(512), m(4, 128)
            ys, xgs = area(big, 0, (1024,)), area(big, 1024, (1024,))
            iota4, iota32, iota64 = R("iota")[:, 0:4], R("iota")[:, 0:32], R("iota")[:, 0:64]
            b = bank4()
            for t in range(2):
                tk = project(b.t[:, t * 64:t * 64 + 36], lambda k: xT[:, k, t * 128:(t + 1) * 128],
                             lambda k: wr[:, k, :], range(8), txT, tw, b.free)
            lg = b.t[:, 0:128].rearrange("p (t n) -> p t n", t=2)
            dve.seq(lambda e: e.memset(gl, LOW))
            dve.seq(lambda e: e.tensor_copy(gl[:, :, 0:4], lg[:, :, 0:4]), tk)
            b.free = dve.seq(lambda e: e.tensor_copy(el, lg[:, :, 4:36]))
            for t in range(2):
                dve.seq(lambda e, t=t: e.max(mx[:, t, :], gl[:, t, :]))
                dve.seq(lambda e, t=t: e.max_index(mi[:, t, :].bitcast(U32), mx[:, t, :], gl[:, t, :]))
                dve.seq(lambda e, t=t: e.tensor_copy(fi[:, t, :], mi[:, t, :].bitcast(U32)))
                dve.seq(lambda e, t=t: e.tensor_scalar(gm[:, t, :], iota4, fi[:, t, 0:1], None, ALU.is_equal))
                tk = dve.seq(lambda e, t=t: e.tensor_scalar(s4[:, t, 0:1], mx[:, t, 0:1], -1.0, None, ALU.mult))
                tk = act.seq(lambda e, t=t: e.activation(gl[:, t, 0:4], gl[:, t, 0:4], ACT.Exp, bias=s4[:, t, 0:1],
                                                         accum_out=s4[:, t, 1:2]), tk)
                dve.seq(lambda e, t=t: e.reciprocal(s4[:, t, 2:3], s4[:, t, 1:2]), tk)
                dve.seq(lambda e, t=t: e.tensor_tensor(
                    el[:, t, :].rearrange("p (g e) -> p g e", g=4), el[:, t, :].rearrange("p (g e) -> p g e", g=4),
                    bc(gm[:, t, :], 2, 8), ALU.mult))
                dve.seq(lambda e, t=t: e.tensor_scalar(gm[:, t, :], gm[:, t, :], 1.0, -LOW, ALU.subtract, ALU.mult))
                dve.seq(lambda e, t=t: e.tensor_tensor(
                    el[:, t, :].rearrange("p (g e) -> p g e", g=4), el[:, t, :].rearrange("p (g e) -> p g e", g=4),
                    bc(gm[:, t, :], 2, 8), ALU.add))
                dve.seq(lambda e, t=t: e.max(mx[:, t, :], el[:, t, :]))
                dve.seq(lambda e, t=t: e.max_index(mi[:, t, :].bitcast(U32), mx[:, t, :], el[:, t, :]))
                dve.seq(lambda e, t=t: e.tensor_copy(fi[:, t, :], mi[:, t, :].bitcast(U32)))
                tk = dve.seq(lambda e, t=t: e.tensor_tensor(s4[:, t, 3:4], mx[:, t, 1:2], mx[:, t, 0:1], ALU.subtract))
                tk = act.seq(lambda e, t=t: e.activation(s4[:, t, 4:5], s4[:, t, 3:4], ACT.Exp), tk)
                dve.seq(lambda e, t=t: e.tensor_scalar(s4[:, t, 5:6], s4[:, t, 4:5], 1.0, None, ALU.add), tk)
                dve.seq(lambda e, t=t: e.reciprocal(s4[:, t, 6:7], s4[:, t, 5:6]))
                dve.seq(lambda e, t=t: e.tensor_tensor(s4[:, t, 6:7], s4[:, t, 6:7], s4[:, t, 2:3], ALU.mult))
                dve.seq(lambda e, t=t: e.tensor_tensor(s4[:, t, 7:8], s4[:, t, 6:7], s4[:, t, 4:5], ALU.mult))
                dve.seq(lambda e, t=t: e.tensor_scalar(mk[:, t, :], iota32, fi[:, t, 0:1], None, ALU.is_equal))
                dve.seq(lambda e, t=t: e.tensor_scalar(oh[:, t, :], iota32, fi[:, t, 1:2], None, ALU.is_equal))
                dve.seq(lambda e, t=t: e.tensor_scalar(tmp[:, t, :], oh[:, t, :], s4[:, t, 7:8], None, ALU.mult))
                dve.seq(lambda e, t=t: e.scalar_tensor_tensor(
                    out=wg[:, t, :], in0=mk[:, t, :], scalar=s4[:, t, 6:7], in1=tmp[:, t, :],
                    op0=ALU.mult, op1=ALU.add))
                tm = dve.seq(lambda e, t=t: e.tensor_tensor(mk[:, t, :], mk[:, t, :], oh[:, t, :], ALU.add))
            b = bank4()
            pe.wait(tm, b.free)
            pe.op(mm(b.t[:, 0:32], triS, mk[:, 0, :], True, True))
            pe.op(mm(b.t[:, 32:64], ones[:, :], mk[:, 0, :], True, False))
            tk = pe.op(mm(b.t[:, 32:64], triS, mk[:, 1, :], False, True))
            dve.seq(lambda e: e.scalar_tensor_tensor(
                out=rk.rearrange("p t e -> p (t e)"), in0=b.t[:, 0:64], scalar=1.0,
                in1=mk.rearrange("p t e -> p (t e)"), op0=ALU.add, op1=ALU.mult), tk)
            b.free = dve.seq(lambda e: e.tensor_scalar(rk, rk, 1.0, None, ALU.subtract))

            dve.seq(lambda e: e.scalar_tensor_tensor(
                out=wres.rearrange("p t e -> p (t e)"), in0=rk.rearrange("p t e -> p (t e)"), scalar=CAP - 0.5,
                in1=wg.rearrange("p t e -> p (t e)"), op0=ALU.is_gt, op1=ALU.mult))
            b = bank4()
            pe.wait(b.free)
            pe.op(mm(b.t[:, 0:32], ones[:, :], mk[:, 0, :], True, False))
            tk = pe.op(mm(b.t[:, 0:32], ones[:, :], mk[:, 1, :], False, True))
            b.free = dve.seq(lambda e: e.tensor_reduce(flag, b.t[:, 0:32], AXX, ALU.max), tk)
            tflag = dve.seq(lambda e: e.tensor_scalar(flag.bitcast(I32), flag, CAP + 0.5, None, ALU.is_gt))

            acc = [[banks[4], banks[5]], [banks[6], banks[7]]]
            accfree = [x.free for p in acc for x in p]
            gate_w, up_w, down_w = A["wg"], A["wu"], A["wd"]
            NP = NE // 2
            tG, tSWT, tX, tH, tY, tD, banksof = {}, {}, {}, {}, {}, {}, {}

            def lists(p):
                i = p % 2
                for j in range(2):
                    e_ = 2 * p + j
                    for t in range(2):
                        dve.seq(lambda e: e.tensor_scalar(
                            S[:, i, t, 64 * j:64 * j + 64], iota64, rk[:, t, e_:e_ + 1], None, ALU.is_equal),
                            tX.get(p - 2), tSWT.get(p - 2))
                        tk = dve.seq(lambda e: e.tensor_scalar(
                            SW[:, i, t, 64 * j:64 * j + 64], iota64, rk[:, t, e_:e_ + 1], wg[:, t, e_:e_ + 1],
                            ALU.is_equal, ALU.mult))
                return tk

            def gather(p):
                tS = lists(p)
                for n in range(2):
                    b = bank4()
                    pe.wait(tS, th, b.free)
                    for t in range(2):
                        tk = pe.op(mm(b.t[:, :], S[:, p % 2, t, :], h[:, t, n * 512:(n + 1) * 512], t == 0, t == 1))
                    b.free = copy(act if n else dve, xgs[:, n * 512:(n + 1) * 512], b.t[:, :], tk, tX.get(p - 1))
                    tG[p, n] = b.free
                b = bank4()
                pe.wait(b.free)
                for t in range(2):
                    tk = pe.op(lambda e: e.transpose(b.t[:, t * 128:(t + 1) * 128], SW[:, p % 2, t, :], ident))
                b.free = tSWT[p] = act.seq(lambda e: e.copy(
                    SWT[:, p % 2, :, :], b.t[:, 0:256].rearrange("p (t n) -> p t n", t=2)), tk, tD.get(p - 2))

            def turn_x(p):
                for n in range(2):
                    b = bank4()
                    pe.wait(tG[p, n], b.free)
                    for k in range(4):
                        s_ = xgs[:, (4 * n + k) * 128:(4 * n + k + 1) * 128]
                        tX[p] = pe.op(lambda e: e.transpose(b.t[:, k * 128:(k + 1) * 128], s_, ident))
                    b.free = tG[p, 2 + n] = copy(act if n else dve, xgT[:, p % 2, 4 * n:4 * n + 4, :],
                                                 b.t[:, :].rearrange("p (k s) -> p k s", k=4), tX[p])

            def hidden(p):
                bk = []
                for w in (gate_w, up_w):
                    cs_ = [chunk((kview(8, 512), w[layer, 2 * p + j].rearrange("(k p) n -> p k n", p=128)))
                           for j in range(2)]
                    b = bank4()
                    bk.append(b)
                    pe.wait(tG[p, 2], tG[p, 3], b.free, cs_[0][1], cs_[1][1])
                    for k in range(8):
                        for j in range(2):
                            tk = pe.op(mm(b.t[64 * j:64 * j + 64, :], xgT[:, p % 2, k, 64 * j:64 * j + 64],
                                          kview(8, 512)(cs_[j][0])[:, k, :], k == 0, k == 7))
                    for c in cs_:
                        done(c, tk)
                    if w is gate_w:
                        b.free = tg = act.seq(lambda e: e.activation(sg, b.t[:, :], ACT.Silu), tk, dve.now())
                b.free = tH[p] = dve.seq(lambda e: e.tensor_tensor(hs, sg, b.t[:, :], ALU.mult), tk, tg, tH.get("t"))

            def turn_h(p):
                b = bank4()
                pe.wait(tH[p], b.free)
                for f in range(4):
                    tk = pe.op(lambda e: e.transpose(b.t[:, f * 128:(f + 1) * 128], hs[:, f * 128:(f + 1) * 128], ident))
                tH["t"] = tk
                b.free = tH["T"] = act.seq(lambda e: e.copy(hT, b.t[:, :].rearrange("p (f s) -> p f s", f=4)), tk,
                                           tY.get(p - 1))

            def down(p):
                cs_ = [chunk((kview(4, 1024), down_w[layer, 2 * p + j].rearrange("(k p) n -> p k n", p=128)))
                       for j in range(2)]
                for n in range(2):
                    b = bank4()
                    pe.wait(tH["T"], b.free, cs_[0][1], cs_[1][1])
                    for f in range(4):
                        for j in range(2):
                            tk = pe.op(mm(b.t[64 * j:64 * j + 64, :], hT[:, f, 64 * j:64 * j + 64],
                                          kview(4, 1024)(cs_[j][0])[:, f, n * 512:(n + 1) * 512], f == 0, f == 3))
                    b.free = tY[p, n] = copy(act if n else dve, ys[:, n * 512:(n + 1) * 512], b.t[:, :], tk,
                                             tD.get(p - 1))
                tY[p] = tk
                for c in cs_:
                    done(c, tk)

            def spread(p):
                for n in range(2):
                    for t in range(2):
                        pe.wait(accfree if p == 0 else None, tY[p, n], tSWT[p])
                        tk = pe.op(mm(acc[t][n].t[:, :], SWT[:, p % 2, t, :], ys[:, n * 512:(n + 1) * 512],
                                      p == 0, p == NP - 1))
                tD[p] = tk

            gather(0)
            turn_x(0)
            for p in range(NP):
                hidden(p)
                if p:
                    spread(p - 1)
                if p + 1 < NP:
                    gather(p + 1)
                turn_h(p)
                if p + 1 < NP:
                    turn_x(p + 1)
                down(p)
            spread(NP - 1)
            add_residual(acc, tD[NP - 1])
            if OVERFLOW:
                crowded(layer, flag, tflag, wres, wtmp)
            for b in banks:
                b.held = False
            return layer_norm(tln)

        def crowded(layer, flag, tflag, wres, wtmp):
            barrier()
            sp.wait(*everyone(), *slot_free)
            X = {n: Queue(xs_[n]) for n in ("pe", "dve", "act")}
            xp, xd, xa, xsp = X["pe"], X["dve"], X["act"], Queue(xs_["pe"])
            gx, hx, hTx = area(big, 2048, (512,)), area(big, 2560, (512,)), area(big, 3072, (4, 128))
            wgv, wuv, wdv = kview(8, 512)(ring[:, 0, :]), kview(8, 512)(ring[:, 1, :]), kview(4, 1024)(ring[:, 2, :])
            tw = (xs_["dma"], 48)
            B = [Bank(x.t) for x in banks]
            for t in range(2):
                g, u = B[0], B[1]
                for bb, wv in ((g, wgv), (u, wuv)):
                    xp.wait(tw, bb.free)
                    for k in range(8):
                        tk = xp.op(mm(bb.t[:, :], xT[:, k, t * 128:(t + 1) * 128], wv[:, k, :], k == 0, k == 7))
                tg = xa.seq(lambda e: e.activation(gx, g.t[:, :], ACT.Silu), tk, xd.now())
                xd.seq(lambda e: e.tensor_tensor(hx, gx, u.t[:, :], ALU.mult), tg)
                th_ = xd.seq(lambda e: e.tensor_scalar(hx, hx, wres[:, t, 0:1], None, ALU.mult))
                g.free = u.free = th_
                xp.wait(th_, B[2].free)
                for f in range(4):
                    tk = xp.op(lambda e: e.transpose(B[2].t[:, f * 128:(f + 1) * 128], hx[:, f * 128:(f + 1) * 128],
                                                     ident))
                B[2].free = tT = xd.seq(lambda e: e.tensor_copy(hTx, B[2].t[:, :].rearrange("p (f s) -> p f s", f=4)), tk)
                for n in range(2):
                    bb = B[3 + n]
                    xp.wait(tT, bb.free)
                    for f in range(4):
                        tk = xp.op(mm(bb.t[:, :], hTx[:, f, :], wdv[:, f, n * 512:(n + 1) * 512], f == 0, f == 3))
                    hh = h[:, t, n * 512:(n + 1) * 512]
                    bb.free = xd.seq(lambda e: e.tensor_tensor(hh, hh, bb.t[:, :], ALU.add), tk)
            xd.seq(lambda e: e.tensor_copy(wtmp[:, :, 0:31], wres[:, :, 1:32]))
            xd.seq(lambda e: e.tensor_copy(wres[:, :, 0:31], wtmp[:, :, 0:31]))
            counted = (xs_["pe"], xs_["dve"], xs_["act"], xs_["dma"], xs_["arrived"])

            def section(q, body, mine, go):
                def play(e):
                    v = e.value_load(flag[0:1, 0:1].bitcast(I32))
                    with e.If(v):
                        with e.Fori(0, NE) as i:
                            body(e, i)
                            if mine is not None:
                                e.wait_ge(mine.sem, mine.n)
                            if go is not None:
                                e.sem_inc(xs_["arrived"], 1)
                                e.wait_ge(go, 1)
                                e.sem_clear(go)
                            else:
                                e.wait_ge(xs_["arrived"], 3)
                                for s_ in counted:
                                    e.sem_clear(s_)
                                for s_ in ("go_pe", "go_act", "go_sp"):
                                    e.sem_inc(xs_[s_], 1)
                q.wait(tflag)
                q.items.append(play)

            def loads(e, i):
                for n, w in enumerate((A["wg"], A["wu"], A["wd"])):
                    k = 4 if n == 2 else 8
                    dst = kview(k, 4096 // k)(ring[:, n, :])
                    e.dma_start(dst, w[layer].rearrange("x (k p) n -> x p k n", p=128)[bass.ds(i, 1)]
                                .rearrange("x p k n -> p (x k) n")).then_inc(xs_["dma"], 16)
                e.wait_ge(xs_["dma"], 48)

            section(sp, loads, None, xs_["go_sp"])
            section(pe, lambda e, i: xp.play(e), xp, xs_["go_pe"])
            section(act, lambda e, i: xa.play(e), xa, xs_["go_act"])
            section(dve, lambda e, i: xd.play(e), xd, None)

        w_in, w_out = A["ssm_w_in"], A["ssm_w_out"]
        tx = to_T(0, tokC) + to_T(1, tokC)
        tln = load_ln(0)
        m = Arena(small, 704)
        dt, dtA, acum, nega, expa, dte = m(2, 32), m(2, 32), m(2, 32), m(32), m(2, 32), m(32)
        t1, t2 = m(2, 32), m(2, 32)
        ssq, rsg = m(4), m(4)
        m = Arena(work, 7680)
        wdt = m(8, 32)
        zs, cv, cs = m(2, 2, 256), m(4, 256), m(2, 4, 256)
        xdt, xD, yv = m(2, 256), m(2, 256), m(2, 256)
        dec = m(2, 4, 128)
        xde, Bl, S0 = m(256), m(128), m(256)
        ygT = area(big, 0, (16, 256))
        tw = sp.dma(lambda e: e.dma_start(wdt, src(w_in, 0, 1024, 6144, 6176)), d2)
        b = bank8()
        for t in range(2):
            tk = project(b.t[:, t * 32:t * 32 + 32], lambda k: xT[:, k, t * 128:(t + 1) * 128],
                         lambda k: wdt[:, k, :], range(8), tx, tw, b.free)
        b.free = dve.seq(lambda e: e.tensor_tensor(dt, b.t[:, 0:64].rearrange("p (t n) -> p t n", t=2),
                                                   bc(R("dt_bias"), 1, 2), ALU.add), tk)
        tk = dve.seq(lambda e: e.scalar_tensor_tensor(out=t1, in0=dt, scalar=-1.0, in1=dt, op0=ALU.mult, op1=ALU.max))
        tk = act.seq(lambda e: e.activation(t1, t1, ACT.Exp, scale=-1.0), tk)
        tk = act.seq(lambda e: e.activation(t2, t1, ACT.Ln, bias=1.0), tk)
        dve.seq(lambda e: e.scalar_tensor_tensor(out=dt, in0=dt, scalar=0.0, in1=t2, op0=ALU.max, op1=ALU.add), tk)
        tk = act.seq(lambda e: e.activation(nega, R("a_log"), ACT.Exp))
        dve.seq(lambda e: e.tensor_scalar(nega, nega, -1.0, None, ALU.mult), tk)
        tk = dve.seq(lambda e: e.tensor_tensor(dtA, dt, bc(nega, 1, 2), ALU.mult))
        b = bank8()
        pe.wait(tk, b.free)
        for t in range(2):
            pe.op(mm(b.t[:, t * 32:t * 32 + 32], triu, dtA[:, t, :], True, True))
        tk = pe.op(mm(b.t[:, 64:96], ones[:, :], dtA[:, 0, :], True, True))
        dve.seq(lambda e: e.tensor_copy(acum.rearrange("p t n -> p (t n)"), b.t[:, 0:64]), tk)
        b.free = dve.seq(lambda e: e.tensor_tensor(dte, b.t[:, 64:96], acum[:, 0, :], ALU.subtract))
        tk = act.seq(lambda e: e.activation(dte, dte, ACT.Exp), b.free)
        tk = act.seq(lambda e: e.activation(expa, acum, ACT.Exp), tk)
        t_small = dve.seq(lambda e: e.tensor_tensor(dte, dte, dt[:, 0, :], ALU.mult), tk)

        T = {}

        def mamba_in(g):
            i = g % 2
            c = chunk((kview(8, 512, n0=0, w=256), src(w_in, 0, 1024, 256 * g, 256 * g + 256)),
                      (kview(8, 512, n0=256, w=256), src(w_in, 0, 1024, 2048 + 256 * g, 2048 + 256 * g + 256)))
            wv = kview(8, 512)(c[0])
            if i == 0:
                T["cBC"] = chunk(
                    (kview(8, 512, n0=0, w=256), src(w_in, 0, 1024, 4096 + 128 * g, 4096 + 128 * g + 256)),
                    (kview(8, 512, n0=256, w=256), src(w_in, 0, 1024, 5120 + 128 * g, 5120 + 128 * g + 256)))
            cBC = T["cBC"]
            wb = kview(8, 512)(cBC[0])
            for half in range(2):
                b = bank8()
                for j in range(2):
                    if half == 0:
                        lw, tw = wv[:, :, 256 + 128 * j:384 + 128 * j], c[1]
                    else:
                        lw, tw = wb[:, :, 256 * j + 128 * i:256 * j + 128 * i + 128], cBC[1]
                    tk = project(b.t[:, j * 256:(j + 1) * 256], lambda k: lw[:, k, :], lambda k: xT[:, k, 0:256],
                                 range(8), tw, b.free)
                    if j == 0:
                        yield
                for j in range(2):
                    blk = 2 * g + j if half == 0 else 16 + 8 * j + g
                    ps = b.t[:, j * 256:(j + 1) * 256]
                    o = cv[:, 2 * half + j, :]
                    dve.seq(lambda e: e.tensor_scalar(
                        o, ps, C("conv_w", 4 * blk + 3), C("conv_b", blk), ALU.mult, ALU.add), tk, T.get(("cs", g - 1)))
                    for s in range(1, 4):
                        td = dve.seq(lambda e: e.scalar_tensor_tensor(
                            out=o[:, s:256], in0=ps[:, 0:256 - s], scalar=C("conv_w", 4 * blk + 3 - s),
                            in1=o[:, s:256], op0=ALU.mult, op1=ALU.add))
                b.free = td
                yield
            if i == 1:
                done(cBC, tk)
            T["cs", g] = act.seq(lambda e: e.activation(cs[:, i], cv, ACT.Silu), td, T.get(("used", g - 2)))
            b = bank8()
            for t in range(2):
                tk = project(b.t[:, t * 256:(t + 1) * 256], lambda k: xT[:, k, t * 128:(t + 1) * 128],
                             lambda k: wv[:, k, 0:256], range(8), c[1], b.free)
                if t == 0:
                    yield
            done(c, tk)
            b.free = T["z", g] = act.seq(lambda e: e.activation(zs[:, i].rearrange("p t n -> p (t n)"), b.t[:, :],
                                                                ACT.Silu), tk, T.get(("gated", g - 2)))
            yield

        def mamba_scan(g):
            i = g % 2
            BT, CT = cs[:, i, 2, :], cs[:, i, 3, :]
            hs = slice(4 * g, 4 * g + 4)
            bx, bb = bank8(), bank8()
            pe.wait(T["cs", g], bx.free, bb.free)
            for t in range(2):
                for j in range(2):
                    tk = pe.op(lambda e: e.transpose(
                        bx.t[:, t * 256 + j * 128:t * 256 + j * 128 + 128], cs[:, i, j, t * 128:(t + 1) * 128], ident))
            pe.op(lambda e: e.transpose(bb.t[:, 0:128], BT[:, 0:128], ident))
            for t in range(2):
                tcb = pe.op(mm(bb.t[:, 128 + 128 * t:256 + 128 * t], BT[:, t * 128:(t + 1) * 128],
                               CT[:, t * 128:(t + 1) * 128], True, True))
            tB = act.seq(lambda e: e.copy(Bl, bb.t[:, 0:128]), tcb, T.get(("S", g - 1)))
            x4 = bx.t[:, :].rearrange("p (t h q) -> p t h q", t=2, h=4)
            dve.seq(lambda e: e.tensor_tensor(
                xdt.rearrange("p t (h q) -> p t h q", h=4), x4, bc(dt[:, :, hs], 3, 64), ALU.mult), tk)
            dve.seq(lambda e: e.tensor_tensor(
                xde.rearrange("p (h q) -> p h q", h=4), x4[:, 0], bc(dte[:, hs], 2, 64), ALU.mult))
            bx.free = txd = dve.seq(lambda e: e.tensor_tensor(
                xD.rearrange("p t (h q) -> p (t h) q", h=4).rearrange("p (t h) q -> p t h q", t=2), x4,
                bc(bc(R("ssm_d")[:, hs], 1, 2), 3, 64), ALU.mult))
            yield
            segs = []
            for t in range(2):
                b = bank8()
                pe.wait(b.free)
                pe.op(mm(b.t[:, :], identb, negU.rearrange("p a b -> p (a b)"), True, True))
                for hh in range(4):
                    tk = pe.op(mm(b.t[:, hh * 128:(hh + 1) * 128],
                                  dtA[:, t, 4 * g + hh:4 * g + hh + 1].broadcast_to([128, 128]),
                                  triu, False, True, skip=True))
                b.free = tk = dve.seq(lambda e: e.tensor_tensor(
                    dec[:, t], b.t[:, :].rearrange("p (h l) -> p h l", h=4), bc(acum[:, t, hs], 2, 128),
                    ALU.subtract), tk)
                segs.append(act.seq(lambda e: e.activation(dec[:, t], dec[:, t], ACT.Exp), tk))
            bs = bank8()
            T["S", g] = tk = pe.op(mm(bs.t[:, 0:256], Bl, xde, True, True), bs.free, tB, txd)
            bs.free = tS0 = act.seq(lambda e: e.copy(S0, bs.t[:, 0:256]), tk)
            for t in range(2):
                tdec = dve.seq(lambda e: e.tensor_tensor(
                    dec[:, t], dec[:, t], bc(bb.t[:, 128 + 128 * t:256 + 128 * t], 1, 4), ALU.mult), segs[t], tB)
            bb.free = tdec
            yield
            by, bo = bank8(), bank8()
            pe.wait(by.free, bo.free, tdec, txd)
            for t in range(2):
                for hh in range(4):
                    ty = pe.op(mm(by.t[:, t * 256 + hh * 64:t * 256 + hh * 64 + 64], dec[:, t, hh, :],
                                  xdt[:, t, hh * 64:(hh + 1) * 64], True, True))
            T["used", g] = to = pe.op(mm(bo.t[:, 0:256], CT[:, 128:256], S0, True, True), tS0)
            by.free = dve.seq(lambda e: e.tensor_tensor(yv, by.t[:, :].rearrange("p (t n) -> p t n", t=2),
                                                        xD, ALU.add), ty, T.get(("y", g - 1)))
            bo.free = dve.seq(lambda e: e.tensor_tensor(
                xde.rearrange("p (h q) -> p h q", h=4), bo.t[:, 0:256].rearrange("p (h q) -> p h q", h=4),
                bc(expa[:, 1, hs], 2, 64), ALU.mult), to)
            dve.seq(lambda e: e.tensor_tensor(yv[:, 1], yv[:, 1], xde, ALU.add))
            T["gated", g] = tk = dve.seq(lambda e: e.tensor_tensor(yv, yv, zs[:, i], ALU.mult), T["z", g])
            for t in range(2):
                tk = act.seq(lambda e: e.activation(xD[:, t], yv[:, t], ACT.Square, accum_out=ssq[:, t:t + 1]), tk)
            dve.seq(lambda e: e.tensor_scalar(rsg[:, 0:2], ssq[:, 0:2], 1.0 / 256, EPS1, ALU.mult, ALU.add), tk)
            rsqrt(rsg[:, 0:2])
            for t in range(2):
                tk = dve.seq(lambda e: e.tensor_scalar(yv[:, t], yv[:, t], rsg[:, t:t + 1], None, ALU.mult))
            yield
            b = bank8()
            pe.wait(b.free, tk)
            for j in range(2):
                for t in range(2):
                    tk = pe.op(lambda e: e.transpose(
                        b.t[:, j * 256 + t * 128:j * 256 + t * 128 + 128], yv[:, t, j * 128:(j + 1) * 128], ident))
            T["y", g] = tk
            for j in range(2):
                ev = act.seq(lambda e: e.activation(
                    ygT[:, 2 * g + j, :], b.t[:, j * 256:(j + 1) * 256], ACT.Copy, scale=C("norm_w", 2 * g + j)), tk)
            b.free = T["ygT"] = ev
            yield

        run(mamba_in(0))
        for g in range(7):
            weave((mamba_scan(g), 1), (mamba_in(g + 1), 2))
        acc = [[bank8(), bank8()] for _ in range(2)]
        weave((mamba_scan(7), 1), (out_proj(w_out, ygT, lambda: T["ygT"], acc, (0,)), 1))
        run(out_proj(w_out, ygT, lambda: T["ygT"], acc, (8,)))
        add_residual(acc, pe.now())
        th, tx = layer_norm(tln)
        th, tx = moe(0, tx, th)

        barrier()
        tln = load_ln(2)
        m = Arena(small, 704)
        cosT, sinT, ang, a2 = m(2, 8), m(2, 8), m(2, 8), m(2, 8)
        pf, lp, lam, mxs, sums, rcp, ss4, rs4 = m(2), m(2), m(4), m(2), m(2), m(2), m(4), m(4)
        m = Arena(work, 7680)
        qs, ks_, vs = m(2, 512), m(2, 512), m(2, 512)
        ta, tb_ = m(2, 64), m(2, 64)
        tc2, td2 = m(2, 64), m(2, 64)
        sc, at, aT, osb = m(2, 256), m(256), m(2, 128), m(2, 512)
        qT, kT = area(big, 0, (4, 256)), area(big, 1024, (4, 256))
        oT = area(big, 2048, (8, 256))
        dve.seq(lambda e: e.tensor_copy(pf, posi[:, :]))
        dve.seq(lambda e: e.tensor_tensor(ang, bc(pf, 2, 8), bc(R("inv"), 1, 2), ALU.mult))
        TP = 2 * math.pi
        C1 = float(np.float32(6.28125))
        C2 = float(np.float32(np.float32(TP - C1).view(np.uint32) & np.uint32(0xFFFFF000)).view(np.float32)) if False else \
            float((np.array([TP - C1], np.float32).view(np.uint32) & np.uint32(0xFFFFF000)).view(np.float32)[0])
        C3 = float(np.float32(TP - C1 - C2))
        MG = 12582912.0

        def wrap(x):
            dve.seq(lambda e: e.tensor_scalar(a2, x, 1.0 / TP, None, ALU.mult))
            dve.seq(lambda e: e.tensor_scalar(a2, a2, MG, None, ALU.add))
            dve.seq(lambda e: e.tensor_scalar(a2, a2, MG, None, ALU.subtract))
            for cc in (C1, C2, C3):
                dve.seq(lambda e, cc=cc: e.scalar_tensor_tensor(out=x, in0=a2, scalar=-cc, in1=x,
                                                                op0=ALU.mult, op1=ALU.add))
            PI = float(np.nextafter(np.float32(math.pi), np.float32(0)))
            return dve.seq(lambda e: e.tensor_scalar(x, x, PI, -PI, ALU.min, ALU.max))

        tk = wrap(ang)
        tk = act.seq(lambda e: e.activation(sinT, ang, ACT.Sin), tk)
        dve.seq(lambda e: e.tensor_scalar(ang, ang, math.pi / 2, None, ALU.add), tk)
        tk = wrap(ang)
        trope = act.seq(lambda e: e.activation(cosT, ang, ACT.Sin), tk)
        dve.seq(lambda e: e.tensor_tensor(lp[:, 0:1], C("lamv", 0), C("lamv", 1), ALU.mult))
        tk = dve.seq(lambda e: e.tensor_tensor(lp[:, 1:2], C("lamv", 2), C("lamv", 3), ALU.mult))
        b = bank8()
        tk = pe.op(mm(b.t[:, 0:2], ones[:, :], lp, True, True), b.free, tk)
        b.free = tk = act.seq(lambda e, b=b: e.activation(lam[:, 0:2], b.t[:, 0:2], ACT.Exp), tk)
        dve.seq(lambda e: e.tensor_tensor(lam[:, 2:3], lam[:, 1:2], lam[:, 0:1], ALU.subtract), tk)
        tlam = dve.seq(lambda e: e.tensor_scalar(lam[:, 2:3], lam[:, 2:3], LI, None, ALU.subtract))
        w = A["attn_w_qkv"]
        scale1 = 64 ** -0.5
        for hg in range(2):
            for which, (dst, dT) in enumerate(((qs, qT), (ks_, kT), (vs, None))):
                c = chunk((kview(8, 512), src(w, 0, 1024, which * 1024 + hg * 512, which * 1024 + hg * 512 + 512)))
                wv = kview(8, 512)(c[0])
                for t in range(2):
                    b = bank8()
                    tk = project(b.t[:, :], lambda k: xT[:, k, t * 128:(t + 1) * 128], lambda k: wv[:, k, :],
                                 range(8), c[1], tx, b.free)
                    b.free = te = act.seq(lambda e, b=b, dst=dst, t=t: e.copy(dst[:, t, :], b.t[:, :]), tk, dve.now())
                done(c, tk)
                tv = te
                if dT is None:
                    continue
                v4 = dst.rearrange("p t (c d) -> p t c d", c=8)
                r1, r2 = v4[:, :, :, 0:8], v4[:, :, :, 8:16]
                cb_, sb_ = bc(cosT, 2, 8), bc(sinT, 2, 8)
                u = [x.rearrange("p t (c d) -> p t c d", c=8) for x in (ta, tb_, tc2, td2)]
                dve.seq(lambda e: e.tensor_tensor(u[0], r1, cb_, ALU.mult), te, trope)
                dve.seq(lambda e: e.tensor_tensor(u[1], r2, sb_, ALU.mult))
                dve.seq(lambda e: e.tensor_tensor(u[2], r2, cb_, ALU.mult))
                dve.seq(lambda e: e.tensor_tensor(u[3], r1, sb_, ALU.mult))
                dve.seq(lambda e: e.tensor_tensor(r1, u[0], u[1], ALU.subtract))
                tr = dve.seq(lambda e: e.tensor_tensor(r2, u[2], u[3], ALU.add))
                for hp in range(2):
                    b = bank8()
                    pe.wait(tr, b.free)
                    for j in range(2):
                        for t in range(2):
                            s = dst[:, t, (2 * hp + j) * 128:(2 * hp + j + 1) * 128]
                            tk = pe.op(lambda e, b=b, s=s, j=j, t=t: e.transpose(
                                b.t[:, j * 256 + t * 128:j * 256 + t * 128 + 128], s, ident))
                    b.free = tT = act.seq(lambda e, b=b, dT=dT, hp=hp: e.copy(
                        dT[:, 2 * hp:2 * hp + 2, :], b.t[:, :].rearrange("p (j t) -> p j t", j=2)), tk)
            for i in range(2):
                kv = 128 * (i + 1)
                bo = bank8()
                for hh in range(4):
                    for cc in range(2):
                        b = bank8()
                        pr = slice(64 * cc, 64 * cc + 64)
                        pe.op(mm(b.t[:, 0:kv], qT[pr, hh, i * 128:(i + 1) * 128], kT[pr, hh, 0:kv], True, False),
                              b.free, tT)
                        tk = pe.op(mm(b.t[:, 0:kv], identb, cB[:, 6 - i:7, :].rearrange("p a b -> p (a b)"),
                                      False, True))
                        dve.seq(lambda e: e.tensor_reduce(mxs[:, cc:cc + 1], b.t[:, 0:kv], AXX, ALU.max), tk)
                        tk = dve.seq(lambda e: e.tensor_scalar(mxs[:, cc:cc + 1], mxs[:, cc:cc + 1], -scale1, None,
                                                               ALU.mult))
                        b.free = tk = act.seq(lambda e: e.activation(
                            sc[:, cc, 0:kv], b.t[:, 0:kv], ACT.Exp, bias=mxs[:, cc:cc + 1], scale=scale1,
                            accum_out=sums[:, cc:cc + 1]), tk)
                    dve.seq(lambda e: e.reciprocal(rcp, sums), tk)
                    dve.seq(lambda e: e.tensor_tensor(rcp[:, 1:2], rcp[:, 1:2], lam[:, 2:3], ALU.mult))
                    dve.seq(lambda e, kv=kv: e.tensor_scalar(at[:, 0:kv], sc[:, 0, 0:kv], rcp[:, 0:1], None, ALU.mult))
                    tk = dve.seq(lambda e, kv=kv: e.scalar_tensor_tensor(
                        out=at[:, 0:kv], in0=sc[:, 1, 0:kv], scalar=rcp[:, 1:2], in1=at[:, 0:kv],
                        op0=ALU.mult, op1=ALU.add))
                    b = bank8()
                    pe.wait(b.free, tk)
                    for kt in range(i + 1):
                        tk = pe.op(lambda e, b=b, kt=kt: e.transpose(b.t[:, kt * 128:(kt + 1) * 128],
                                                                     at[:, kt * 128:(kt + 1) * 128], ident))
                    b.free = tk = act.seq(lambda e, b=b, i=i: e.copy(
                        aT[:, 0:i + 1, :], b.t[:, 0:kv].rearrange("p (a b) -> p a b", a=i + 1)), tk, pe.now())
                    pe.wait(tk, tv, bo.free if hh == 0 else None)
                    for kt in range(i + 1):
                        tko = pe.op(mm(bo.t[:, hh * 128:(hh + 1) * 128], aT[:, kt, :], vs[:, kt, hh * 128:(hh + 1) * 128],
                                       kt == 0, kt == i))
                o4 = bo.t[:, :].rearrange("p (h e) -> p h e", h=4)
                tk = act.seq(lambda e, i=i, bo=bo: e.activation(osb[:, i], bo.t[:, :], ACT.Square), tko, pe.now())
                dve.seq(lambda e, i=i: e.tensor_reduce(ss4, osb[:, i].rearrange("p (h e) -> p h e", h=4), AXX, ALU.add), tk)
                dve.seq(lambda e: e.tensor_scalar(rs4, ss4, 1.0 / 128, EPS1, ALU.mult, ALU.add))
                rsqrt(rs4)
                dve.seq(lambda e: e.tensor_scalar(rs4, rs4, 1.0 - LI, None, ALU.mult))
                bo.free = tk = dve.seq(lambda e, i=i, o4=o4: e.tensor_tensor(
                    osb[:, i].rearrange("p (h e) -> p h e", h=4), o4, bc(rs4, 2, 128), ALU.mult))
                b = bank8()
                pe.wait(b.free, tk)
                for hh in range(4):
                    tk = pe.op(lambda e, b=b, hh=hh, i=i: e.transpose(b.t[:, hh * 128:(hh + 1) * 128],
                                                                      osb[:, i, hh * 128:(hh + 1) * 128], ident))
                b.free = toT = act.seq(lambda e, b=b, hg=hg, i=i: e.activation(
                    oT[:, 4 * hg:4 * hg + 4, i * 128:(i + 1) * 128], b.t[:, :].rearrange("p (h t) -> p h t", h=4),
                    ACT.Copy, scale=C("subln")), tk)
        acc = [[bank8(), bank8()] for _ in range(2)]
        run(out_proj(A["attn_w_o"], oT, lambda: toT, acc, (0,)))
        add_residual(acc, pe.now())
        th, tx = layer_norm(tln)
        th, tx = moe(1, tx, th)

        barrier()
        tmeta = sp.dma(lambda e: e.dma_start(h[0:16, 2, :], A["meta"]), d2)
        m = Arena(small, 704)
        ssq, rs = m(4), m(4)
        s2, mxn, sm, esk = m(3, 2), m(3), m(3), m(3)

        def rms_T(tok, gname, cols):
            zt = area(work, 0, (1024,))
            ev = None
            for t in (0, 1, 2):
                act.seq(lambda e, t=t: e.activation(zt, h[:, t, :], ACT.Square, accum_out=ssq[:, t:t + 1]),
                        tok, pe.now(), dve.now())
                tk = act.now()
                dve.seq(lambda e, t=t: e.tensor_scalar(rs[:, t:t + 1], ssq[:, t:t + 1], 1.0 / 1024, EPS2, ALU.mult, ALU.add), tk)
                rsqrt(rs[:, t:t + 1])
                tk = dve.seq(lambda e, t=t: e.tensor_scalar(zt, h[:, t, :], rs[:, t:t + 1], None, ALU.mult))
                c0, nt = cols[t]
                for k in range(0, 8, 4):
                    b = bank8()
                    pe.wait(tk, b.free)
                    for kk in range(4):
                        tp = pe.op(lambda e, b=b, kk=kk, k=k, nt=nt: e.transpose(
                            b.t[:, kk * 128:kk * 128 + nt], zt[0:nt, (k + kk) * 128:(k + kk + 1) * 128],
                            ident[0:nt, 0:nt]))
                    for kk in range(4):
                        b.free = ev = act.seq(lambda e, b=b, kk=kk, k=k, nt=nt, c0=c0: e.activation(
                            xT[:, k + kk, c0:c0 + nt], b.t[:, kk * 128:kk * 128 + nt], ACT.Copy,
                            scale=C(gname, k + kk)), tp)
            return ev

        tx = rms_T([th, tmeta], "ng0", [(0, 128), (128, 128), (256, 128)])
        barrier()
        w = A["even_w_in"]
        m = Arena(work, 7680)
        kp = m(3, 64)
        cqT, ckT = m(3, 384), m(2, 384)
        base = m.at
        lat = m(3, 704)
        yT = area(big, 0, (16, 272))
        rt = lnb[:, :, :].rearrange("p a b -> p (a b)")
        trt = sp.dma(lambda e: e.dma_start(rt[:, 0:576], A["rope"]), d2, everyone())
        cM, sM = area(rt, 0, (3, 32)), area(rt, 96, (3, 32))
        cS, sS = area(rt, 192, (3, 64)), area(rt, 384, (3, 64))

        def rows_proj(wv, ncols, tw, evac, *after):
            for t in range(3):
                b = bank8()
                tk = project(b.t[:, 0:ncols], lambda k: xT[:, k, t * 128:(t + 1) * 128], lambda k: wv(k), range(8),
                             tw, b.free, *after)
                b.free = te = evac(t, b, tk)
            return tk, te

        c0 = chunk((kview(8, 512), src(w, 0, 1024, 0, 512)))
        c1 = chunk((kview(8, 192), src(w, 0, 1024, 512, 704)))
        v0, v1 = kview(8, 512)(c0[0]), kview(8, 192)(c1[0])
        tk, te = rows_proj(lambda k: v0[:, k, :], 512, c0[1],
                           lambda t, b, tk: act.seq(lambda e: e.copy(lat[:, t, 0:512], b.t[:, 0:512]), tk), tx)
        done(c0, tk)
        tk, te = rows_proj(lambda k: v1[:, k, :], 192, c1[1],
                           lambda t, b, tk: act.seq(lambda e: e.copy(lat[:, t, 512:704], b.t[:, 0:192]), tk))
        done(c1, tk)
        copy(dve, kp, lat[:, :, 640:704], te)
        junk = area(work, base + 2112, (384,))
        for (a0, n, gname, dT) in ((0, 384, "gq", cqT), (384, 256, "gkv", ckT)):
            for t in range(3):
                tk = act.seq(lambda e, t=t, a0=a0, n=n: e.activation(junk[:, 0:n], lat[:, t, a0:a0 + n], ACT.Square,
                                                                    accum_out=ssq[:, t:t + 1]), dve.now())
            dve.seq(lambda e, n=n: e.tensor_scalar(rs[:, 0:3], ssq[:, 0:3], 1.0 / n, EPS2, ALU.mult, ALU.add), tk)
            rsqrt(rs[:, 0:3])
            tk = dve.seq(lambda e, a0=a0, n=n: e.tensor_tensor(lat[:, :, a0:a0 + n], lat[:, :, a0:a0 + n],
                                                             bc(rs[:, 0:3], 2, n), ALU.mult))
            for j in range(n // 128):
                b = bank8()
                pe.wait(tk, b.free)
                for t in range(3):
                    tp = pe.op(lambda e, b=b, t=t, j=j, a0=a0: e.transpose(
                        b.t[:, t * 128:(t + 1) * 128], lat[:, t, a0 + j * 128:a0 + (j + 1) * 128], ident))
                b.free = tlat = act.seq(lambda e, b=b, j=j, dT=dT, gname=gname: e.activation(
                    dT[:, j, :], b.t[:, 0:384], ACT.Copy, scale=C(gname, j)), tp)
        barrier()
        m = Arena(work, 7680)
        m.at = base
        ub = [m(3, 2, 192)]
        vb = m(3, 2, 128)
        uq = m(3, 2, 64)
        QN, KN = m(2, 272), m(2, 272)
        QR, KR = m(2, 272), m(2, 272)
        pt = area(rt, 576, (3, 272))
        pe_ = area(small, 64, (272,))
        es = area(small, 336, (272,))
        U = ub[0]

        def norm_rope(D, grow, ro, half, ct, st_, ev, gr_bc=True):
            sq = area(rt, 576, (3, 2, 192))
            tk = act.seq(lambda e: e.activation(sq[:, :, :, 0:D], U[:, :, :, 0:D], ACT.Square), ev, pe.now(), dve.now())
            dve.seq(lambda e: e.tensor_reduce(s2, sq[:, :, :, 0:D], AXX, ALU.add), tk)
            dve.seq(lambda e: e.tensor_scalar(s2, s2, 1.0 / D, EPS2, ALU.mult, ALU.add))
            rsqrt(s2)
            dve.seq(lambda e: e.tensor_tensor(U[:, :, :, 0:D], U[:, :, :, 0:D], bc(s2, 3, D), ALU.mult))
            dve.seq(lambda e: e.tensor_tensor(U[:, :, :, 0:D], U[:, :, :, 0:D], bc(bc(grow, 1, 2), 1, 3), ALU.mult))
            x1, x2 = U[:, :, :, ro:ro + half], U[:, :, :, ro + half:ro + 2 * half]
            c_, s_ = bc(ct, 2, 2), bc(st_, 2, 2)
            a, b2, c2, d2_ = (area(rt, 576 + i * 384, (3, 2, half)) for i in range(3 + 0)) if False else \
                (area(rt, 576, (3, 2, half)), area(rt, 576 + 384, (3, 2, half)), area(rt, 576 + 768, (3, 2, half)),
                 uq[:, :, :, 0:half])
            dve.seq(lambda e: e.tensor_tensor(a, x1, c_, ALU.mult), trt)
            dve.seq(lambda e: e.tensor_tensor(b2, x2, s_, ALU.mult))
            dve.seq(lambda e: e.tensor_tensor(c2, x1, s_, ALU.mult))
            dve.seq(lambda e: e.tensor_tensor(d2_, x2, c_, ALU.mult))
            dve.seq(lambda e: e.tensor_tensor(x1, a, b2, ALU.subtract))
            return dve.seq(lambda e: e.tensor_tensor(x2, c2, d2_, ALU.add))

        def turn_unit(tok, dN, dR):
            for j in range(2):
                b = bank8()
                pe.wait(tok, b.free)
                for t in range(3):
                    nt = 16 if t == 2 else 128
                    tp = pe.op(lambda e, b=b, t=t, j=j, nt=nt: e.transpose(
                        b.t[:, t * 128:t * 128 + nt], U[0:nt, t, j, 0:128], ident[0:nt, 0:nt]))
                b.free = ev = act.seq(lambda e, b=b, j=j: e.copy(dN[:, j, :], b.t[:, 0:272]), tp)
                if dR is not None:
                    b = bank8()
                    pe.wait(b.free)
                    for t in range(3):
                        nt = 16 if t == 2 else 128
                        tp = pe.op(lambda e, b=b, t=t, j=j, nt=nt: e.transpose(
                            b.t[0:64, t * 128:t * 128 + nt], U[0:nt, t, j, 128:192], ident[0:nt, 0:nt]))
                    b.free = ev = act.seq(lambda e, b=b, j=j: e.copy(dR[0:64, j, :], b.t[0:64, 0:272]), tp)
            return ev

        def attend(hd, qn, kn, qr, kr, V, scale, masked, *after):
            bt = [bank8(), bank8(), bank8()]
            for i in range(3):
                nq = 16 if i == 2 else 128
                q0 = 128 * i
                b = bank8()
                pe.wait(b.free, *after)
                tk = pe.op(mm(b.t[0:nq, 0:272], qn[:, q0:q0 + nq], kn, True, qr is None and not masked))
                if qr is not None:
                    tk = pe.op(mm(b.t[0:nq, 0:272], qr[0:64, q0:q0 + nq], kr[0:64, :], False, True))
                if masked:
                    tk = pe.op(mm(b.t[0:nq, 0:272], identb[:, 0:nq], swm[:, i, :], False, True))
                mx_, sm_, ek = mxn[0:nq, i:i + 1], sm[0:nq, i:i + 1], esk[0:nq, i:i + 1]
                dve.seq(lambda e, b=b, nq=nq, mx_=mx_: e.tensor_reduce(mx_, b.t[0:nq, 0:272], AXX, ALU.max), tk)
                if masked:
                    snk = R("sink")[0:nq, hd - 8:hd - 7]
                    dve.seq(lambda e, mx_=mx_: e.tensor_scalar(mx_, mx_, scale, None, ALU.mult))
                    dve.seq(lambda e, mx_=mx_, snk=snk: e.tensor_tensor(mx_, mx_, snk, ALU.max))
                    tk = dve.seq(lambda e, mx_=mx_: e.tensor_scalar(mx_, mx_, -1.0, None, ALU.mult))
                    tk2 = act.seq(lambda e, ek=ek, snk=snk, mx_=mx_: e.activation(ek, snk, ACT.Exp, bias=mx_), tk)
                else:
                    tk = dve.seq(lambda e, mx_=mx_: e.tensor_scalar(mx_, mx_, -scale, None, ALU.mult))
                b.free = tk = act.seq(lambda e, b=b, nq=nq, mx_=mx_, sm_=sm_: e.activation(
                    es[0:nq, :], b.t[0:nq, 0:272], ACT.Exp, bias=mx_, scale=scale, accum_out=sm_), tk)
                if masked:
                    dve.seq(lambda e, sm_=sm_, ek=ek: e.tensor_tensor(sm_, sm_, ek, ALU.add), tk)
                dve.seq(lambda e, sm_=sm_: e.reciprocal(sm_, sm_), tk)
                tk = dve.seq(lambda e, nq=nq, sm_=sm_: e.tensor_scalar(pe_[0:nq, :], es[0:nq, :], sm_, None, ALU.mult),
                             pe.now())
                for kt in range(3):
                    nk = 16 if kt == 2 else 128
                    pe.wait(tk, bt[kt].free if i == 0 else None)
                    tp = pe.op(lambda e, kt=kt, nk=nk, q0=q0, nq=nq: e.transpose(
                        bt[kt].t[0:nk, q0:q0 + nq], pe_[0:nq, kt * 128:kt * 128 + nk], ident[0:nq, 0:nq]))
            for kt in range(3):
                nk = 16 if kt == 2 else 128
                bt[kt].free = tk = copy(dve if kt == 1 else act, pt[0:nk, kt, :], bt[kt].t[0:nk, 0:272], tp)
                pe.wait(tk)
            b = bank8()
            pe.wait(b.free)
            for kt in range(3):
                nk = 16 if kt == 2 else 128
                tk = pe.op(mm(b.t[:, 0:272], V(kt)[0:nk, :], pt[0:nk, kt, :], kt == 0, kt == 2))
            b.free = tk = act.seq(lambda e, b=b: e.copy(yT[:, hd, :], b.t[:, 0:272]), tk)
            return tk

        ckv = chunk((kview(2, 2048), src(A["w_ukv"], 0, 256, 0, 2048)))
        wkv = kview(2, 2048)(ckv[0])
        for u in range(4):
            if u % 2 == 0:
                cq = chunk((kview(3, 768), src(A["w_uq"], 0, 384, 384 * u, 384 * u + 768)))
                wq = kview(3, 768)(cq[0])
            for t in range(3):
                b = bank8()
                tk = project(b.t[:, 0:384], lambda k: cqT[:, k, t * 128:(t + 1) * 128],
                             lambda k: wq[:, k, (u % 2) * 384:(u % 2) * 384 + 384], range(3), cq[1], tlat, b.free)
                b.free = te = act.seq(lambda e, b=b, t=t: e.copy(
                    U[:, t, :, :], b.t[:, 0:384].rearrange("p (j d) -> p j d", j=2)), tk, dve.now())
            if u % 2 == 1:
                done(cq, tk)
            tn = norm_rope(192, R("mgq"), 128, 32, cM, sM, te)
            tq = turn_unit(tn, QN, QR)
            for t in range(3):
                b = bank8()
                tk = project(b.t[:, :], lambda k: ckT[:, k, t * 128:(t + 1) * 128],
                             lambda k: wkv[:, k, u * 512:(u + 1) * 512], range(2), ckv[1], b.free)
                kv4 = b.t[:, :].rearrange("p (j d) -> p j d", j=2)
                act.seq(lambda e, kv4=kv4, t=t: e.copy(U[:, t, :, 0:128], kv4[:, :, 0:128]), tk, tq)
                b.free = te = act.seq(lambda e, kv4=kv4, t=t: e.copy(vb[:, t, :, :], kv4[:, :, 128:256]))
            te = dve.seq(lambda e: e.tensor_copy(U[:, :, :, 128:192], bc(kp, 2, 2)), tq, pe.now())
            if u == 3:
                done(ckv, tk)
            tn = norm_rope(192, R("mgk"), 128, 32, cM, sM, [te, act.now()])
            tk_ = turn_unit(tn, KN, KR)
            for j in range(2):
                ta_ = attend(2 * u + j, QN[:, j, :], KN[:, j, :], QR[:, j, :], KR[:, j, :],
                             lambda kt, j=j: vb[:, kt, j, :], 192 ** -0.5, False, tq, tk_)
        barrier()
        c = chunk((kview(8, 512), src(w, 0, 1024, 1728, 2240)))
        wv = kview(8, 512)(c[0])

        def ev_kv(t, b, tk):
            act.seq(lambda e: e.copy(U[:, t, :, 0:128], b.t[:, 0:256].rearrange("p (j d) -> p j d", j=2)), tk)
            return act.seq(lambda e: e.copy(vb[:, t, :, :], b.t[:, 256:512].rearrange("p (j d) -> p j d", j=2)))

        tk, te = rows_proj(lambda k: wv[:, k, :], 512, c[1], ev_kv)
        done(c, tk)
        tn = norm_rope(128, R("sgk"), 0, 64, cS, sS, te)
        tk_ = turn_unit(tn, KN, None)
        for u in range(4):
            if u % 2 == 0:
                c = chunk((kview(8, 512), src(w, 0, 1024, 704 + 256 * u, 704 + 256 * u + 512)))
                wv = kview(8, 512)(c[0])
            o = (u % 2) * 256
            tk, te = rows_proj(lambda k: wv[:, k, o:o + 256], 256, c[1],
                               lambda t, b, tk: act.seq(lambda e: e.copy(
                                   U[:, t, :, 0:128], b.t[:, 0:256].rearrange("p (j d) -> p j d", j=2)), tk, dve.now(), pe.now()))
            if u % 2 == 1:
                done(c, tk)
            tn = norm_rope(128, R("sgq"), 0, 64, cS, sS, te)
            tq = turn_unit(tn, QN, None)
            for j in range(2):
                hd = 2 * u + j
                gk = hd // 4
                ta_ = attend(8 + hd, QN[:, j, :], KN[:, gk, :], None, None,
                             lambda kt, gk=gk: vb[:, kt, gk, :], 128 ** -0.5, True, tq, tk_)
        barrier()
        sgt = area(work, base, (2, 272))
        for cb in range(4):
            c = chunk((kview(8, 512), src(w, 0, 1024, 2240 + 512 * cb, 2240 + 512 * cb + 512)))
            wv = kview(8, 512)(c[0])
            for j in range(4):
                n = 4 * cb + j
                b = bank8()
                tk = project(b.t[:, 0:272], lambda k: wv[:, k, j * 128:(j + 1) * 128], lambda k: xT[:, k, 0:272],
                             range(8), c[1], b.free)
                b.free = tg = act.seq(lambda e, b=b, n=n: e.activation(sgt[:, n % 2, :], b.t[:, 0:272], ACT.Silu),
                                      tk, dve.now())
                ty = dve.seq(lambda e, n=n: e.tensor_tensor(yT[:, n, :], yT[:, n, :], sgt[:, n % 2, :], ALU.mult), tg)
            done(c, tk)
        for n in range(2):
            acc = [bank8() for _ in range(3)]
            for k0 in (0, 8):
                c = chunk((kview(8, 512), src(A["even_w_out"], k0 * 128, k0 * 128 + 1024, n * 512, n * 512 + 512)))
                wv = kview(8, 512)(c[0])
                for t in range(3):
                    nt = 16 if t == 2 else 128
                    tk = project(acc[t].t[0:nt, :], lambda k: yT[:, k, t * 128:t * 128 + nt],
                                 lambda k: wv[:, k - k0, :], range(k0, k0 + 8), c[1], ty,
                                 acc[t].free if k0 == 0 else None, start=k0 == 0, stop=k0 == 8)
                done(c, tk)
            for t in range(3):
                nt = 16 if t == 2 else 128
                hh = h[0:nt, t, n * 512:(n + 1) * 512]
                acc[t].free = th = dve.seq(lambda e, hh=hh, t=t, nt=nt, acc=acc: e.tensor_tensor(
                    hh, hh, acc[t].t[0:nt, :], ALU.add), tk)

        barrier()
        tx = rms_T(th, "ng1", [(16, 128), (144, 128), (0, 16)])
        barrier()
        w = A["odd_w_in"]
        m = Arena(small, 704)
        spl = m(32)
        sp2 = m(32)
        sp3 = m(32)
        L = C("lam", 0, 32)
        tk = dve.seq(lambda e: e.scalar_tensor_tensor(out=spl, in0=L, scalar=-1.0, in1=L, op0=ALU.mult, op1=ALU.max))
        tk = act.seq(lambda e: e.activation(spl, spl, ACT.Exp, scale=-1.0), tk)
        tk = act.seq(lambda e: e.activation(sp2, spl, ACT.Ln, bias=1.0), tk)
        dve.seq(lambda e: e.tensor_scalar(sp3, L, -1.0, 0.0, ALU.mult, ALU.max))
        dve.seq(lambda e: e.tensor_tensor(sp2, sp2, sp3, ALU.add), tk)
        dve.seq(lambda e: e.tensor_scalar(spl, sp2, 8.0, None, ALU.mult))
        tspl = dve.seq(lambda e: e.tensor_scalar(sp3, sp2, -8.0, None, ALU.mult))
        m = Arena(work, 7680)
        xc = m(2, 272)
        sgt = m(2, 272)
        rr = m(2, 2, 272)
        ii = m(2, 2, 272)
        aa = m(2, 2, 272)
        tt = m(2, 2, 272)
        tu = m(2, 2, 272)
        hf = m(2, 2, 272)
        for cb in range(8):
            c = chunk((kview(8, 512, n0=0, w=256), src(w, 0, 1024, 256 * cb, 256 * cb + 256)),
                      (kview(8, 512, n0=256, w=256), src(w, 0, 1024, 2048 + 256 * cb, 2048 + 256 * cb + 256)))
            wv = kview(8, 512)(c[0])
            if cb % 4 == 0:
                g0 = 2 * cb
                pieces = []
                for ki, wn in enumerate(("lru_w_a", "lru_w_x")):
                    for r in range(2):
                        at0 = (ki * 2 + r) * 1024
                        pieces.append((lambda v, at0=at0: v[:, at0:at0 + 1024].rearrange("p (n e) -> p n e", n=8),
                                       A[wn][r, g0:g0 + 8].rearrange("n d e -> d n e")))
                cl = chunk(*pieces)
                wl = cl[0].rearrange("p (a r n e) -> p a r n e", a=2, r=2, n=8)
            for j in range(2):
                n = 2 * cb + j
                b = bank8()
                tk = project(b.t[:, 0:272], lambda k: wv[:, k, j * 128:(j + 1) * 128], lambda k: xT[:, k, 0:272],
                             range(8), c[1], tx, b.free)
                ps = b.t[:, 0:272]
                o = xc[:, j, :]
                dve.seq(lambda e, ps=ps, o=o, n=n: e.tensor_scalar(o, ps, C("lconv_w", 4 * n + 2), C("lconv_b", n),
                                                                   ALU.mult, ALU.add), tk, pe.now())
                for tap, (d0, d1, s0, s1) in ((0, (2, 272, 0, 270)), (1, (1, 272, 0, 271)), (3, (0, 271, 1, 272))):
                    b.free = txc = dve.seq(lambda e, ps=ps, o=o, n=n, tap=tap, d0=d0, d1=d1, s0=s0, s1=s1:
                                           e.scalar_tensor_tensor(out=o[:, d0:d1], in0=ps[:, s0:s1],
                                                                  scalar=C("lconv_w", 4 * n + tap), in1=o[:, d0:d1],
                                                                  op0=ALU.mult, op1=ALU.add))
                b = bank8()
                tk = project(b.t[:, 0:272], lambda k: wv[:, k, 256 + j * 128:256 + (j + 1) * 128],
                             lambda k: xT[:, k, 0:272], range(8), c[1], b.free)
                b.free = tsg = act.seq(lambda e, b=b, j=j: e.activation(sgt[:, j, :], b.t[:, 0:272], ACT.Silu),
                                       tk, dve.now())
            done(c, tk)
            for j in range(2):
                n = 2 * cb + j
                for ki, (dst, bias) in enumerate(((rr, "ba"), (ii, "bx"))):
                    for r in range(2):
                        b = bank8()
                        tk = pe.op(mm(b.t[:, 0:272], wl[:, ki, r, n % 8, :], xc[:, j, :], True, True),
                                   txc, cl[1], b.free)
                        b.free = tri = act.seq(lambda e, b=b, dst=dst, j=j, r=r, bias=bias, n=n: e.activation(
                            dst[:, j, r, :], b.t[:, 0:272], ACT.Sigmoid, bias=C(bias, 16 * r + n)), tk, dve.now())
            if cb % 4 == 3:
                done(cl, tk)
            for j in range(2):
                n = 2 * cb + j
                for r in range(2):
                    i_ = 16 * r + n
                    act.seq(lambda e, j=j, r=r, i_=i_: e.activation(aa[:, j, r, :], rr[:, j, r, :], ACT.Exp,
                                                                    scale=sp3[:, i_:i_ + 1]), tspl)
                    tta = act.seq(lambda e, j=j, r=r, i_=i_: e.activation(tt[:, j, r, :], rr[:, j, r, :], ACT.Tanh,
                                                                         scale=spl[:, i_:i_ + 1]))
            dve.seq(lambda e: e.tensor_scalar(tu, tt, 1.0, None, ALU.add), tta)
            dve.seq(lambda e: e.reciprocal(tu, tu))
            dve.seq(lambda e: e.scalar_tensor_tensor(out=tt.rearrange("p a b c -> p (a b c)"),
                                                     in0=tt.rearrange("p a b c -> p (a b c)"), scalar=2.0,
                                                     in1=tu.rearrange("p a b c -> p (a b c)"),
                                                     op0=ALU.mult, op1=ALU.mult))
            tk = act.seq(lambda e: e.activation(tt, tt, ACT.Sqrt), dve.now())
            dve.wait(tk)
            dve.seq(lambda e: e.tensor_tensor(tt, tt, ii, ALU.mult))
            dve.seq(lambda e: e.tensor_tensor(tt, tt, bc(xc, 2, 2), ALU.mult))
            for j in range(2):
                dve.seq(lambda e, j=j: e.tensor_tensor_scan(hf[:, j, 0, :], aa[:, j, 0, :], tt[:, j, 0, :], 0.0,
                                                            ALU.mult, ALU.add))
                dve.seq(lambda e, j=j: e.tensor_tensor_scan(hf[:, j, 1, ::-1], aa[:, j, 1, ::-1], tt[:, j, 1, ::-1],
                                                            0.0, ALU.mult, ALU.add))
                dve.seq(lambda e, j=j: e.tensor_tensor(hf[:, j, 0, :], hf[:, j, 0, :], hf[:, j, 1, :], ALU.add))
                ty = dve.seq(lambda e, j=j, cb=cb: e.tensor_tensor(yT[:, 2 * cb + j, :], hf[:, j, 0, :],
                                                                   sgt[:, j, :], ALU.mult), tsg)
        for n in range(2):
            acc = [bank8() for _ in range(2)]
            for k0 in (0, 8):
                c = chunk((kview(8, 512), src(A["odd_w_out"], k0 * 128, k0 * 128 + 1024, n * 512, n * 512 + 512)))
                wv = kview(8, 512)(c[0])
                for t in range(2):
                    tk = project(acc[t].t[:, :], lambda k: yT[:, k, 16 + t * 128:144 + t * 128],
                                 lambda k: wv[:, k - k0, :], range(k0, k0 + 8), c[1], ty,
                                 acc[t].free if k0 == 0 else None, start=k0 == 0, stop=k0 == 8)
                done(c, tk)
            for t in range(2):
                hh = h[:, t, n * 512:(n + 1) * 512]
                acc[t].free = th = dve.seq(lambda e, hh=hh, t=t, acc=acc: e.tensor_tensor(hh, hh, acc[t].t[:, :], ALU.add), tk)
        tout = sp.dma(lambda e: e.dma_start(out.rearrange("a (t p) d -> p (a t) d", p=128), h[:, 0:2, :]), out_sem, th)
        sp.wait(tout)

        block = ctx.enter_context(nc.Block())

        @block.sync
        def _(e):
            sp.play(e)

        @block.tensor
        def _(e):
            pe.play(e)

        @block.vector
        def _(e):
            dve.play(e)

        @block.scalar
        def _(e):
            act.play(e)

        @block.gpsimd
        def _(e):
            pool.play(e)


def host_layout(I):
    f = np.float32
    D = {}
    c = np.ascontiguousarray
    D["x"] = I["x"]
    p, q = np.arange(128)[:, None], np.arange(128)[None, :]
    D["cF"] = c(np.stack([(p == q), (p <= q), (p < q)], 1).astype(f))
    bits = lambda a: (np.ascontiguousarray(a, dtype=f).view(np.uint32) >> 16).astype(np.uint16)
    cb = np.zeros((128, 8, 128), f)
    cb[:, 0] = p == q
    cb[:, 1:5] = np.where(p > q, NEG, 0.0)[:, None]
    cb[:, 6] = np.where(q > p, NEG, 0.0)
    D["cB"] = bits(cb)
    pos = np.concatenate([np.arange(256) + 16, np.arange(16)])
    sw = np.zeros((128, 3, 272), f)
    for t in range(2):
        qi = 128 * t + np.arange(128)[:, None]
        kj = np.arange(256)[None, :]
        sw[:, t, :256] = np.where(np.abs(qi - kj) <= 128, 0.0, NEG)
    mi = np.arange(16)[:, None]
    kj = np.arange(256)[None, :]
    sw[:16, 2, :256] = np.where((kj < 128) & (16 + kj - mi <= 128), 0.0, NEG)
    D["swm"] = bits(sw)
    col = np.zeros((128, NCOL), f)

    def put(name, a):
        b, w = COLS[name]
        a = np.asarray(a).reshape(w, -1).T
        col[:a.shape[0], b:b + w] = a

    put("conv_w", I["ssm_conv_w"][0].reshape(4, 32, 128).transpose(1, 0, 2))
    put("conv_b", I["ssm_conv_b"][0])
    put("norm_w", I["ssm_norm_w"][0])
    put("subln", I["attn_subln_w"][0])
    put("ng0", I["norm_g_2"][0])
    put("ng1", I["norm_g_2"][1])
    put("gq", I["mla_g_q_lat_2"][0])
    put("gkv", I["mla_g_kv_lat_2"][0])
    put("lconv_w", I["lru_conv_w_2"][0].reshape(4, 16, 128).transpose(1, 0, 2))
    put("lconv_b", I["lru_conv_b_2"][0])
    put("ba", I["lru_b_a_2"][0])
    put("bx", I["lru_b_x_2"][0])
    put("lam", I["lru_lambda_2"][0])
    put("lamv", np.stack([I[n][0] for n in ("attn_lam_q1", "attn_lam_k1", "attn_lam_q2", "attn_lam_k2")]))
    D["col"] = col
    row = np.zeros((1, NROW), f)
    inv = np.power(f(500000.0), -np.arange(0, 16, 2, dtype=f) / f(16)).astype(f)
    for name, a in (("dt_bias", I["ssm_dt_bias"]), ("a_log", I["ssm_a_log"]), ("ssm_d", I["ssm_d"]),
                    ("mgq", I["mla_g_qn_2"]), ("mgk", I["mla_g_kn_2"]), ("sgq", I["swa_g_qn_2"]),
                    ("sgk", I["swa_g_kn_2"]), ("sink", I["swa_sink_2"]), ("inv", inv),
                    ("iota", np.arange(64, dtype=f))):
        b, w = ROWS[name]
        row[0, b:b + w] = np.asarray(a).reshape(-1)
    D["row"] = row
    D["pos"] = c(I["positions"].reshape(2, 128).T.astype(np.int32))
    D["lnp"] = c(np.stack([np.stack([I["ln_mix_g"][0], I["ln_mix_b"][0]]), np.stack([I["ln_ffn_g"][0], I["ln_ffn_b"][0]]),
                           np.stack([I["ln_mix_g"][1], I["ln_mix_b"][1]]), np.stack([I["ln_ffn_g"][1], I["ln_ffn_b"][1]])]))
    wr = np.concatenate([I["moe_w_group"], I["moe_w_expert"]], axis=2)
    D["wr"] = c(wr.reshape(2, 8, 128, 36).transpose(0, 2, 1, 3))
    D["ssm_w_in"], D["ssm_w_out"] = I["ssm_w_in"][0], I["ssm_w_out"][0]
    D["attn_w_qkv"], D["attn_w_o"] = I["attn_w_qkv"][0], I["attn_w_o"][0]
    D["wg"], D["wu"], D["wd"] = I["moe_w_gate"], I["moe_w_up"], I["moe_w_down"]
    D["meta"] = I["meta_tokens_2"]
    D["even_w_in"], D["even_w_out"] = I["even_w_in_2"][0], I["even_w_out_2"][0]
    D["w_uq"] = I["mla_w_uq_2"][0].reshape(384, 1536)
    D["w_ukv"] = I["mla_w_ukv_2"][0].reshape(256, 2048)
    D["odd_w_in"], D["odd_w_out"] = I["odd_w_in_2"][0], I["odd_w_out_2"][0]
    D["lru_w_a"], D["lru_w_x"] = I["lru_w_a_2"][0], I["lru_w_x_2"][0]

    def rope(dim):
        i = (f(10000.0) ** (-np.arange(0, dim, 2, dtype=f) / f(dim))).astype(f)
        a = np.zeros((384, dim // 2), f)
        a[:272] = pos.astype(f)[:, None] * i[None, :]
        r = lambda v: v.astype(f).reshape(3, 128, dim // 2).transpose(1, 0, 2).reshape(128, -1)
        return r(np.cos(a)), r(np.sin(a))

    D["rope"] = c(np.concatenate([*rope(64), *rope(128)], axis=1))
    return D


def kernel(**inputs):
    import concourse.bacc as _bacc
    from concourse import mybir as _mybir
    from concourse.bass_utils import run_bass_kernel_spmd as _run

    I = {k: np.asarray(v) for k, v in inputs.items()}
    D = host_layout(I)
    nc = _bacc.Bacc("TRN2", target_bir_lowering=False, num_devices=1)
    arrays, aps = {}, {}
    for name, a in D.items():
        a = np.ascontiguousarray(a)
        arrays[f"in_{name}"] = a
        aps[name] = nc.dram_tensor(f"in_{name}", a.shape, _mybir.dt.from_np(a.dtype), kind="ExternalInput").ap()
    out = nc.dram_tensor("out_0", (1, 256, 1024), _mybir.dt.float32, kind="ExternalOutput").ap()
    build(nc, aps, out)
    r = _run(nc, [arrays], core_ids=[0])
    return r.results[0]["out_0"]
```

```python
import math
from contextlib import ExitStack

import numpy as np
import concourse.bass as bass
from concourse import mybir

ALU = mybir.AluOpType
ACT = mybir.ActivationFunctionType
AXX = mybir.AxisListType.X
F32 = mybir.dt.float32
BF16 = mybir.dt.bfloat16
I32 = mybir.dt.int32
U32 = mybir.dt.uint32
U16 = mybir.dt.uint16

NSLOT = 7
CAP = 64
NE = 32
ALPHA = 4.0 ** 0.25
EPS1 = 1e-5
EPS2 = 1e-6
NEG = -1e30
LOW = -3.0e38
LI = 0.8 - 0.6 * math.exp(-0.3)

COLS = {}
_n = 0
for _name, _w in (("conv_w", 128), ("conv_b", 32), ("norm_w", 16), ("subln", 1), ("ng0", 8), ("ng1", 8),
                  ("gq", 3), ("gkv", 2), ("lconv_w", 64), ("lconv_b", 16), ("ba", 32), ("bx", 32),
                  ("lam", 32), ("lamv", 4)):
    COLS[_name] = (_n, _w)
    _n += _w
NCOL = _n
ROWS = {}
_n = 0
for _name, _w in (("dt_bias", 32), ("a_log", 32), ("ssm_d", 32), ("mgq", 192), ("mgk", 192),
                  ("sgq", 128), ("sgk", 128), ("sink", 8), ("inv", 8), ("iota", 64)):
    ROWS[_name] = (_n, _w)
    _n += _w
NROW = _n


class Later:

    def matmul(self, *a, **k):
        return lambda e: e.matmul(*a, **k)

    def transpose(self, *a, **k):
        return lambda e: e.transpose(*a, **k)

    def tensor_copy(self, *a, **k):
        return lambda e: e.tensor_copy(*a, **k)

    def memset(self, *a, **k):
        return lambda e: e.memset(*a, **k)

    def tensor_tensor(self, *a, **k):
        return lambda e: e.tensor_tensor(*a, **k)

    def tensor_scalar(self, *a, **k):
        return lambda e: e.tensor_scalar(*a, **k)

    def scalar_tensor_tensor(self, *a, **k):
        return lambda e: e.scalar_tensor_tensor(*a, **k)

    def tensor_reduce(self, *a, **k):
        return lambda e: e.tensor_reduce(*a, **k)

    def reciprocal(self, *a, **k):
        return lambda e: e.reciprocal(*a, **k)

    def bn_stats(self, *a, **k):
        return lambda e: e.bn_stats(*a, **k)

    def bn_aggr(self, *a, **k):
        return lambda e: e.bn_aggr(*a, **k)

    def max(self, *a, **k):
        return lambda e: e.max(*a, **k)

    def max_index(self, *a, **k):
        return lambda e: e.max_index(*a, **k)

    def tensor_tensor_scan(self, *a, **k):
        return lambda e: e.tensor_tensor_scan(*a, **k)

    def copy(self, *a, **k):
        return lambda e: e.copy(*a, **k)

    def activation(self, *a, **k):
        return lambda e: e.activation(*a, **k)

    def dma_start(self, *a, **k):
        return lambda e: e.dma_start(*a, **k)

    def wait_ge(self, *a, **k):
        return lambda e: e.wait_ge(*a, **k)


LATER = Later()


class Queue:

    def __init__(self, sem):
        self.sem, self.items, self.n, self.seen = sem, [], 0, {}

    def wait(self, *toks):
        for tok in toks:
            if tok is None:
                continue
            if isinstance(tok, list):
                self.wait(*tok)
                continue
            sem, val = tok
            if self.seen.get(sem.name, 0) < val:
                self.seen[sem.name] = val
                self.items.append(LATER.wait_ge(sem, val))

    def now(self):
        return (self.sem, self.n) if self.n else None

    def raw(self, fn, *after):
        self.wait(*after)
        self.items.append(fn(LATER))

    def op(self, fn, *after):
        self.wait(*after)
        self.n += 1
        go = fn(LATER)
        self.items.append(lambda e: go(e).then_inc(self.sem, 1))
        return (self.sem, self.n)

    def seq(self, fn, *after):
        return self.op(fn, self.now(), *after)

    def dma(self, fn, dsem, *after):
        self.wait(*after)
        dsem[1] += 16
        go, s = fn(LATER), dsem[0]
        self.items.append(lambda e: go(e).then_inc(s, 16))
        return (dsem[0], dsem[1])

    def play(self, e):
        for f in self.items:
            f(e)


class Bank:

    def __init__(self, t):
        self.t, self.tok, self.held = t, None, False

    @property
    def free(self):
        return self.tok

    @free.setter
    def free(self, tok):
        self.tok, self.held = tok, False


def weave(*gens):
    gens = [list(g) for g in gens]
    while gens:
        for g in list(gens):
            for _ in range(g[1]):
                try:
                    next(g[0])
                except StopIteration:
                    gens.remove(g)
                    break


def chain(*gens):
    for g in gens:
        yield from g


def run(gen):
    for _ in gen:
        pass


def bc(ap, axis, n):
    a = ap.unsqueeze(axis)
    s = list(a.shape)
    s[axis] = n
    return a.broadcast_to(s)


def build(nc, A, out):
    ctx = ExitStack()
    with ctx:
        def sb(name, shape, dt=F32):
            return ctx.enter_context(nc.sbuf_tensor(name, shape, dt))

        def sem(name):
            return ctx.enter_context(nc.semaphore(name))

        pe, dve, act, pool, sp = (Queue(sem("s_" + n)) for n in ("pe", "dve", "act", "pool", "sp"))
        banks = [Bank(ctx.enter_context(nc.psum_tensor(f"ps{i}", [128, 512], F32))) for i in range(8)]
        rot = [0, 0]

        def bank8():
            for _ in range(8):
                rot[0] += 1
                b = banks[rot[0] % 8]
                if not b.held:
                    b.held = True
                    return b
            raise AssertionError("every bank is held")

        def bank4():
            rot[1] += 1
            return banks[rot[1] % 4]

        ring = sb("ring", [128, NSLOT, 4096])
        slot_sem = [[sem(f"slot{i}"), 0] for i in range(NSLOT)]
        slot_free = [None] * NSLOT
        slots = list(range(NSLOT))
        rp = [0]

        cF = sb("cF", [128, 3, 128])
        ident, triu, triS = cF[:, 0, :], cF[:, 1, :], cF[:, 2, :]
        cB = sb("cB", [128, 8, 128], BF16)
        identb, negU = cB[:, 0, :], cB[:, 1:5, :]
        swm = sb("swm", [128, 3, 272], BF16)
        ones = sb("ones", [128, 128])
        halves = sb("halves", [128, 8])
        flags = sb("flags", [128, 2])
        col = sb("col", [128, NCOL])
        row = sb("row", [128, NROW])
        posi = sb("posi", [128, 2], I32)
        wrt = sb("wrt", [128, 2, 8, 36])

        def C(name, i=0, n=1):
            b = COLS[name][0]
            return col[:, b + i:b + i + n]

        def R(name):
            b, w = ROWS[name]
            return row[:, b:b + w]

        h = sb("h", [128, 3, 1024])
        xT = sb("xT", [128, 8, 384])
        lnb = sb("lnb", [128, 2, 1024])
        big = sb("big", [128, 16 * 272])
        work = sb("work", [128, 7680])
        small = sb("small", [128, 704])

        xs_ = {n: sem("x_" + n) for n in ("pe", "dve", "act", "dma", "arrived", "go_pe", "go_act", "go_sp")}
        ln_sem = [sem("lnd"), 0]
        c_sem = [sem("cst"), 0]
        out_sem = [sem("outd"), 0]
        d2 = [sem("d2"), 0]

        def area(t, at, shape):
            n = int(np.prod(shape))
            ap = t[:, at:at + n]
            if len(shape) == 2:
                ap = ap.rearrange("p (a b) -> p a b", a=shape[0])
            elif len(shape) == 3:
                ap = ap.rearrange("p (a b c) -> p a b c", a=shape[0], b=shape[1])
            elif len(shape) == 4:
                ap = ap.rearrange("p (a b c d) -> p a b c d", a=shape[0], b=shape[1], c=shape[2])
            return ap

        class Arena:
            def __init__(self, t, size):
                self.t, self.size, self.at = t, size, 0

            def __call__(self, *shape):
                n = int(np.prod(shape))
                assert self.at + n <= self.size, (self.at, n, self.size)
                a = area(self.t, self.at, shape)
                self.at += n
                return a

        def everyone():
            return [q.now() for q in (pe, dve, act, pool)]

        def barrier():
            t = everyone()
            for q in (pe, dve, act, pool):
                q.wait(*t)

        def cload(dst, src):
            return sp.dma(lambda e: e.dma_start(dst, src), c_sem)

        cload(h[:, 0:2, :], A["x"].rearrange("a (t p) d -> p (a t) d", p=128))
        cload(cF[:, :, :], A["cF"])
        cload(cB[:, :, :].bitcast(U16), A["cB"])
        cload(col[:, :], A["col"])
        cload(row[:, :], A["row"].broadcast_to([128, NROW]))
        cload(posi[:, :], A["pos"])
        cload(wrt[:, :, :, :], A["wr"].rearrange("l p k n -> p l k n"))
        cload(swm[:, :, :].bitcast(U16), A["swm"])

        def chunk(*pieces):
            i = slots[rp[0] % len(slots)]
            rp[0] += 1
            v = ring[:, i, :]
            for n, (view, src) in enumerate(pieces):
                tok = sp.dma(lambda e, d=view(v), s=src: e.dma_start(d, s), slot_sem[i],
                             slot_free[i] if n == 0 else None)
            slot_free[i] = None
            return v, tok, i

        def done(c, tok):
            slot_free[c[2]] = tok

        def kview(k, n, k0=0, n0=0, w=None):
            return lambda v: v[:, 0:k * n].rearrange("p (k n) -> p k n", k=k)[:, :, n0:n0 + (w or n)]

        def src(w, r0, r1, c0, c1):
            return w[r0:r1, c0:c1].rearrange("(k p) n -> p k n", p=128)

        def load_ln(i):
            return act.dma(lambda e: e.dma_start(lnb[:, :, :], A["lnp"][i:i + 1, :, :].broadcast_to([128, 2, 1024])),
                          ln_sem, dve.now(), pool.now())

        t_ones = dve.seq(lambda e: e.memset(ones[:, :], 1.0))
        dve.seq(lambda e: e.memset(halves[:, :], -0.5))
        t_xz = dve.seq(lambda e: e.memset(xT[:, :, 256:384], 0.0))
        tz = dve.seq(lambda e: e.memset(h[:, 2, :], 0.0))
        tokC = sp.dma(lambda e: e.dma_start(h[0:16, 2, :], A["meta"]), c_sem, tz)
        for q in (pe, dve, act, pool):
            q.wait(tokC, t_xz)

        def copy(q, dst, src_, *after):
            if q is act:
                return act.seq(lambda e: e.copy(dst, src_), *after)
            return q.seq(lambda e: e.tensor_copy(dst, src_), *after)

        def rsqrt(x):
            n = halves[:, 0:int(np.prod(x.shape[1:]))]
            if len(x.shape) == 3:
                n = n.rearrange("p (a b) -> p a b", a=x.shape[1])
            dve.wait(pool.seq(lambda e: e.tensor_tensor(x, x, n, ALU.pow), dve.now()))

        def to_T(t, tok, ks=(0, 4)):
            last = []
            for k in ks:
                b = bank8()
                pe.wait(tok, b.free)
                for kk in range(4):
                    tp = pe.op(lambda e: e.transpose(b.t[:, kk * 128:kk * 128 + 128],
                                                     h[:, t, (k + kk) * 128:(k + kk + 1) * 128], ident))
                b.free = copy(act, xT[:, k:k + 4, t * 128:(t + 1) * 128],
                              b.t[:, :].rearrange("p (k t) -> p k t", k=4), tp)
                last.append(b.free)
            return last

        def add_residual(acc, t, tacc):
            for n in range(2):
                b = acc[t][n]
                hh = h[:, t, n * 512:(n + 1) * 512]
                b.free = dve.seq(lambda e: e.scalar_tensor_tensor(
                    out=hh, in0=hh, scalar=ALPHA, in1=b.t[:, :], op0=ALU.mult, op1=ALU.add), tacc[t, n])

        m = Arena(small, 704)
        st, mv, rs_, nm = m(2, 2, 6), m(2, 2), m(2), m(2)
        gl, el, mk, wg, rk, oh, tmp = m(2, 8), m(2, 32), m(2, 32), m(2, 32), m(2, 32), m(2, 32), m(2, 32)
        gm, mx, mi, fi, s4 = m(2, 4), m(2, 8), m(2, 8), m(2, 8), m(2, 8)
        wres, wtmp = m(2, 32), m(2, 32)

        def layer_norm(t, tln, turned=True):
            for n in range(2):
                dve.seq(lambda e: e.bn_stats(st[:, t, n, :], h[:, t, n * 512:(n + 1) * 512]))
            dve.seq(lambda e: e.bn_aggr(mv[:, t, :], st[:, t, :, :].rearrange("p a b -> p (a b)")))
            r_, nm_ = rs_[:, t:t + 1], nm[:, t:t + 1]
            dve.seq(lambda e: e.tensor_scalar(r_, mv[:, t, 1:2], EPS1, None, ALU.add))
            rsqrt(r_)
            tk = dve.seq(lambda e: e.scalar_tensor_tensor(out=nm_, in0=mv[:, t, 0:1], scalar=-1.0, in1=r_,
                                                          op0=ALU.mult, op1=ALU.mult))
            tk = [act.seq(lambda e: e.activation(h[:, t, n * 512:(n + 1) * 512], h[:, t, n * 512:(n + 1) * 512],
                                                 ACT.Identity, bias=nm_, scale=r_), tk) for n in range(2)]
            last = []
            for n in range(2):
                c_ = slice(n * 512, (n + 1) * 512)
                dve.seq(lambda e: e.tensor_tensor(h[:, t, c_], h[:, t, c_], lnb[:, 0, c_], ALU.mult), tk[n], tln)
                th = dve.seq(lambda e: e.tensor_tensor(h[:, t, c_], h[:, t, c_], lnb[:, 1, c_], ALU.add))
                if turned:
                    last.append(to_T(t, th, (4 * n,))[-1])
            return th, last

        def mixed(layer, acc, tacc, tln):
            dve.wait(act.now(), pool.now())
            b = bank8()
            for t in range(2):
                add_residual(acc, t, tacc)
                th, tx = layer_norm(t, tln)
                tk = project(b.t[:, 64 * t:64 * t + 36], lambda k: xT[:, k, t * 128:(t + 1) * 128],
                             lambda k: wrt[:, layer, k, :], range(8), tx, b.free)
            route(b, tk)
            return th

        def mm(outp, l, r, start, stop, skip=False):
            return lambda e: e.matmul(outp, l, r, start=start, stop=stop, skip_group_check=skip)

        def project(bout, lhs, rhs, ks, *after, start=True, stop=True):
            ks = list(ks)
            pe.wait(*after)
            for k in ks[:-1]:
                pe.raw(mm(bout, lhs(k), rhs(k), start and k == ks[0], False))
            k = ks[-1]
            return pe.op(mm(bout, lhs(k), rhs(k), start and k == ks[0], stop))

        def out_proj(w, actT, t_act, acc, tacc, halves_):
            kt = w.shape[0] // 128
            for k0 in halves_:
                cs_ = [chunk((kview(8, 512), src(w, k0 * 128, k0 * 128 + 1024, n * 512, n * 512 + 512)))
                       for n in range(2)]
                for t in range(2):
                    for n in range(2):
                        b = acc[t][n]
                        tacc[t, n] = project(b.t[:, :], lambda k: actT[:, k, t * 128:(t + 1) * 128],
                                             lambda k: kview(8, 512)(cs_[n][0])[:, k - k0, :], range(k0, k0 + 8),
                                             cs_[n][1], t_act(), b.free if k0 == 0 else None,
                                             start=k0 == 0, stop=k0 == kt - 8)
                        yield
                for n in range(2):
                    done(cs_[n], tacc[1, n])

        def route(b, tk):
            iota4, iota32 = bc(R("iota")[:, 0:4], 1, 2), bc(R("iota")[:, 0:32], 1, 2)
            lg = b.t[:, 0:128].rearrange("p (t n) -> p t n", t=2)
            dve.seq(lambda e: e.memset(gl, LOW))
            dve.seq(lambda e: e.tensor_copy(gl[:, :, 0:4], lg[:, :, 0:4]), tk)
            b.free = dve.seq(lambda e: e.tensor_copy(el, lg[:, :, 4:36]))

            def largest(x):
                for t in range(2):
                    dve.seq(lambda e: e.max(mx[:, t, :], x[:, t, :]))
                    dve.seq(lambda e: e.max_index(mi[:, t, :].bitcast(U32), mx[:, t, :], x[:, t, :]))
                dve.seq(lambda e: e.tensor_copy(fi, mi.bitcast(U32)))

            g4 = gl[:, :, 0:4]
            e4 = el.rearrange("p t (g e) -> p t g e", g=4)
            largest(gl)
            tk = dve.seq(lambda e: e.tensor_tensor(g4, g4, bc(mx[:, :, 0], 2, 4), ALU.subtract))
            tk = act.seq(lambda e: e.activation(g4, g4, ACT.Exp), tk)
            dve.seq(lambda e: e.tensor_tensor(gm, iota4, bc(fi[:, :, 0], 2, 4), ALU.is_equal))
            dve.seq(lambda e: e.tensor_tensor(e4, e4, bc(gm, 3, 8), ALU.mult))
            dve.seq(lambda e: e.tensor_scalar(gm, gm, 1.0, -LOW, ALU.subtract, ALU.mult))
            dve.seq(lambda e: e.tensor_tensor(e4, e4, bc(gm, 3, 8), ALU.add))
            dve.seq(lambda e: e.tensor_reduce(s4[:, :, 1], g4, AXX, ALU.add), tk)
            largest(el)
            tk = dve.seq(lambda e: e.tensor_tensor(s4[:, :, 3], mx[:, :, 1], mx[:, :, 0], ALU.subtract))
            tk = act.seq(lambda e: e.activation(s4[:, :, 4], s4[:, :, 3], ACT.Exp), tk)
            dve.seq(lambda e: e.tensor_tensor(mk, iota32, bc(fi[:, :, 0], 2, 32), ALU.is_equal))
            dve.seq(lambda e: e.tensor_tensor(oh, iota32, bc(fi[:, :, 1], 2, 32), ALU.is_equal))
            dve.seq(lambda e: e.scalar_tensor_tensor(out=s4[:, :, 5], in0=s4[:, :, 4], scalar=1.0, in1=s4[:, :, 1],
                                                op0=ALU.add, op1=ALU.mult), tk)
            dve.seq(lambda e: e.reciprocal(s4[:, :, 6], s4[:, :, 5]))
            dve.seq(lambda e: e.tensor_tensor(s4[:, :, 7], s4[:, :, 6], s4[:, :, 4], ALU.mult))
            dve.seq(lambda e: e.tensor_tensor(wg, mk, bc(s4[:, :, 6], 2, 32), ALU.mult))
            dve.seq(lambda e: e.tensor_tensor(tmp, oh, bc(s4[:, :, 7], 2, 32), ALU.mult))
            dve.seq(lambda e: e.tensor_tensor(wg, wg, tmp, ALU.add))
            dve.seq(lambda e: e.tensor_tensor(mk, mk, oh, ALU.add))

        def moe(layer, th):
            barrier()
            assert not any(b.held for b in banks)
            tln = load_ln(layer * 2 + 1)
            m = Arena(work, 7680)
            flag = flags[:, layer:layer + 1]
            S, SW, SWT = m(2, 2, 128), m(2, 2, 128), m(2, 2, 128)
            xgT, sg, hs, hT = m(2, 8, 128), m(512), m(512), m(4, 128)
            ys, xgs = area(big, 0, (1024,)), area(big, 1024, (1024,))
            iota64 = R("iota")[:, 0:64]
            tm = dve.now()
            b = bank4()
            pe.wait(tm, b.free)
            pe.op(mm(b.t[:, 0:32], triS, mk[:, 0, :], True, True))
            pe.op(mm(b.t[:, 32:64], ones[:, :], mk[:, 0, :], True, False))
            tk = pe.op(mm(b.t[:, 32:64], triS, mk[:, 1, :], False, True))
            dve.seq(lambda e: e.scalar_tensor_tensor(
                out=rk.rearrange("p t e -> p (t e)"), in0=b.t[:, 0:64], scalar=1.0,
                in1=mk.rearrange("p t e -> p (t e)"), op0=ALU.add, op1=ALU.mult), tk)
            b.free = dve.seq(lambda e: e.tensor_scalar(rk, rk, 1.0, None, ALU.subtract))

            acc = [[banks[4], banks[5]], [banks[6], banks[7]]]
            accfree = [x.free for p in acc for x in p]
            gate_w, up_w, down_w = A["wg"], A["wu"], A["wd"]
            NP = NE // 2
            tG, tSWT, tX, tH, tY, tD, tacc = {}, {}, {}, {}, {}, {}, {}

            def lists(p):
                i = p % 2
                for j in range(2):
                    e_ = 2 * p + j
                    for t in range(2):
                        dve.seq(lambda e: e.tensor_scalar(
                            S[:, i, t, 64 * j:64 * j + 64], iota64, rk[:, t, e_:e_ + 1], None, ALU.is_equal),
                            tX.get(p - 2), tSWT.get(p - 2))
                        tk = dve.seq(lambda e: e.tensor_scalar(
                            SW[:, i, t, 64 * j:64 * j + 64], iota64, rk[:, t, e_:e_ + 1], wg[:, t, e_:e_ + 1],
                            ALU.is_equal, ALU.mult))
                return tk

            def gather(p):
                tS = lists(p)
                for n in range(2):
                    b = bank4()
                    pe.wait(tS, th, b.free)
                    for t in range(2):
                        tk = pe.op(mm(b.t[:, :], S[:, p % 2, t, :], h[:, t, n * 512:(n + 1) * 512], t == 0, t == 1))
                    b.free = copy(act if n else dve, xgs[:, n * 512:(n + 1) * 512], b.t[:, :], tk, tX.get(p - 1))
                    tG[p, n] = b.free
                b = bank4()
                pe.wait(b.free)
                for t in range(2):
                    tk = pe.op(lambda e: e.transpose(b.t[:, t * 128:(t + 1) * 128], SW[:, p % 2, t, :], ident))
                b.free = tSWT[p] = act.seq(lambda e: e.copy(
                    SWT[:, p % 2, :, :], b.t[:, 0:256].rearrange("p (t n) -> p t n", t=2)), tk, tD.get(p - 2))

            def turn_x(p):
                for n in range(2):
                    b = bank4()
                    pe.wait(tG[p, n], b.free)
                    for k in range(4):
                        s_ = xgs[:, (4 * n + k) * 128:(4 * n + k + 1) * 128]
                        tX[p] = pe.op(lambda e: e.transpose(b.t[:, k * 128:(k + 1) * 128], s_, ident))
                    b.free = tG[p, 2 + n] = copy(act if n else dve, xgT[:, p % 2, 4 * n:4 * n + 4, :],
                                                 b.t[:, :].rearrange("p (k s) -> p k s", k=4), tX[p])

            def hidden(p):
                bk = []
                for w in (gate_w, up_w):
                    cs_ = [chunk((kview(8, 512), w[layer, 2 * p + j].rearrange("(k p) n -> p k n", p=128)))
                           for j in range(2)]
                    b = bank4()
                    bk.append(b)
                    pe.wait(tG[p, 2], tG[p, 3], b.free, cs_[0][1], cs_[1][1])
                    for k in range(8):
                        for j in range(2):
                            tk = pe.op(mm(b.t[64 * j:64 * j + 64, :], xgT[:, p % 2, k, 64 * j:64 * j + 64],
                                          kview(8, 512)(cs_[j][0])[:, k, :], k == 0, k == 7))
                    for c in cs_:
                        done(c, tk)
                    if w is gate_w:
                        b.free = tg = act.seq(lambda e: e.activation(sg, b.t[:, :], ACT.Silu), tk, dve.now())
                b.free = tH[p] = dve.seq(lambda e: e.tensor_tensor(hs, sg, b.t[:, :], ALU.mult), tk, tg, tH.get("t"))

            def turn_h(p):
                b = bank4()
                pe.wait(tH[p], b.free)
                for f in range(4):
                    tk = pe.op(lambda e: e.transpose(b.t[:, f * 128:(f + 1) * 128], hs[:, f * 128:(f + 1) * 128], ident))
                tH["t"] = tk
                b.free = tH["T"] = act.seq(lambda e: e.copy(hT, b.t[:, :].rearrange("p (f s) -> p f s", f=4)), tk,
                                           tY.get(p - 1))

            def down(p):
                cs_ = [chunk((kview(4, 1024), down_w[layer, 2 * p + j].rearrange("(k p) n -> p k n", p=128)))
                       for j in range(2)]
                for n in range(2):
                    b = bank4()
                    pe.wait(tH["T"], b.free, cs_[0][1], cs_[1][1])
                    for f in range(4):
                        for j in range(2):
                            tk = pe.op(mm(b.t[64 * j:64 * j + 64, :], hT[:, f, 64 * j:64 * j + 64],
                                          kview(4, 1024)(cs_[j][0])[:, f, n * 512:(n + 1) * 512], f == 0, f == 3))
                    b.free = tY[p, n] = copy(act if n else dve, ys[:, n * 512:(n + 1) * 512], b.t[:, :], tk,
                                             tD.get(p - 1))
                tY[p] = tk
                for c in cs_:
                    done(c, tk)

            def spread(p):
                for n in range(2):
                    for t in range(2):
                        pe.wait(accfree if p == 0 else None, tY[p, n], tSWT[p])
                        tk = tacc[t, n] = pe.op(mm(acc[t][n].t[:, :], SWT[:, p % 2, t, :],
                                                   ys[:, n * 512:(n + 1) * 512], p == 0, p == NP - 1))
                tD[p] = tk

            gather(0)
            turn_x(0)
            dve.seq(lambda e: e.scalar_tensor_tensor(
                out=wres.rearrange("p t e -> p (t e)"), in0=rk.rearrange("p t e -> p (t e)"), scalar=CAP - 0.5,
                in1=wg.rearrange("p t e -> p (t e)"), op0=ALU.is_gt, op1=ALU.mult))
            b = bank4()
            pe.wait(b.free)
            pe.op(mm(b.t[:, 0:32], ones[:, :], mk[:, 0, :], True, False))
            tk = pe.op(mm(b.t[:, 0:32], ones[:, :], mk[:, 1, :], False, True))
            b.free = dve.seq(lambda e: e.tensor_reduce(flag, b.t[:, 0:32], AXX, ALU.max), tk)
            tflag = dve.seq(lambda e: e.tensor_scalar(flag.bitcast(I32), flag, CAP + 0.5, None, ALU.is_gt))
            for p in range(NP):
                hidden(p)
                if p:
                    spread(p - 1)
                if p + 1 < NP:
                    gather(p + 1)
                turn_h(p)
                if p + 1 < NP:
                    turn_x(p + 1)
                down(p)
            spread(NP - 1)
            for t in range(2):
                add_residual(acc, t, tacc)
            crowded(layer, flag, tflag, wres, wtmp)
            for b in banks:
                b.held = False
            return tln

        def crowded(layer, flag, tflag, wres, wtmp):
            barrier()
            sp.wait(*everyone(), *slot_free)
            X = {n: Queue(xs_[n]) for n in ("pe", "dve", "act")}
            xp, xd, xa, xsp = X["pe"], X["dve"], X["act"], Queue(xs_["pe"])
            gx, hx, hTx = area(big, 2048, (512,)), area(big, 2560, (512,)), area(big, 3072, (4, 128))
            wgv, wuv, wdv = kview(8, 512)(ring[:, 0, :]), kview(8, 512)(ring[:, 1, :]), kview(4, 1024)(ring[:, 2, :])
            tw = (xs_["dma"], 48)
            B = [Bank(x.t) for x in banks]
            for t in range(2):
                g, u = B[0], B[1]
                for bb, wv in ((g, wgv), (u, wuv)):
                    xp.wait(tw, bb.free)
                    for k in range(8):
                        tk = xp.op(mm(bb.t[:, :], xT[:, k, t * 128:(t + 1) * 128], wv[:, k, :], k == 0, k == 7))
                tg = xa.seq(lambda e: e.activation(gx, g.t[:, :], ACT.Silu), tk, xd.now())
                xd.seq(lambda e: e.tensor_tensor(hx, gx, u.t[:, :], ALU.mult), tg)
                th_ = xd.seq(lambda e: e.tensor_scalar(hx, hx, wres[:, t, 0:1], None, ALU.mult))
                g.free = u.free = th_
                xp.wait(th_, B[2].free)
                for f in range(4):
                    tk = xp.op(lambda e: e.transpose(B[2].t[:, f * 128:(f + 1) * 128], hx[:, f * 128:(f + 1) * 128],
                                                     ident))
                B[2].free = tT = xd.seq(lambda e: e.tensor_copy(hTx, B[2].t[:, :].rearrange("p (f s) -> p f s", f=4)), tk)
                for n in range(2):
                    bb = B[3 + n]
                    xp.wait(tT, bb.free)
                    for f in range(4):
                        tk = xp.op(mm(bb.t[:, :], hTx[:, f, :], wdv[:, f, n * 512:(n + 1) * 512], f == 0, f == 3))
                    hh = h[:, t, n * 512:(n + 1) * 512]
                    bb.free = xd.seq(lambda e: e.tensor_tensor(hh, hh, bb.t[:, :], ALU.add), tk)
            xd.seq(lambda e: e.tensor_copy(wtmp[:, :, 0:31], wres[:, :, 1:32]))
            xd.seq(lambda e: e.tensor_copy(wres[:, :, 0:31], wtmp[:, :, 0:31]))
            counted = (xs_["pe"], xs_["dve"], xs_["act"], xs_["dma"], xs_["arrived"])

            def section(q, body, mine, go):
                def play(e):
                    v = e.value_load(flag[0:1, 0:1].bitcast(I32))
                    with e.If(v):
                        with e.Fori(0, NE) as i:
                            body(e, i)
                            if mine is not None:
                                e.wait_ge(mine.sem, mine.n)
                            if go is not None:
                                e.sem_inc(xs_["arrived"], 1)
                                e.wait_ge(go, 1)
                                e.sem_clear(go)
                            else:
                                e.wait_ge(xs_["arrived"], 3)
                                for s_ in counted:
                                    e.sem_clear(s_)
                                for s_ in ("go_pe", "go_act", "go_sp"):
                                    e.sem_inc(xs_[s_], 1)
                q.wait(tflag)
                q.items.append(play)

            def loads(e, i):
                for n, w in enumerate((A["wg"], A["wu"], A["wd"])):
                    k = 4 if n == 2 else 8
                    dst = kview(k, 4096 // k)(ring[:, n, :])
                    e.dma_start(dst, w[layer].rearrange("x (k p) n -> x p k n", p=128)[bass.ds(i, 1)]
                                .rearrange("x p k n -> p (x k) n")).then_inc(xs_["dma"], 16)
                e.wait_ge(xs_["dma"], 48)

            section(sp, loads, None, xs_["go_sp"])
            section(pe, lambda e, i: xp.play(e), xp, xs_["go_pe"])
            section(act, lambda e, i: xa.play(e), xa, xs_["go_act"])
            section(dve, lambda e, i: xd.play(e), xd, None)

        w_in, w_out = A["ssm_w_in"], A["ssm_w_out"]
        tx = to_T(0, tokC) + to_T(1, tokC)
        tln = load_ln(0)
        m = Arena(small, 704)
        dt, dtA, acum, nega, expa, dte = m(2, 32), m(2, 32), m(2, 32), m(32), m(2, 32), m(32)
        t1, t2 = m(2, 32), m(2, 32)
        ssq, rsg = m(4), m(4)
        m = Arena(work, 7680)
        wdt = m(8, 32)
        zs, cv, cs = m(2, 2, 256), m(4, 256), m(2, 4, 256)
        xdt, xD, yv = m(2, 256), m(2, 256), m(2, 256)
        dec = m(2, 4, 128)
        xde, Bl, S0 = m(256), m(128), m(256)
        ygT = area(big, 0, (16, 256))
        tw = sp.dma(lambda e: e.dma_start(wdt, src(w_in, 0, 1024, 6144, 6176)), d2)
        b = bank8()
        for t in range(2):
            tk = project(b.t[:, t * 32:t * 32 + 32], lambda k: xT[:, k, t * 128:(t + 1) * 128],
                         lambda k: wdt[:, k, :], range(8), tx, tw, b.free)
        b.free = dve.seq(lambda e: e.tensor_tensor(dt, b.t[:, 0:64].rearrange("p (t n) -> p t n", t=2),
                                                   bc(R("dt_bias"), 1, 2), ALU.add), tk)
        tk = dve.seq(lambda e: e.scalar_tensor_tensor(out=t1, in0=dt, scalar=-1.0, in1=dt, op0=ALU.mult, op1=ALU.max))
        tk = act.seq(lambda e: e.activation(t1, t1, ACT.Exp, scale=-1.0), tk)
        tk = act.seq(lambda e: e.activation(t2, t1, ACT.Ln, bias=1.0), tk)
        dve.seq(lambda e: e.scalar_tensor_tensor(out=dt, in0=dt, scalar=0.0, in1=t2, op0=ALU.max, op1=ALU.add), tk)
        tk = act.seq(lambda e: e.activation(nega, R("a_log"), ACT.Exp))
        dve.seq(lambda e: e.tensor_scalar(nega, nega, -1.0, None, ALU.mult), tk)
        tk = dve.seq(lambda e: e.tensor_tensor(dtA, dt, bc(nega, 1, 2), ALU.mult))
        b = bank8()
        pe.wait(tk, b.free)
        for t in range(2):
            pe.op(mm(b.t[:, t * 32:t * 32 + 32], triu, dtA[:, t, :], True, True))
        tk = pe.op(mm(b.t[:, 64:96], ones[:, :], dtA[:, 0, :], True, True))
        dve.seq(lambda e: e.tensor_copy(acum.rearrange("p t n -> p (t n)"), b.t[:, 0:64]), tk)
        b.free = dve.seq(lambda e: e.tensor_tensor(dte, b.t[:, 64:96], acum[:, 0, :], ALU.subtract))
        tk = act.seq(lambda e: e.activation(dte, dte, ACT.Exp), b.free)
        tk = act.seq(lambda e: e.activation(expa, acum, ACT.Exp), tk)
        t_small = dve.seq(lambda e: e.tensor_tensor(dte, dte, dt[:, 0, :], ALU.mult), tk)

        T = {}

        def mamba_in(g):
            i = g % 2
            c = chunk((kview(8, 512, n0=0, w=256), src(w_in, 0, 1024, 256 * g, 256 * g + 256)),
                      (kview(8, 512, n0=256, w=256), src(w_in, 0, 1024, 2048 + 256 * g, 2048 + 256 * g + 256)))
            wv = kview(8, 512)(c[0])
            if i == 0:
                T["cBC"] = chunk(
                    (kview(8, 512, n0=0, w=256), src(w_in, 0, 1024, 4096 + 128 * g, 4096 + 128 * g + 256)),
                    (kview(8, 512, n0=256, w=256), src(w_in, 0, 1024, 5120 + 128 * g, 5120 + 128 * g + 256)))
            cBC = T["cBC"]
            wb = kview(8, 512)(cBC[0])
            for half in range(2):
                b = bank8()
                for j in range(2):
                    if half == 0:
                        lw, tw = wv[:, :, 256 + 128 * j:384 + 128 * j], c[1]
                    else:
                        lw, tw = wb[:, :, 256 * j + 128 * i:256 * j + 128 * i + 128], cBC[1]
                    tk = project(b.t[:, j * 256:(j + 1) * 256], lambda k: lw[:, k, :], lambda k: xT[:, k, 0:256],
                                 range(8), tw, b.free)
                    if j == 0:
                        yield
                for j in range(2):
                    blk = 2 * g + j if half == 0 else 16 + 8 * j + g
                    ps = b.t[:, j * 256:(j + 1) * 256]
                    o = cv[:, 2 * half + j, :]
                    dve.seq(lambda e: e.tensor_scalar(
                        o, ps, C("conv_w", 4 * blk + 3), C("conv_b", blk), ALU.mult, ALU.add), tk, T.get(("cs", g - 1)))
                    for s in range(1, 4):
                        td = dve.seq(lambda e: e.scalar_tensor_tensor(
                            out=o[:, s:256], in0=ps[:, 0:256 - s], scalar=C("conv_w", 4 * blk + 3 - s),
                            in1=o[:, s:256], op0=ALU.mult, op1=ALU.add))
                b.free = td
                yield
            if i == 1:
                done(cBC, tk)
            T["cs", g] = act.seq(lambda e: e.activation(cs[:, i], cv, ACT.Silu), td, T.get(("used", g - 2)))
            b = bank8()
            for t in range(2):
                tk = project(b.t[:, t * 256:(t + 1) * 256], lambda k: xT[:, k, t * 128:(t + 1) * 128],
                             lambda k: wv[:, k, 0:256], range(8), c[1], b.free)
                if t == 0:
                    yield
            done(c, tk)
            b.free = T["z", g] = act.seq(lambda e: e.activation(zs[:, i].rearrange("p t n -> p (t n)"), b.t[:, :],
                                                                ACT.Silu), tk, T.get(("gated", g - 2)))
            yield

        def mamba_scan(g):
            i = g % 2
            BT, CT = cs[:, i, 2, :], cs[:, i, 3, :]
            hs = slice(4 * g, 4 * g + 4)
            bx, bb = bank8(), bank8()
            pe.wait(T["cs", g], bx.free, bb.free)
            for t in range(2):
                for j in range(2):
                    tk = pe.op(lambda e: e.transpose(
                        bx.t[:, t * 256 + j * 128:t * 256 + j * 128 + 128], cs[:, i, j, t * 128:(t + 1) * 128], ident))
            pe.op(lambda e: e.transpose(bb.t[:, 0:128], BT[:, 0:128], ident))
            for t in range(2):
                tcb = pe.op(mm(bb.t[:, 128 + 128 * t:256 + 128 * t], BT[:, t * 128:(t + 1) * 128],
                               CT[:, t * 128:(t + 1) * 128], True, True))
            tB = act.seq(lambda e: e.copy(Bl, bb.t[:, 0:128]), tcb, T.get(("S", g - 1)))
            x4 = bx.t[:, :].rearrange("p (t h q) -> p t h q", t=2, h=4)
            dve.seq(lambda e: e.tensor_tensor(
                xdt.rearrange("p t (h q) -> p t h q", h=4), x4, bc(dt[:, :, hs], 3, 64), ALU.mult), tk)
            dve.seq(lambda e: e.tensor_tensor(
                xde.rearrange("p (h q) -> p h q", h=4), x4[:, 0], bc(dte[:, hs], 2, 64), ALU.mult))
            bx.free = txd = dve.seq(lambda e: e.tensor_tensor(
                xD.rearrange("p t (h q) -> p (t h) q", h=4).rearrange("p (t h) q -> p t h q", t=2), x4,
                bc(bc(R("ssm_d")[:, hs], 1, 2), 3, 64), ALU.mult))
            yield
            segs = []
            for t in range(2):
                b = bank8()
                pe.wait(b.free)
                pe.op(mm(b.t[:, :], identb, negU.rearrange("p a b -> p (a b)"), True, True))
                for hh in range(4):
                    tk = pe.op(mm(b.t[:, hh * 128:(hh + 1) * 128],
                                  dtA[:, t, 4 * g + hh:4 * g + hh + 1].broadcast_to([128, 128]),
                                  triu, False, True, skip=True))
                b.free = tk = dve.seq(lambda e: e.tensor_tensor(
                    dec[:, t], b.t[:, :].rearrange("p (h l) -> p h l", h=4), bc(acum[:, t, hs], 2, 128),
                    ALU.subtract), tk)
                segs.append(act.seq(lambda e: e.activation(dec[:, t], dec[:, t], ACT.Exp), tk))
            bs = bank8()
            T["S", g] = tk = pe.op(mm(bs.t[:, 0:256], Bl, xde, True, True), bs.free, tB, txd)
            bs.free = tS0 = act.seq(lambda e: e.copy(S0, bs.t[:, 0:256]), tk)
            for t in range(2):
                tdec = dve.seq(lambda e: e.tensor_tensor(
                    dec[:, t], dec[:, t], bc(bb.t[:, 128 + 128 * t:256 + 128 * t], 1, 4), ALU.mult), segs[t], tB)
            bb.free = tdec
            yield
            by, bo = bank8(), bank8()
            pe.wait(by.free, bo.free, tdec, txd)
            for t in range(2):
                for hh in range(4):
                    ty = pe.op(mm(by.t[:, t * 256 + hh * 64:t * 256 + hh * 64 + 64], dec[:, t, hh, :],
                                  xdt[:, t, hh * 64:(hh + 1) * 64], True, True))
            T["used", g] = to = pe.op(mm(bo.t[:, 0:256], CT[:, 128:256], S0, True, True), tS0)
            by.free = dve.seq(lambda e: e.tensor_tensor(yv, by.t[:, :].rearrange("p (t n) -> p t n", t=2),
                                                        xD, ALU.add), ty, T.get(("y", g - 1)))
            bo.free = dve.seq(lambda e: e.tensor_tensor(
                xde.rearrange("p (h q) -> p h q", h=4), bo.t[:, 0:256].rearrange("p (h q) -> p h q", h=4),
                bc(expa[:, 1, hs], 2, 64), ALU.mult), to)
            dve.seq(lambda e: e.tensor_tensor(yv[:, 1], yv[:, 1], xde, ALU.add))
            T["gated", g] = tk = dve.seq(lambda e: e.tensor_tensor(yv, yv, zs[:, i], ALU.mult), T["z", g])
            for t in range(2):
                tk = act.seq(lambda e: e.activation(xD[:, t], yv[:, t], ACT.Square, accum_out=ssq[:, t:t + 1]), tk)
            dve.seq(lambda e: e.tensor_scalar(rsg[:, 0:2], ssq[:, 0:2], 1.0 / 256, EPS1, ALU.mult, ALU.add), tk)
            rsqrt(rsg[:, 0:2])
            for t in range(2):
                tk = dve.seq(lambda e: e.tensor_scalar(yv[:, t], yv[:, t], rsg[:, t:t + 1], None, ALU.mult))
            yield
            b = bank8()
            pe.wait(b.free, tk)
            for j in range(2):
                for t in range(2):
                    tk = pe.op(lambda e: e.transpose(
                        b.t[:, j * 256 + t * 128:j * 256 + t * 128 + 128], yv[:, t, j * 128:(j + 1) * 128], ident))
            T["y", g] = tk
            for j in range(2):
                ev = act.seq(lambda e: e.activation(
                    ygT[:, 2 * g + j, :], b.t[:, j * 256:(j + 1) * 256], ACT.Copy, scale=C("norm_w", 2 * g + j)), tk)
            b.free = T["ygT"] = ev
            yield

        run(mamba_in(0))
        for g in range(7):
            weave((mamba_scan(g), 1), (mamba_in(g + 1), 2))
        acc = [[bank8(), bank8()] for _ in range(2)]
        tacc = {}
        weave((mamba_scan(7), 1), (out_proj(w_out, ygT, lambda: T["ygT"], acc, tacc, (0,)), 1))
        run(out_proj(w_out, ygT, lambda: T["ygT"], acc, tacc, (8,)))
        tln = moe(0, mixed(0, acc, tacc, tln))
        tx = [x for t in range(2) for x in layer_norm(t, tln)[1]]

        barrier()
        tln = load_ln(2)
        slots.remove(NSLOT - 1)
        m = Arena(small, 704)
        cosT, sinT, ang, a2 = m(2, 8), m(2, 8), m(2, 8), m(2, 8)
        pf, lp, lam = m(2), m(2), m(4)
        mxs, sums, ss = [m(2, 2), m(2, 2)], [m(2, 2), m(2, 2)], m(4, 2)
        u4 = [m(2, 64) for _ in range(4)]
        m = Arena(work, 7680)
        qs, ks_, vs = m(2, 512), m(2, 512), [m(2, 512), m(2, 512)]
        es = [m(2, 384), m(2, 384)]
        aT, osb = [m(3, 128), m(3, 128)], m(4, 2, 128)
        oT = area(big, 0, (8, 256))
        qT = [area(big, 2048, (4, 256)), area(big, 3072, (4, 256))]
        kT = [area(ring[:, NSLOT - 1, :], i * 1024, (4, 256)) for i in range(2)]
        dve.seq(lambda e: e.tensor_copy(pf, posi[:, :]))
        dve.seq(lambda e: e.tensor_tensor(ang, bc(pf, 2, 8), bc(R("inv"), 1, 2), ALU.mult))
        TP = 2 * math.pi
        C1 = float(np.float32(6.28125))
        C2 = float((np.array([TP - C1], np.float32).view(np.uint32) & np.uint32(0xFFFFF000)).view(np.float32)[0])
        C3 = float(np.float32(TP - C1 - C2))
        MG = 12582912.0

        def wrap(x):
            dve.seq(lambda e: e.tensor_scalar(a2, x, 1.0 / TP, None, ALU.mult))
            dve.seq(lambda e: e.tensor_scalar(a2, a2, MG, None, ALU.add))
            dve.seq(lambda e: e.tensor_scalar(a2, a2, MG, None, ALU.subtract))
            for cc in (C1, C2, C3):
                dve.seq(lambda e, cc=cc: e.scalar_tensor_tensor(out=x, in0=a2, scalar=-cc, in1=x,
                                                                op0=ALU.mult, op1=ALU.add))
            PI = float(np.nextafter(np.float32(math.pi), np.float32(0)))
            return dve.seq(lambda e: e.tensor_scalar(x, x, PI, -PI, ALU.min, ALU.max))

        tk = wrap(ang)
        tk = act.seq(lambda e: e.activation(sinT, ang, ACT.Sin), tk)
        dve.seq(lambda e: e.tensor_scalar(ang, ang, math.pi / 2, None, ALU.add), tk)
        tk = wrap(ang)
        trope = act.seq(lambda e: e.activation(cosT, ang, ACT.Sin), tk)
        dve.seq(lambda e: e.tensor_tensor(lp[:, 0:1], C("lamv", 0), C("lamv", 1), ALU.mult))
        tk = dve.seq(lambda e: e.tensor_tensor(lp[:, 1:2], C("lamv", 2), C("lamv", 3), ALU.mult))
        b = bank8()
        tk = pe.op(mm(b.t[:, 0:2], ones[:, :], lp, True, True), b.free, tk)
        b.free = tk = act.seq(lambda e, b=b: e.activation(lam[:, 0:2], b.t[:, 0:2], ACT.Exp), tk)
        dve.seq(lambda e: e.tensor_tensor(lam[:, 2:3], lam[:, 1:2], lam[:, 0:1], ALU.subtract), tk)
        tlam = dve.seq(lambda e: e.tensor_scalar(lam[:, 2:3], lam[:, 2:3], LI, None, ALU.subtract))
        w = A["attn_w_qkv"]
        scale1 = 64 ** -0.5
        T = {}

        def qkv(hg, which, t):
            if t == 0:
                T["c", which] = chunk((kview(8, 512), src(w, 0, 1024, which * 1024 + hg * 512,
                                                          which * 1024 + hg * 512 + 512)))
            c = T["c", which]
            dst = (qs, ks_, vs[hg])[which]
            b = bank8()
            tk = project(b.t[:, :], lambda k: xT[:, k, t * 128:(t + 1) * 128],
                         lambda k: kview(8, 512)(c[0])[:, k, :], range(8), c[1], tx, b.free)
            b.free = T["r", which] = T["v", hg] = act.seq(lambda e: e.copy(dst[:, t, :], b.t[:, :]), tk)
            if t == 1:
                done(c, tk)

        def rope(which):
            v4 = (qs, ks_)[which].rearrange("p t (c d) -> p t c d", c=8)
            r1, r2 = v4[:, :, :, 0:8], v4[:, :, :, 8:16]
            cb_, sb_ = bc(cosT, 2, 8), bc(sinT, 2, 8)
            u = [x.rearrange("p t (c d) -> p t c d", c=8) for x in u4]
            dve.seq(lambda e: e.tensor_tensor(u[0], r1, cb_, ALU.mult), T["r", which], trope)
            dve.seq(lambda e: e.tensor_tensor(u[1], r2, sb_, ALU.mult))
            dve.seq(lambda e: e.tensor_tensor(u[2], r2, cb_, ALU.mult))
            dve.seq(lambda e: e.tensor_tensor(u[3], r1, sb_, ALU.mult))
            dve.seq(lambda e: e.tensor_tensor(r1, u[0], u[1], ALU.subtract))
            T["roped", which] = dve.seq(lambda e: e.tensor_tensor(r2, u[2], u[3], ALU.add))

        def turn_qk(hg, which):
            dT, s_ = (qT, kT)[which][hg], (qs, ks_)[which]
            for hp in range(2):
                b = bank8()
                pe.wait(T["roped", which], b.free)
                for j in range(2):
                    for t in range(2):
                        tk = pe.op(lambda e: e.transpose(
                            b.t[:, j * 256 + t * 128:j * 256 + t * 128 + 128],
                            s_[:, t, (2 * hp + j) * 128:(2 * hp + j + 1) * 128], ident))
                b.free = T["T", hg, which] = act.seq(lambda e: e.copy(
                    dT[:, 2 * hp:2 * hp + 2, :], b.t[:, :].rearrange("p (j t) -> p j t", j=2)), tk)

        def scores(hd):
            hg, hh, i = hd // 4, hd % 4, hd % 2
            e_, mx_, sm_ = es[i], mxs[i], sums[i]
            pe.wait(T["T", hg, 0], T["T", hg, 1])
            bs = []
            for cc in range(2):
                b = bank8()
                bs.append(b)
                pr = slice(64 * cc, 64 * cc + 64)
                pe.op(mm(b.t[:, 0:384], identb, cB[:, 5:8, :].rearrange("p a b -> p (a b)"), True, True), b.free)
                pe.op(mm(b.t[:, 0:128], qT[hg][pr, hh, 0:128], kT[hg][pr, hh, 0:128], False, True, skip=True))
                tk = pe.op(mm(b.t[:, 128:384], qT[hg][pr, hh, 128:256], kT[hg][pr, hh, :], False, True, skip=True))
                for t, ks in enumerate((slice(0, 128), slice(128, 384))):
                    dve.seq(lambda e: e.tensor_reduce(mx_[:, cc, t:t + 1], b.t[:, ks], AXX, ALU.max), tk)
            tk = dve.seq(lambda e: e.tensor_scalar(mx_, mx_, -scale1, None, ALU.mult))
            for cc in range(2):
                b = bs[cc]
                for t, ks in enumerate((slice(0, 128), slice(128, 384))):
                    b.free = te = act.seq(lambda e: e.activation(
                        e_[:, cc, ks], b.t[:, ks], ACT.Exp, bias=mx_[:, cc, t:t + 1], scale=scale1,
                        accum_out=sm_[:, cc, t:t + 1]), tk)
            dve.seq(lambda e: e.reciprocal(sm_, sm_), te)
            dve.seq(lambda e: e.tensor_scalar(sm_[:, 1, :], sm_[:, 1, :], lam[:, 2:3], None, ALU.mult))
            for t, ks in enumerate((slice(0, 128), slice(128, 384))):
                dve.seq(lambda e: e.tensor_scalar(e_[:, 0, ks], e_[:, 0, ks], sm_[:, 0, t:t + 1], None, ALU.mult))
                T["p", hd] = dve.seq(lambda e: e.scalar_tensor_tensor(
                    out=e_[:, 0, ks], in0=e_[:, 1, ks], scalar=sm_[:, 1, t:t + 1], in1=e_[:, 0, ks],
                    op0=ALU.mult, op1=ALU.add))

        def turn_p(hd):
            b = bank8()
            pe.wait(b.free, T["p", hd])
            for kt in range(3):
                tk = pe.op(lambda e: e.transpose(b.t[:, kt * 128:(kt + 1) * 128],
                                                 es[hd % 2][:, 0, kt * 128:(kt + 1) * 128], ident))
            b.free = T["pT", hd] = act.seq(lambda e: e.copy(
                aT[hd % 2], b.t[:, 0:384].rearrange("p (a b) -> p a b", a=3)), tk)

        def values(hd):
            hg, hh = hd // 4, hd % 4
            b = bank8()
            pe.wait(b.free, T["pT", hd], T["v", hg])
            v = vs[hg][:, :, hh * 128:(hh + 1) * 128]
            pe.op(mm(b.t[:, 0:128], aT[hd % 2][:, 0, :], v[:, 0, :], True, True))
            pe.op(mm(b.t[:, 128:256], aT[hd % 2][:, 1, :], v[:, 0, :], True, False))
            tk = pe.op(mm(b.t[:, 128:256], aT[hd % 2][:, 2, :], v[:, 1, :], False, True))
            tc_ = act.seq(lambda e: e.copy(osb[:, hh], b.t[:, 0:256].rearrange("p (t e) -> p t e", t=2)), tk,
                          T.get("osb"))
            for t in range(2):
                b.free = T["o"] = act.seq(lambda e: e.activation(
                    b.t[:, t * 128:(t + 1) * 128], b.t[:, t * 128:(t + 1) * 128], ACT.Square,
                    accum_out=ss[:, hh, t:t + 1]), T.get("ss"))

        def subln(hg):
            dve.seq(lambda e: e.tensor_scalar(ss, ss, 1.0 / 128, EPS1, ALU.mult, ALU.add), T["o"])
            rsqrt(ss)
            dve.seq(lambda e: e.tensor_scalar(ss, ss, 1.0 - LI, None, ALU.mult))
            tk = T["ss"] = dve.seq(lambda e: e.tensor_tensor(osb, osb, bc(ss, 3, 128), ALU.mult))
            for hp in range(2):
                b = bank8()
                pe.wait(b.free, tk)
                for j in range(2):
                    for t in range(2):
                        tp = pe.op(lambda e: e.transpose(b.t[:, (2 * j + t) * 128:(2 * j + t + 1) * 128],
                                                         osb[:, 2 * hp + j, t, :], ident))
                T["osb"] = tp
                hd = 4 * hg + 2 * hp
                b.free = T["oT", hg] = act.seq(lambda e: e.activation(
                    oT[:, hd:hd + 2, :], b.t[:, :].rearrange("p (h t) -> p h t", h=2), ACT.Copy,
                    scale=C("subln")), tp)

        def attn_out(ks):
            for t in range(2):
                for n in range(2):
                    b = acc[t][n]
                    tacc[t, n] = project(b.t[:, :], lambda k: oT[:, k, t * 128:(t + 1) * 128],
                                         lambda k: kview(8, 512)(co[n][0])[:, k, :], ks, co[n][1],
                                         T["oT", ks[0] // 4], b.free if ks[0] == 0 else None,
                                         start=ks[0] == 0, stop=ks[-1] == 7)
                    yield

        for which in range(3):
            for t in range(2):
                qkv(0, which, t)
            if which < 2:
                rope(which)
        turn_qk(0, 0)
        turn_qk(0, 1)
        scores(0)
        for hd in range(8):
            if hd == 3:
                turn_qk(1, 1)
            if hd < 7:
                scores(hd + 1)
            if hd < 3:
                qkv(1, hd, 0)
                qkv(1, hd, 1)
                if hd < 2:
                    rope(hd)
                if hd == 2:
                    turn_qk(1, 0)
            elif hd == 4:
                acc, tacc = [[bank8(), bank8()] for _ in range(2)], {}
                co = [chunk((kview(8, 512), src(A["attn_w_o"], 0, 1024, n * 512, n * 512 + 512))) for n in range(2)]
                first_half = attn_out(range(0, 4))
            if hd >= 4:
                next(first_half)
            turn_p(hd)
            values(hd)
            if hd % 4 == 3:
                subln(hd // 4)
        run(attn_out(range(4, 8)))
        for n in range(2):
            done(co[n], tacc[1, n])
        slots.append(NSLOT - 1)
        tln = moe(1, mixed(1, acc, tacc, tln))

        barrier()
        del slots[NSLOT - 2:]
        m = m_small = Arena(small, 704)
        m(32)
        ssq, rs = m(4), m(4)
        s2 = [m(3, 2), m(3, 2)]
        mxn, sm, esk = [m(3), m(3)], [m(3), m(3)], m(3)

        def rms_T(t, tok, gname, c0, nt):
            zt, s_, r_ = area(work, 4608 + t * 1024, (1024,)), ssq[:, t:t + 1], rs[:, t:t + 1]
            tk = act.seq(lambda e: e.activation(zt, h[:, t, :], ACT.Square, accum_out=s_), tok)
            dve.seq(lambda e: e.tensor_scalar(r_, s_, 1.0 / 1024, EPS2, ALU.mult, ALU.add), tk)
            rsqrt(r_)
            tk = dve.seq(lambda e: e.tensor_scalar(zt, h[:, t, :], r_, None, ALU.mult))
            for k in range(0, 8, 4):
                b = bank8()
                pe.wait(tk, b.free)
                for kk in range(4):
                    tp = pe.op(lambda e: e.transpose(
                        b.t[:, kk * 128:kk * 128 + nt], zt[0:nt, (k + kk) * 128:(k + kk + 1) * 128],
                        ident[0:nt, 0:nt]))
                dst = xT[:, k:k + 4, c0:c0 + nt]
                b.free = ev = dve.seq(lambda e: e.tensor_tensor(
                    dst, b.t[:, :].rearrange("p (k t) -> p k t", k=4)[:, :, 0:nt],
                    bc(C(gname, k, 4), 2, nt), ALU.mult), tp)
            return ev

        w = A["even_w_in"]
        m = Arena(work, 7680)
        kp = m(3, 64)
        cqT, ckT = m(3, 384), m(2, 384)
        lat, junk = area(work, m.at, (3, 704)), area(work, m.at + 2112, (384,))
        sqb_q, uq = m(3, 2, 192), m(3, 2, 64)
        es, pt = [m(3, 272), m(3, 272)], [m(3, 272), m(3, 272)]
        RQ, RK = m(3, 2, 64), m(3, 2, 64)
        tail = ring[:, NSLOT - 2:NSLOT, :].rearrange("p s n -> p (s n)")
        m = Arena(tail, 8192)
        UQ, UK = m(3, 2, 192), m(3, 2, 192)
        vb = [m(3, 2, 128), m(3, 2, 128)]
        QN, KN = [m(2, 272), m(2, 272)], [m(2, 272), m(2, 272)]
        QR, KR = [m(272), m(272)], [m(272), m(272)]
        yT = area(big, 0, (16, 272))
        rt = lnb[:, :, :].rearrange("p a b -> p (a b)")
        squares = [sqb_q, area(rt, 576, (3, 2, 192))]
        cM, sM = area(rt, 0, (3, 32)), area(rt, 96, (3, 32))
        cS, sS = area(rt, 192, (3, 64)), area(rt, 384, (3, 64))
        T = {}

        def meta_proj(bank, lhs, rhs, ks, ncols, *after, start=True, stop=True):
            pe.wait(*after)
            ks = list(ks)
            for k in ks:
                j = k % 4
                tk = pe.op(mm(bank.t[32 * j:32 * j + 16, 0:ncols], lhs(k), rhs(k), start and k < ks[0] + 4,
                              stop and k > ks[-1] - 4))
            return tk

        def meta_sum(dst, x, bank, view, *after):
            for j in range(4):
                p_ = view(bank.t[32 * j:32 * j + 16])
                if j == 0 and x is None:
                    tk = dve.seq(lambda e: e.tensor_copy(dst, p_), *after)
                else:
                    a_ = x if j == 0 else dst
                    tk = dve.seq(lambda e: e.tensor_tensor(dst, a_, p_, ALU.add), *after)
            return tk

        def rows_proj(wv, ncols, tw, outs):
            for t in range(3):
                b = bank8()
                if t < 2:
                    tk = project(b.t[:, 0:ncols], lambda k: xT[:, k, t * 128:(t + 1) * 128], wv, range(8), tw, b.free)
                    for dst, a0 in outs:
                        b.free = te = act.seq(lambda e: e.copy(
                            dst(t, 128), b.t[:, a0:a0 + 256].rearrange("p (j d) -> p j d", j=2)), tk)
                else:
                    tk = meta_proj(b, lambda k: xT[:, k, 256:272], wv, range(8), ncols, tw, b.free)
                    for dst, a0 in outs:
                        b.free = meta_sum(dst(t, 16), None, b, lambda v: v[:, a0:a0 + 256].rearrange(
                            "p (j d) -> p j d", j=2), tk)
            return tk, [te, b.free]

        def gate(n):
            if n % 4 == 0:
                T["cg"] = chunk((kview(8, 512), src(w, 0, 1024, 2240 + 128 * n, 2240 + 128 * n + 512)))
            c = T["cg"]
            b = bank8()
            j = n % 4
            tk = project(b.t[:, 0:272], lambda k: kview(8, 512)(c[0])[:, k, j * 128:(j + 1) * 128],
                         lambda k: xT[:, k, 0:272], range(8), c[1], b.free)
            b.free = T["g", n] = act.seq(lambda e: e.activation(yT[:, n, :], b.t[:, 0:272], ACT.Silu), tk)
            if j == 3:
                done(c, tk)

        def norm_rope(U, UR, D, grow, ro, half, ct, st_, *ev):
            i = 0 if UR is RQ else 1
            sqb = squares[i]
            sq, s_ = sqb[:, :, :, 0:D], s2[0]
            tk = act.seq(lambda e: e.activation(sq, U[:, :, :, 0:D], ACT.Square), *ev, T.get(("rope", i)))
            dve.seq(lambda e: e.tensor_reduce(s_, sq, AXX, ALU.add), tk)
            dve.seq(lambda e: e.tensor_scalar(s_, s_, 1.0 / D, EPS2, ALU.mult, ALU.add))
            rsqrt(s_)
            dve.seq(lambda e: e.tensor_tensor(U[:, :, :, 0:D], U[:, :, :, 0:D], bc(s_, 3, D), ALU.mult))
            dve.seq(lambda e: e.tensor_tensor(U[:, :, :, 0:D], U[:, :, :, 0:D], bc(bc(grow, 1, 2), 1, 3), ALU.mult))
            x1, x2 = U[:, :, :, ro:ro + half], U[:, :, :, ro + half:ro + 2 * half]
            c_, s_ = bc(ct, 2, 2), bc(st_, 2, 2)
            f = sqb.rearrange("p t j d -> p (t j d)")
            u = [area(f, i * 384, (3, 2, half)) for i in range(3)] + [uq[:, :, :, 0:half]]
            dve.seq(lambda e: e.tensor_tensor(u[0], x1, c_, ALU.mult), trt)
            dve.seq(lambda e: e.tensor_tensor(u[1], x2, s_, ALU.mult))
            dve.seq(lambda e: e.tensor_tensor(u[2], x1, s_, ALU.mult))
            dve.seq(lambda e: e.tensor_tensor(u[3], x2, c_, ALU.mult))
            if ro:
                x1, x2 = UR[:, :, :, 0:half], UR[:, :, :, half:2 * half]
            dve.seq(lambda e: e.tensor_tensor(x1, u[0], u[1], ALU.subtract))
            T["rope", i] = dve.seq(lambda e: e.tensor_tensor(x2, u[2], u[3], ALU.add))
            return T["rope", i]

        def turn_unit(U, UR, tok, dN, dR):
            for j in range(2 if dR is None else 3):
                b = bank8()
                pe.wait(tok, b.free)
                for t in range(3):
                    nt = 16 if t == 2 else 128
                    s_ = U[0:nt, t, j, 0:128] if j < 2 else UR[0:nt, t].rearrange("p j d -> p (j d)")
                    tp = pe.op(lambda e: e.transpose(b.t[:, t * 128:t * 128 + nt], s_, ident[0:nt, 0:nt]))
                d = dN[:, j, :] if j < 2 else dR
                b.free = ev = act.seq(lambda e: e.copy(d, b.t[:, 0:272]), tp)
            return ev

        def proj_q(u):
            if u < 4:
                if u % 2 == 0:
                    T["cq"] = chunk((kview(3, 768), src(A["w_uq"], 0, 384, 384 * u, 384 * u + 768)))
                c = T["cq"]
                wq = kview(3, 768)(c[0])
                for t in range(3):
                    b = bank8()
                    tk = project(b.t[:, 0:384], lambda k: cqT[:, k, t * 128:(t + 1) * 128],
                                 lambda k: wq[:, k, (u % 2) * 384:(u % 2) * 384 + 384], range(3), c[1], tlat, b.free)
                    b.free = te = act.seq(lambda e: e.copy(
                        UQ[:, t, :, :], b.t[:, 0:384].rearrange("p (j d) -> p j d", j=2)), tk)
            else:
                if u % 2 == 0:
                    T["cq"] = chunk((kview(8, 512), src(w, 0, 1024, 704 + 256 * (u - 4), 704 + 256 * (u - 4) + 512)))
                c = T["cq"]
                wv = kview(8, 512)(c[0])
                o = (u % 2) * 256
                tk, te = rows_proj(lambda k: wv[:, k, o:o + 256], 256, c[1], [(lambda t, n: UQ[0:n, t, :, 0:128], 0)])
            if u % 2 == 1:
                done(c, tk)
            T["UQ", u] = te

        def proj_kv(u):
            i = u % 2
            if u < 4:
                if u == 0:
                    T["ckv"] = chunk((kview(2, 2048), src(A["w_ukv"], 0, 256, 0, 2048)))
                c = T["ckv"]
                wkv = kview(2, 2048)(c[0])
                for t in range(3):
                    b = bank8()
                    tk = project(b.t[:, :], lambda k: ckT[:, k, t * 128:(t + 1) * 128],
                                 lambda k: wkv[:, k, u * 512:(u + 1) * 512], range(2), c[1], tlat, b.free)
                    kv4 = b.t[:, :].rearrange("p (j d) -> p j d", j=2)
                    act.seq(lambda e: e.copy(UK[:, t, :, 0:128], kv4[:, :, 0:128]), tk)
                    b.free = te = act.seq(lambda e: e.copy(vb[i][:, t, :, :], kv4[:, :, 128:256]))
                tp_ = pool.seq(lambda e: e.tensor_copy(UK[:, :, :, 128:192], bc(kp, 2, 2)), T["kp"], tk)
                if u == 3:
                    done(c, tk)
                T["UK", u] = [te, tp_]
            elif u == 4:
                c = chunk((kview(8, 512), src(w, 0, 1024, 1728, 2240)))
                wv = kview(8, 512)(c[0])

                tk, te = rows_proj(lambda k: wv[:, k, :], 512, c[1], [(lambda t, n: UK[0:n, t, :, 0:128], 0),
                                                                      (lambda t, n: vb[0][0:n, t, :, :], 256)])
                done(c, tk)
                T["UK", u] = te

        def norm_q(u):
            T["nq"] = norm_rope(UQ, RQ, *((192, R("mgq"), 128, 32, cM, sM) if u < 4 else (128, R("sgq"), 0, 64, cS, sS)),
                                T["UQ", u])

        def norm_k(u):
            if u <= 4:
                T["nk"] = norm_rope(UK, RK, *((192, R("mgk"), 128, 32, cM, sM) if u < 4 else
                                          (128, R("sgk"), 0, 64, cS, sS)), T["UK", u])

        def turn_q(u):
            T["Q", u] = turn_unit(UQ, RQ, T["nq"], QN[u % 2], QR[u % 2] if u < 4 else None)

        def turn_k(u):
            if u <= 4:
                T["K", u] = turn_unit(UK, RK, T["nk"], KN[u % 2], KR[u % 2] if u < 4 else None)

        def scores(u, j):
            i = u % 2
            wide = u >= 4
            q_, kn = QN[i][:, j, :], KN[i][:, j, :]
            if wide:
                kn = KN[0][:, (2 * (u - 4) + j) // 4, :]
            scale = 128 ** -0.5 if wide else 192 ** -0.5
            pe.wait(T["Q", u], T["K", min(u, 4)])
            e_, mx_, sm_ = es[j], mxn[j], sm[j]
            bs = []
            for t in range(3):
                nq = 16 if t == 2 else 128
                q0 = 128 * t
                b = bank8()
                bs.append(b)
                pe.wait(b.free)
                pe.op(mm(b.t[0:nq, 0:272], q_[:, q0:q0 + nq], kn, True, False))
                if wide:
                    tk = pe.op(mm(b.t[0:nq, 0:272], identb[:, 0:nq], swm[:, t, :], False, True))
                else:
                    pr = slice(64 * j, 64 * j + 64)
                    tk = pe.op(mm(b.t[0:nq, 0:272], QR[i][pr, q0:q0 + nq], KR[i][pr, :], False, True))
                dve.seq(lambda e: e.tensor_reduce(mx_[0:nq, t:t + 1], b.t[0:nq, 0:272], AXX, ALU.max), tk)
            if wide:
                snk = R("sink")[:, 2 * (u - 4) + j:2 * (u - 4) + j + 1]
                dve.seq(lambda e: e.tensor_scalar(mx_, mx_, scale, snk, ALU.mult, ALU.max))
                tk = dve.seq(lambda e: e.tensor_scalar(mx_, mx_, -1.0, None, ALU.mult))
                tk = dve.seq(lambda e: e.tensor_scalar(esk, mx_, snk, None, ALU.add))
            else:
                tk = dve.seq(lambda e: e.tensor_scalar(mx_, mx_, -scale, None, ALU.mult))
            for t in range(3):
                nq = 16 if t == 2 else 128
                b = bs[t]
                b.free = tk = act.seq(lambda e: e.activation(
                    e_[0:nq, t, :], b.t[0:nq, 0:272], ACT.Exp, bias=mx_[0:nq, t:t + 1], scale=scale,
                    accum_out=sm_[0:nq, t:t + 1]), tk)
            if wide:
                tk = act.seq(lambda e: e.activation(esk, esk, ACT.Exp))
                dve.seq(lambda e: e.tensor_tensor(sm_, sm_, esk, ALU.add), tk)
            dve.seq(lambda e: e.reciprocal(sm_, sm_), tk)
            for t in range(3):
                nq = 16 if t == 2 else 128
                T["p", j] = dve.seq(lambda e: e.tensor_scalar(e_[0:nq, t, :], e_[0:nq, t, :], sm_[0:nq, t:t + 1],
                                                              None, ALU.mult))

        def turn_p(j, other=dve):
            for kt in range(3):
                nk = 16 if kt == 2 else 128
                b = bank8()
                pe.wait(b.free, T["p", j])
                for t in range(3):
                    nq = 16 if t == 2 else 128
                    tp = pe.op(lambda e: e.transpose(
                        b.t[0:nk, t * 128:t * 128 + nq], es[j][0:nq, t, kt * 128:kt * 128 + nk], ident[0:nq, 0:nq]))
                b.free = T["pT", j, kt] = copy(other if kt == 1 else act, pt[j][0:nk, kt, :], b.t[0:nk, 0:272], tp)

        def values(u, j):
            hd = 2 * u + j
            b = bank8()
            pe.wait(b.free)
            for kt in range(3):
                nk = 16 if kt == 2 else 128
                V = vb[u % 2][0:nk, kt, j, :] if u < 4 else vb[0][0:nk, kt, (2 * (u - 4) + j) // 4, :]
                tk = pe.op(mm(b.t[:, 0:272], V, pt[j][0:nk, kt, :], kt == 0, kt == 2), T["pT", j, kt])
            b.free = T["y"] = dve.seq(lambda e: e.tensor_tensor(yT[:, hd, :], yT[:, hd, :], b.t[:, 0:272], ALU.mult),
                                      tk, T["g", hd])

        spl, sp2, sp3 = m_small(32), m_small(32), m_small(32)
        L = C("lam", 0, 32)
        tk = dve.seq(lambda e: e.scalar_tensor_tensor(out=spl, in0=L, scalar=-1.0, in1=L, op0=ALU.mult, op1=ALU.max))
        tk = act.seq(lambda e: e.activation(spl, spl, ACT.Exp, scale=-1.0), tk)
        tk = act.seq(lambda e: e.activation(sp2, spl, ACT.Ln, bias=1.0), tk)
        dve.seq(lambda e: e.tensor_scalar(sp3, L, -1.0, 0.0, ALU.mult, ALU.max))
        dve.seq(lambda e: e.tensor_tensor(sp2, sp2, sp3, ALU.add), tk)
        dve.seq(lambda e: e.tensor_scalar(spl, sp2, 8.0, None, ALU.mult))
        tspl = dve.seq(lambda e: e.tensor_scalar(sp3, sp2, -8.0, None, ALU.mult))
        for a_ in (mxn[0], mxn[1], sm[0], sm[1]):
            dve.seq(lambda e: e.memset(a_, 1.0))
        c0 = chunk((kview(8, 512), src(w, 0, 1024, 0, 512)))
        c1 = chunk((kview(8, 192), src(w, 0, 1024, 512, 704)))
        v0, v1 = kview(8, 512)(c0[0]), kview(8, 192)(c1[0])
        tx = []
        for t in range(3):
            th = layer_norm(t, tln, turned=False)[0] if t < 2 else None
            tx.append(rms_T(t, th, "ng0", 128 * t, 128 if t < 2 else 16))
            for c, v, a0, n in ((c0, v0, 0, 512), (c1, v1, 512, 192)):
                b = bank8()
                if t < 2:
                    tk = project(b.t[:, 0:n], lambda k: xT[:, k, t * 128:(t + 1) * 128], lambda k: v[:, k, :],
                                 range(8), c[1], b.free, tx[t])
                    b.free = te = act.seq(lambda e: e.copy(lat[:, t, a0:a0 + n], b.t[:, 0:n]), tk)
                else:
                    tk = meta_proj(b, lambda k: xT[:, k, 256:272], lambda k: v[:, k, :], range(8), n, c[1], b.free,
                                   tx[t])
                    b.free = meta_sum(lat[0:16, 2, a0:a0 + n], None, b, lambda v_: v_[:, 0:n], tk)
                    te = [te, b.free]
                    done(c, tk)
        trt = act.dma(lambda e: e.dma_start(rt[:, 0:576], A["rope"]), d2, dve.now())
        gate(0)
        gate(1)
        T["kp"] = copy(dve, kp, lat[:, :, 640:704], te)
        latents = ((0, 384, "gq", cqT), (384, 256, "gkv", ckT))
        for s_, (a0, n, gname, dT) in enumerate(latents):
            r_ = s2[s_].rearrange("p a b -> p (a b)")[:, 0:3]
            for t in range(3):
                tk = act.seq(lambda e: e.activation(junk[:, 0:n], lat[:, t, a0:a0 + n], ACT.Square,
                                                    accum_out=r_[:, t:t + 1]), te)
            dve.seq(lambda e: e.tensor_scalar(r_, r_, 1.0 / n, EPS2, ALU.mult, ALU.add), tk)
            rsqrt(r_)
            tk = dve.seq(lambda e: e.tensor_tensor(lat[:, :, a0:a0 + n], lat[:, :, a0:a0 + n], bc(r_, 2, n), ALU.mult))
            for j in range(n // 128):
                b = bank8()
                pe.wait(tk, b.free)
                for t in range(3):
                    tp = pe.op(lambda e: e.transpose(
                        b.t[:, t * 128:(t + 1) * 128], lat[:, t, a0 + j * 128:a0 + (j + 1) * 128], ident))
                b.free = tlat = act.seq(lambda e: e.activation(dT[:, j, :], b.t[:, 0:384], ACT.Copy,
                                                               scale=C(gname, j)), tp)
            (proj_q if s_ == 0 else proj_kv)(0)
        norm_q(0)
        gate(2)
        norm_k(0)
        gate(3)
        turn_q(0)
        gate(4)
        turn_k(0)
        for u in range(4):
            proj_q(u + 1)
            scores(u, 0)
            scores(u, 1)
            norm_q(u + 1)
            proj_kv(u + 1)
            turn_p(0, act)
            norm_k(u + 1)
            gate(2 * u + 5)
            turn_p(1, act)
            values(u, 0)
            values(u, 1)
            gate(2 * u + 6)
            turn_q(u + 1)
            turn_k(u + 1)
        tmla = T["y"]
        wo, facc, fc = A["even_w_out"], [bank8() for _ in range(3)], {}

        def even_out(n, k0, t, ks, acc, y):
            if (n, k0) not in fc:
                fc[n, k0] = chunk((kview(8, 512), src(wo, k0 * 128, k0 * 128 + 1024, n * 512, n * 512 + 512)))
            c = fc[n, k0]
            nt = 16 if t == 2 else 128
            args = (lambda k: yT[:, k0 + k, t * 128:t * 128 + nt], lambda k: kview(8, 512)(c[0])[:, k, :], ks)
            after, ends = (c[1], y, acc[t].free if k0 == 0 else None), dict(
                start=k0 == 0 and ks[0] == 0, stop=k0 == 8 and ks[-1] == 7)
            if t == 2:
                tk = meta_proj(acc[t], *args, 512, *after, **ends)
            else:
                tk = project(acc[t].t[:, :], *args, *after, **ends)
            if t == 2 and ks[-1] == 7:
                done(c, tk)
            return tk

        fill = [lambda: gate(13), lambda: gate(14), lambda: gate(15)]
        fill += [lambda t=t, ks=ks: even_out(0, 0, t, ks, facc, tmla) for t in range(3)
                 for ks in (range(0, 4), range(4, 8))]
        for u in range(4, 8):
            scores(u, 0)
            if u < 7:
                proj_q(u + 1)
            scores(u, 1)
            if u == 7:
                fill.pop(0)()
            turn_p(0)
            if u < 7:
                norm_q(u + 1)
            fill.pop(0)()
            values(u, 0)
            turn_p(1)
            fill.pop(0)()
            values(u, 1)
            if u < 7:
                turn_q(u + 1)
        assert not fill
        th, tx = {}, []
        for q in (act, dve):
            q.wait(*everyone())
        for n in range(2):
            acc = facc if n == 0 else [bank8() for _ in range(3)]
            for k0 in (0, 8)[1 - n:]:
                for t in range(3):
                    tk = even_out(n, k0, t, range(8), acc, tmla if k0 == 0 else T["y"])
                    if k0 == 8:
                        nt = 16 if t == 2 else 128
                        hh = h[0:nt, t, n * 512:(n + 1) * 512]
                        if t == 2:
                            acc[t].free = th[t] = meta_sum(hh, hh, acc[t], lambda v: v, tk)
                        else:
                            acc[t].free = th[t] = dve.seq(lambda e: e.tensor_tensor(hh, hh, acc[t].t[:, :],
                                                                                    ALU.add), tk)
                        if n == 1 and t > 0:
                            tx.append(rms_T(t - 1, th[t - 1], "ng1", 16 + 128 * (t - 1), 128))
        tx.append(rms_T(2, th[2], "ng1", 0, 16))

        w = A["odd_w_in"]
        m = Arena(work, 7680)
        xc, sgt = [m(2, 272), m(2, 272)], [m(2, 272), m(2, 272)]
        rr, tu, hf = [m(2, 2, 272), m(2, 2, 272)], m(2, 2, 272), m(2, 2, 272)
        m = Arena(tail, 8192)
        ii, aa, tt = ([m(2, 2, 272), m(2, 2, 272)] for _ in range(3))
        flat = lambda x: x.rearrange("p a b c -> p (a b c)")
        T = {}

        def conv_in(cb):
            i = cb % 2
            c = T["w", cb] = chunk(
                (kview(8, 512, n0=0, w=256), src(w, 0, 1024, 256 * cb, 256 * cb + 256)),
                (kview(8, 512, n0=256, w=256), src(w, 0, 1024, 2048 + 256 * cb, 2048 + 256 * cb + 256)))
            wv = kview(8, 512)(c[0])
            for j in range(2):
                n = 2 * cb + j
                b = bank8()
                tk = project(b.t[:, 0:272], lambda k: wv[:, k, j * 128:(j + 1) * 128], lambda k: xT[:, k, 0:272],
                             range(8), c[1], tx, b.free)
                ps = b.t[:, 0:272]
                o = xc[i][:, j, :]
                dve.seq(lambda e: e.tensor_scalar(o, ps, C("lconv_w", 4 * n + 2), C("lconv_b", n),
                                                  ALU.mult, ALU.add), tk, T.get(("ix", cb - 2)))
                for tap, (d0, d1, s0, s1) in ((0, (2, 272, 0, 270)), (1, (1, 272, 0, 271)), (3, (0, 271, 1, 272))):
                    b.free = T["xc", cb] = dve.seq(lambda e: e.scalar_tensor_tensor(
                        out=o[:, d0:d1], in0=ps[:, s0:s1], scalar=C("lconv_w", 4 * n + tap), in1=o[:, d0:d1],
                        op0=ALU.mult, op1=ALU.add))

        def gate_in(cb):
            i, c = cb % 2, T["w", cb]
            wv = kview(8, 512)(c[0])
            for j in range(2):
                b = bank8()
                tk = project(b.t[:, 0:272], lambda k: wv[:, k, 256 + j * 128:256 + (j + 1) * 128],
                             lambda k: xT[:, k, 0:272], range(8), c[1], b.free)
                b.free = T["sg", cb] = act.seq(lambda e: e.activation(sgt[i][:, j, :], b.t[:, 0:272], ACT.Silu),
                                               tk, T.get(("y", cb - 2)))
            done(c, tk)

        def gates(cb):
            i = cb % 2
            if cb % 4 == 0:
                pieces = []
                for ki, wn in enumerate(("lru_w_a", "lru_w_x")):
                    for r in range(2):
                        at0 = (ki * 2 + r) * 1024
                        pieces.append((lambda v, at0=at0: v[:, at0:at0 + 1024].rearrange("p (n e) -> p n e", n=8),
                                       A[wn][r, 2 * cb:2 * cb + 8].rearrange("n d e -> d n e")))
                T["cl"] = chunk(*pieces)
            cl = T["cl"]
            wl = cl[0].rearrange("p (a r n e) -> p a r n e", a=2, r=2, n=8)
            for ki, (dst, bias) in enumerate(((rr[i], "ba"), (ii[i], "bx"))):
                for j in range(2):
                    n = 2 * cb + j
                    for r in range(2):
                        b = bank8()
                        tk = pe.op(mm(b.t[:, 0:272], wl[:, ki, r, n % 8, :], xc[i][:, j, :], True, True),
                                   T["xc", cb], cl[1], b.free)
                        b.free = tri = act.seq(lambda e: e.activation(
                            dst[:, j, r, :], b.t[:, 0:272], ACT.Sigmoid, bias=C(bias, 16 * r + n)), tk,
                            T.get(("b", cb - 2)))
            if cb % 4 == 3:
                done(cl, tk)
            T["ix", cb] = pool.seq(lambda e: e.tensor_tensor(ii[i], ii[i], bc(xc[i], 2, 2), ALU.mult), tri, T["xc", cb])
            for j in range(2):
                for r in range(2):
                    i_ = 16 * r + 2 * cb + j
                    T["t", cb] = act.seq(lambda e: e.activation(tt[i][:, j, r, :], rr[i][:, j, r, :], ACT.Tanh,
                                                         scale=spl[:, i_:i_ + 1]), tspl, T.get(("y", cb - 2)))
            for j in range(2):
                for r in range(2):
                    i_ = 16 * r + 2 * cb + j
                    T["a", cb] = act.seq(lambda e: e.activation(aa[i][:, j, r, :], rr[i][:, j, r, :], ACT.Exp,
                                                                scale=sp3[:, i_:i_ + 1]))

        def square(cb):
            i = cb % 2
            dve.seq(lambda e: e.tensor_scalar(flat(tu), flat(tt[i]), 1.0, None, ALU.add), T["t", cb])
            dve.seq(lambda e: e.reciprocal(flat(tu), flat(tu)))
            T["sq", cb] = dve.seq(lambda e: e.scalar_tensor_tensor(
                out=flat(tt[i]), in0=flat(tt[i]), scalar=2.0, in1=flat(tu), op0=ALU.mult, op1=ALU.mult))

        def root(cb):
            i = cb % 2
            T["root", cb] = act.seq(lambda e: e.activation(tt[i], tt[i], ACT.Sqrt), T["sq", cb])

        def scan(cb):
            i = cb % 2
            T["b", cb] = dve.seq(lambda e: e.tensor_tensor(flat(tt[i]), flat(tt[i]), flat(ii[i]), ALU.mult),
                                 T["root", cb], T["ix", cb])
            for j in range(2):
                dve.seq(lambda e: e.tensor_tensor_scan(hf[:, j, 0, :], aa[i][:, j, 0, :], tt[i][:, j, 0, :], 0.0,
                                                       ALU.mult, ALU.add), T["a", cb])
                dve.seq(lambda e: e.tensor_tensor_scan(hf[:, j, 1, ::-1], aa[i][:, j, 1, ::-1], tt[i][:, j, 1, ::-1],
                                                       0.0, ALU.mult, ALU.add))
            dve.seq(lambda e: e.tensor_tensor(hf[:, :, 0, :], hf[:, :, 0, :], hf[:, :, 1, :], ALU.add))
            T["y", cb] = dve.seq(lambda e: e.tensor_tensor(yT[:, 2 * cb:2 * cb + 2, :], hf[:, :, 0, :], sgt[i],
                                                           ALU.mult), T["sg", cb])

        conv_in(0)
        gate_in(0)
        for cb in range(8):
            gates(cb)
            if cb:
                root(cb - 1)
            if cb < 7:
                conv_in(cb + 1)
            if cb:
                scan(cb - 1)
            square(cb)
            if cb < 7:
                gate_in(cb + 1)
        root(7)
        scan(7)
        acc = [[bank8() for _ in range(2)] for _ in range(2)]
        for k0 in (0, 8):
            for n in range(2):
                c = chunk((kview(8, 512), src(A["odd_w_out"], k0 * 128, k0 * 128 + 1024, n * 512, n * 512 + 512)))
                wv = kview(8, 512)(c[0])
                for t in range(2):
                    b = acc[t][n]
                    tk = project(b.t[:, :], lambda k: yT[:, k, 16 + t * 128:144 + t * 128],
                                 lambda k: wv[:, k - k0, :], range(k0, k0 + 8), c[1], T["y", 3 if k0 == 0 else 7],
                                 b.free if k0 == 0 else None, start=k0 == 0, stop=k0 == 8)
                    if k0 == 8:
                        hh = h[:, t, n * 512:(n + 1) * 512]
                        b.free = th = dve.seq(lambda e: e.tensor_tensor(hh, hh, b.t[:, :], ALU.add), tk)
                        tout = act.dma(lambda e: e.dma_start(out[0, t * 128:t * 128 + 128, n * 512:(n + 1) * 512], hh),
                                      out_sem, th)
                done(c, tk)
        sp.wait(tout)

        block = ctx.enter_context(nc.Block())

        @block.sync
        def _(e):
            sp.play(e)

        @block.tensor
        def _(e):
            pe.play(e)

        @block.vector
        def _(e):
            dve.play(e)

        @block.scalar
        def _(e):
            act.play(e)

        @block.gpsimd
        def _(e):
            pool.play(e)


def host_layout(I):
    f = np.float32
    D = {}
    c = np.ascontiguousarray
    D["x"] = I["x"]
    p, q = np.arange(128)[:, None], np.arange(128)[None, :]
    D["cF"] = c(np.stack([(p == q), (p <= q), (p < q)], 1).astype(f))
    bits = lambda a: (np.ascontiguousarray(a, dtype=f).view(np.uint32) >> 16).astype(np.uint16)
    cb = np.zeros((128, 8, 128), f)
    cb[:, 0] = p == q
    cb[:, 1:5] = np.where(p > q, NEG, 0.0)[:, None]
    cb[:, 5] = cb[:, 7] = np.where(q > p, NEG, 0.0)
    D["cB"] = bits(cb)
    pos = np.concatenate([np.arange(256) + 16, np.arange(16)])
    sw = np.zeros((128, 3, 272), f)
    for t in range(2):
        qi = 128 * t + np.arange(128)[:, None]
        kj = np.arange(256)[None, :]
        sw[:, t, :256] = np.where(np.abs(qi - kj) <= 128, 0.0, NEG)
    mi = np.arange(16)[:, None]
    kj = np.arange(256)[None, :]
    sw[:16, 2, :256] = np.where((kj < 128) & (16 + kj - mi <= 128), 0.0, NEG)
    D["swm"] = bits(sw)
    col = np.zeros((128, NCOL), f)

    def put(name, a):
        b, w = COLS[name]
        a = np.asarray(a).reshape(w, -1).T
        col[:a.shape[0], b:b + w] = a

    put("conv_w", I["ssm_conv_w"][0].reshape(4, 32, 128).transpose(1, 0, 2))
    put("conv_b", I["ssm_conv_b"][0])
    put("norm_w", I["ssm_norm_w"][0])
    put("subln", I["attn_subln_w"][0])
    put("ng0", I["norm_g_2"][0])
    put("ng1", I["norm_g_2"][1])
    put("gq", I["mla_g_q_lat_2"][0])
    put("gkv", I["mla_g_kv_lat_2"][0])
    put("lconv_w", I["lru_conv_w_2"][0].reshape(4, 16, 128).transpose(1, 0, 2))
    put("lconv_b", I["lru_conv_b_2"][0])
    put("ba", I["lru_b_a_2"][0])
    put("bx", I["lru_b_x_2"][0])
    put("lam", I["lru_lambda_2"][0])
    put("lamv", np.stack([I[n][0] for n in ("attn_lam_q1", "attn_lam_k1", "attn_lam_q2", "attn_lam_k2")]))
    D["col"] = col
    row = np.zeros((1, NROW), f)
    inv = np.power(f(500000.0), -np.arange(0, 16, 2, dtype=f) / f(16)).astype(f)
    for name, a in (("dt_bias", I["ssm_dt_bias"]), ("a_log", I["ssm_a_log"]), ("ssm_d", I["ssm_d"]),
                    ("mgq", I["mla_g_qn_2"]), ("mgk", I["mla_g_kn_2"]), ("sgq", I["swa_g_qn_2"]),
                    ("sgk", I["swa_g_kn_2"]), ("sink", I["swa_sink_2"]), ("inv", inv),
                    ("iota", np.arange(64, dtype=f))):
        b, w = ROWS[name]
        row[0, b:b + w] = np.asarray(a).reshape(-1)
    D["row"] = row
    D["pos"] = c(I["positions"].reshape(2, 128).T.astype(np.int32))
    D["lnp"] = c(np.stack([np.stack([I["ln_mix_g"][0], I["ln_mix_b"][0]]), np.stack([I["ln_ffn_g"][0], I["ln_ffn_b"][0]]),
                           np.stack([I["ln_mix_g"][1], I["ln_mix_b"][1]]), np.stack([I["ln_ffn_g"][1], I["ln_ffn_b"][1]])]))
    wr = np.concatenate([I["moe_w_group"], I["moe_w_expert"]], axis=2)
    D["wr"] = c(wr.reshape(2, 8, 128, 36).transpose(0, 2, 1, 3))
    D["ssm_w_in"], D["ssm_w_out"] = I["ssm_w_in"][0], I["ssm_w_out"][0]
    D["attn_w_qkv"], D["attn_w_o"] = I["attn_w_qkv"][0], I["attn_w_o"][0]
    D["wg"], D["wu"], D["wd"] = I["moe_w_gate"], I["moe_w_up"], I["moe_w_down"]
    D["meta"] = I["meta_tokens_2"]
    D["even_w_in"], D["even_w_out"] = I["even_w_in_2"][0], I["even_w_out_2"][0]
    D["w_uq"] = I["mla_w_uq_2"][0].reshape(384, 1536)
    D["w_ukv"] = I["mla_w_ukv_2"][0].reshape(256, 2048)
    D["odd_w_in"], D["odd_w_out"] = I["odd_w_in_2"][0], I["odd_w_out_2"][0]
    D["lru_w_a"], D["lru_w_x"] = I["lru_w_a_2"][0], I["lru_w_x_2"][0]

    def rope(dim):
        i = (f(10000.0) ** (-np.arange(0, dim, 2, dtype=f) / f(dim))).astype(f)
        a = np.zeros((384, dim // 2), f)
        a[:272] = pos.astype(f)[:, None] * i[None, :]
        r = lambda v: v.astype(f).reshape(3, 128, dim // 2).transpose(1, 0, 2).reshape(128, -1)
        return r(np.cos(a)), r(np.sin(a))

    D["rope"] = c(np.concatenate([*rope(64), *rope(128)], axis=1))
    return D


def kernel(**inputs):
    import concourse.bacc as _bacc
    from concourse import mybir as _mybir
    from concourse.bass_utils import run_bass_kernel_spmd as _run

    I = {k: np.asarray(v) for k, v in inputs.items()}
    D = host_layout(I)
    nc = _bacc.Bacc("TRN2", target_bir_lowering=False, num_devices=1)
    arrays, aps = {}, {}
    for name, a in D.items():
        a = np.ascontiguousarray(a)
        arrays[f"in_{name}"] = a
        aps[name] = nc.dram_tensor(f"in_{name}", a.shape, _mybir.dt.from_np(a.dtype), kind="ExternalInput").ap()
    out = nc.dram_tensor("out_0", (1, 256, 1024), _mybir.dt.float32, kind="ExternalOutput").ap()
    build(nc, aps, out)
    r = _run(nc, [arrays], core_ids=[0])
    return r.results[0]["out_0"]
```
